# Optimizing a Trainium2 kernel written in Bass

```python
import math
import jax, jax.numpy as jnp
from jax import lax
import numpy as np

D_MODEL = 1024
BATCH = 1
SEQ = 256
DEPTH = 2

GRID_W = 64
CTX_LEN = 256
N_MIXERS = 2
HEAD_DIM = 64
N_HEADS = D_MODEL // HEAD_DIM
A_KV_HEADS = 4
A_GROUPS = N_HEADS // A_KV_HEADS
A_WINDOW = 128
A_BLOCK = 128
A_INNER = N_HEADS * HEAD_DIM
A_KV_DIM = A_KV_HEADS * HEAD_DIM
A_IN_DIM = 2 * A_INNER + 2 * A_KV_DIM
B_KH_MAX = 8
B_KW = 16
B_QW = 16
B_REG_W = 2 * B_KW
B_INNER = N_HEADS * HEAD_DIM
B_IN_DIM = 4 * B_INNER
ROPE_BASE = 10000.0
LN_EPS = 1e-5
NEG_INF = -1e30
DEEPNORM_ALPHA = (2.0 * DEPTH) ** 0.25
DEEPNORM_BETA = (8.0 * DEPTH) ** -0.25
N_LAYERS_A = (DEPTH + 1) // 2
N_LAYERS_B = DEPTH // 2


def layer_norm(x, g, b):
    xf = x.astype(jnp.float32)
    mu = jnp.mean(xf, axis=-1, keepdims=True)
    var = jnp.mean(jnp.square(xf - mu), axis=-1, keepdims=True)
    y = (xf - mu) * lax.rsqrt(var + LN_EPS)
    return (y * g.astype(jnp.float32) + b.astype(jnp.float32)).astype(x.dtype)

def axial_rope_tables(n_tok):
    t = jnp.arange(n_tok)
    row = (t // GRID_W).astype(jnp.float32)
    col = (t % GRID_W).astype(jnp.float32)
    n_freq = HEAD_DIM // 4
    inv = ROPE_BASE ** (-jnp.arange(n_freq, dtype=jnp.float32) / n_freq)
    ang_r = row[:, None] * inv[None]
    ang_c = col[:, None] * inv[None]
    return (jnp.cos(ang_r), jnp.sin(ang_r), jnp.cos(ang_c), jnp.sin(ang_c))

def _rotate(x, cos, sin):
    a, b = jnp.split(x, 2, axis=-1)
    cos = cos[None, :, None, :].astype(x.dtype)
    sin = sin[None, :, None, :].astype(x.dtype)
    return jnp.concatenate([a * cos - b * sin, b * cos + a * sin], axis=-1)

def apply_axial_rope(x, rope):
    cos_r, sin_r, cos_c, sin_c = rope
    xr, xc = jnp.split(x, 2, axis=-1)
    return jnp.concatenate([_rotate(xr, cos_r, sin_r), _rotate(xc, cos_c, sin_c)], axis=-1)

def ctx_attention(q, k, v, sink):
    B, C = q.shape[0], q.shape[1]
    s = jnp.einsum('bqkgd,bckd->bkgqc', q, k).astype(jnp.float32) * (HEAD_DIM ** -0.5)
    if sink is not None:
        s_sink = jnp.broadcast_to(sink[None, :, :, None, None], s.shape[:-1] + (1,))
        p = jax.nn.softmax(jnp.concatenate([s, s_sink], axis=-1), axis=-1)[..., :C]
    else:
        p = jax.nn.softmax(s, axis=-1)
    o = jnp.einsum('bkgqc,bckd->bqkgd', p.astype(v.dtype), v)
    return o.reshape(B, C, -1)

def _split_a(p):
    return jnp.split(p, [A_INNER, A_INNER + A_KV_DIM, A_INNER + 2 * A_KV_DIM], axis=-1)

def mixer_a(u, uc, w_in, w_out, sink, rope, ctx_out):
    B, S, _ = u.shape
    C = uc.shape[1]
    scale = HEAD_DIM ** -0.5
    q, k, v, g = _split_a(u @ w_in)
    q = apply_axial_rope(q.reshape(B, S, N_HEADS, HEAD_DIM), rope).reshape(B, S, A_KV_HEADS, A_GROUPS, HEAD_DIM)
    k = apply_axial_rope(k.reshape(B, S, A_KV_HEADS, HEAD_DIM), rope)
    v = v.reshape(B, S, A_KV_HEADS, HEAD_DIM)
    qc, kc, vc, gc = _split_a(uc @ w_in)
    kc = kc.reshape(B, C, A_KV_HEADS, HEAD_DIM)
    vc = vc.reshape(B, C, A_KV_HEADS, HEAD_DIM)
    sink_l = sink.reshape(A_KV_HEADS, A_GROUPS).astype(jnp.float32)
    span = A_BLOCK + 2 * A_WINDOW
    pad = ((0, 0), (A_WINDOW, A_WINDOW), (0, 0), (0, 0))
    kp = jnp.pad(k, pad)
    vp = jnp.pad(v, pad)

    def block(bi):
        start = bi * A_BLOCK
        qb = lax.dynamic_slice_in_dim(q, start, A_BLOCK, axis=1)
        kb = lax.dynamic_slice_in_dim(kp, start, span, axis=1)
        vb = lax.dynamic_slice_in_dim(vp, start, span, axis=1)
        qi = start + jnp.arange(A_BLOCK)
        kj = start - A_WINDOW + jnp.arange(span)
        mask = (jnp.abs(qi[:, None] - kj[None, :]) <= A_WINDOW) & (kj >= 0)[None, :] & (kj < S)[None, :]
        s_lat = jnp.einsum('bqkgd,bjkd->bkgqj', qb, kb).astype(jnp.float32) * scale
        s_lat = jnp.where(mask, s_lat, NEG_INF)
        s_ctx = jnp.einsum('bqkgd,bckd->bkgqc', qb, kc).astype(jnp.float32) * scale
        s_sink = jnp.broadcast_to(sink_l[None, :, :, None, None], s_lat.shape[:-1] + (1,))
        p = jax.nn.softmax(jnp.concatenate([s_lat, s_ctx, s_sink], axis=-1), axis=-1)
        p_lat = p[..., :span].astype(v.dtype)
        p_ctx = p[..., span:span + C].astype(v.dtype)
        o = jnp.einsum('bkgqj,bjkd->bqkgd', p_lat, vb) + jnp.einsum('bkgqc,bckd->bqkgd', p_ctx, vc)
        return o.reshape(B, A_BLOCK, A_INNER)

    o = lax.map(block, jnp.arange(S // A_BLOCK))
    o = jnp.transpose(o, (1, 0, 2, 3)).reshape(B, S, A_INNER)
    y = (o * jax.nn.silu(g)) @ w_out
    if not ctx_out:
        return y, None
    oc = ctx_attention(qc.reshape(B, C, A_KV_HEADS, A_GROUPS, HEAD_DIM), kc, vc, sink_l)
    yc = (oc * jax.nn.silu(gc)) @ w_out
    return y, yc

def mixer_b(u, uc, w_in, w_out, rel_bias, ctx_out):
    B, S, _ = u.shape
    C = uc.shape[1]
    rows = S // GRID_W
    kh = min(B_KH_MAX, rows)
    scale = HEAD_DIM ** -0.5
    q, k, v, g = jnp.split(u @ w_in, 4, axis=-1)
    q = q.reshape(B, rows, GRID_W, N_HEADS, HEAD_DIM)
    k = k.reshape(B, rows, GRID_W, N_HEADS, HEAD_DIM)
    v = v.reshape(B, rows, GRID_W, N_HEADS, HEAD_DIM)
    qc, kc, vc, gc = jnp.split(uc @ w_in, 4, axis=-1)
    kc = kc.reshape(B, C, N_HEADS, HEAD_DIM)
    vc = vc.reshape(B, C, N_HEADS, HEAD_DIM)

    n_cb = GRID_W // B_QW
    c0 = np.arange(n_cb) * B_QW
    cs_blk = np.clip(c0 - B_KW // 2, 0, GRID_W - B_REG_W)
    key_col = cs_blk[:, None] + np.arange(B_REG_W)
    q_col = c0[:, None] + np.arange(B_QW)
    cs_q = np.clip(q_col - B_KW // 2, 0, GRID_W - B_KW)
    col_mask = (key_col[:, None, :] >= cs_q[:, :, None]) & (key_col[:, None, :] < cs_q[:, :, None] + B_KW)
    col_idx = np.clip(key_col[:, None, :] - q_col[:, :, None] + (B_KW - 1), 0, 2 * B_KW - 2)
    key_col = jnp.asarray(key_col, dtype=jnp.int32)
    col_idx = jnp.asarray(col_idx, dtype=jnp.int32)
    col_mask = jnp.asarray(col_mask)[:, :, None, :]
    bias_tab = rel_bias.astype(jnp.float32)

    def row_block(r):
        rs = jnp.clip(r - kh // 2, 0, rows - kh)
        q_r = lax.dynamic_index_in_dim(q, r, axis=1, keepdims=False).reshape(B, n_cb, B_QW, N_HEADS, HEAD_DIM)
        k_rows = lax.dynamic_slice_in_dim(k, rs, kh, axis=1)
        v_rows = lax.dynamic_slice_in_dim(v, rs, kh, axis=1)
        k_reg = k_rows[:, :, key_col]
        v_reg = v_rows[:, :, key_col]
        s = jnp.einsum('bnqhd,brnjhd->bhnqrj', q_r, k_reg).astype(jnp.float32) * scale
        row_idx = rs + jnp.arange(kh) - r + (B_KH_MAX - 1)
        bias = bias_tab[:, row_idx[:, None, None, None], col_idx[None]]
        s = s + jnp.transpose(bias, (0, 2, 3, 1, 4))[None]
        s = jnp.where(col_mask, s, NEG_INF).reshape(B, N_HEADS, n_cb, B_QW, kh * B_REG_W)
        s_ctx = jnp.einsum('bnqhd,bchd->bhnqc', q_r, kc).astype(jnp.float32) * scale
        p = jax.nn.softmax(jnp.concatenate([s, s_ctx], axis=-1), axis=-1)
        p_lat = p[..., :kh * B_REG_W].reshape(B, N_HEADS, n_cb, B_QW, kh, B_REG_W).astype(v.dtype)
        p_ctx = p[..., kh * B_REG_W:].astype(v.dtype)
        o = jnp.einsum('bhnqrj,brnjhd->bnqhd', p_lat, v_reg) + jnp.einsum('bhnqc,bchd->bnqhd', p_ctx, vc)
        return o.reshape(B, GRID_W, B_INNER)

    o = lax.map(row_block, jnp.arange(rows))
    o = jnp.transpose(o, (1, 0, 2, 3)).reshape(B, S, B_INNER)
    y = (o * jax.nn.silu(g)) @ w_out
    if not ctx_out:
        return y, None
    oc = ctx_attention(qc.reshape(B, C, N_HEADS, 1, HEAD_DIM), kc[:, :, :, :], vc, None)
    yc = (oc * jax.nn.silu(gc)) @ w_out
    return y, yc

def first_inputs(seed: int = 0) -> dict:
    key = jax.random.key(seed)
    ks = jax.random.split(key, 14)
    f32 = jnp.float32
    d = D_MODEL
    return {
        "x": jax.random.normal(ks[0], (BATCH, SEQ, d), f32),
        "c": jax.random.normal(ks[1], (BATCH, d), f32),
        "ctx": jax.random.normal(ks[2], (BATCH, CTX_LEN, d), f32),
        "c_ctx": jax.random.normal(ks[3], (d,), f32),
        "w_ada": jax.random.normal(ks[4], (DEPTH, d, 3 * d), f32) * d ** -0.5,
        "b_ada": 0.01 * jax.random.normal(ks[5], (DEPTH, 3 * d), f32),
        "ln_g": 1.0 + 0.05 * jax.random.normal(ks[6], (DEPTH, d), f32),
        "ln_b": 0.02 * jax.random.normal(ks[7], (DEPTH, d), f32),
        "a_w_in": jax.random.normal(ks[8], (N_LAYERS_A, d, A_IN_DIM), f32) * d ** -0.5,
        "a_w_out": jax.random.normal(ks[9], (N_LAYERS_A, A_INNER, d), f32) * (A_INNER ** -0.5 * DEEPNORM_BETA),
        "a_sink": 0.5 * jax.random.normal(ks[10], (N_LAYERS_A, N_HEADS), f32),
        "b_w_in": jax.random.normal(ks[11], (N_LAYERS_B, d, B_IN_DIM), f32) * d ** -0.5,
        "b_w_out": jax.random.normal(ks[12], (N_LAYERS_B, B_INNER, d), f32) * (B_INNER ** -0.5 * DEEPNORM_BETA),
        "b_rel_bias": 0.5 * jax.random.normal(ks[13], (N_LAYERS_B, N_HEADS, 2 * B_KH_MAX - 1, 2 * B_KW - 1), f32),
    }

def first_block(x, c, ctx, c_ctx, w_ada, b_ada, ln_g, ln_b, a_w_in, a_w_out, a_sink, b_w_in, b_w_out, b_rel_bias):
    S = x.shape[1]
    rope = axial_rope_tables(S)
    silu_c = jax.nn.silu(c)
    silu_cc = jax.nn.silu(c_ctx)
    h, hc = x, ctx
    for i in range(DEPTH):
        shift, scale, gate = jnp.split(silu_c @ w_ada[i] + b_ada[i], 3, axis=-1)
        shift_c, scale_c, gate_c = jnp.split(silu_cc @ w_ada[i] + b_ada[i], 3, axis=-1)
        ctx_out = i < DEPTH - 1
        u = h * (1.0 + scale[:, None, :]) + shift[:, None, :]
        uc = hc * (1.0 + scale_c) + shift_c
        j = i // N_MIXERS
        if i % N_MIXERS == 0:
            y, yc = mixer_a(u, uc, a_w_in[j], a_w_out[j], a_sink[j], rope, ctx_out)
        else:
            y, yc = mixer_b(u, uc, b_w_in[j], b_w_out[j], b_rel_bias[j], ctx_out)
        h = layer_norm(DEEPNORM_ALPHA * h + gate[:, None, :] * y, ln_g[i], ln_b[i])
        if ctx_out:
            hc = layer_norm(DEEPNORM_ALPHA * hc + gate_c * yc, ln_g[i], ln_b[i])
    return h


DEPTH_2 = 1

D_MIX = D_MODEL
D_ATTN = D_MIX // 2
N_HEADS_2 = D_ATTN // HEAD_DIM
D_CONV = D_MIX - D_ATTN
D_IN = 3 * D_ATTN + 2 * D_CONV
CONV_WIDTH = 31
DILATED_BRANCHES = ((128, 1), (512, 4), (2048, 16))
ATTN_BLOCK = 128
N_GROUPS = 4
EXPERTS_PER_GROUP = 8
N_EXPERTS = N_GROUPS * EXPERTS_PER_GROUP
TOP_K_INNER = 2
D_EXPERT = D_MODEL // 2
MOE_BLOCK = 256
NORM_EPS = 1e-6
N_MOD = 6


def rms_norm(x, g):
    x32 = x.astype(jnp.float32)
    y = x32 * lax.rsqrt(jnp.mean(x32 * x32, axis=-1, keepdims=True) + NORM_EPS)
    return (y * g.astype(jnp.float32)).astype(x.dtype)

def layer_norm_2(x, g, b):
    x32 = x.astype(jnp.float32)
    mu = jnp.mean(x32, axis=-1, keepdims=True)
    var = jnp.mean(jnp.square(x32 - mu), axis=-1, keepdims=True)
    y = (x32 - mu) * lax.rsqrt(var + NORM_EPS)
    return (y * g.astype(jnp.float32) + b.astype(jnp.float32)).astype(x.dtype)

def alibi_slopes(n_heads):
    return jnp.asarray(2.0 ** (-8.0 * np.arange(1, n_heads + 1) / n_heads), dtype=jnp.float32)

def dilated_branch(q, k, v, slopes, window, dil):
    B, H, S, Dh = q.shape
    L = S // dil
    n_back = window // dil
    nb = -(-L // ATTN_BLOCK)
    Lp = nb * ATTN_BLOCK

    def to_blocks(t):
        t = t.reshape(B, H, L, dil, Dh).transpose(0, 1, 3, 2, 4)
        t = jnp.pad(t, ((0, 0), (0, 0), (0, 0), (0, Lp - L), (0, 0)))
        return t.reshape(B, H, dil, nb, ATTN_BLOCK, Dh)

    def with_prev(t):
        prev = jnp.pad(t[:, :, :, :-1], ((0, 0), (0, 0), (0, 0), (1, 0), (0, 0), (0, 0)))
        return jnp.concatenate([prev, t], axis=4)

    qb = to_blocks(q)
    kc = with_prev(to_blocks(k))
    vc = with_prev(to_blocks(v))
    s = jnp.einsum('bhrnqd,bhrnkd->bhrnqk', qb, kc,
                   preferred_element_type=jnp.float32) * (HEAD_DIM ** -0.5)
    qi = np.arange(ATTN_BLOCK)[:, None] + ATTN_BLOCK
    ki = np.arange(2 * ATTN_BLOCK)[None, :]
    delta = qi - ki
    blk_ok = (np.arange(nb)[:, None, None] > 0) | (ki[None] >= ATTN_BLOCK)
    valid = (delta >= 0) & (delta <= n_back) & blk_ok
    bias = -slopes[:, None, None] * jnp.asarray(delta * dil, dtype=jnp.float32)
    s = s + bias[None, :, None, None]
    s = jnp.where(valid[None, None, None], s, -jnp.inf)
    m = jnp.max(s, axis=-1)
    p = jnp.exp(s - m[..., None])
    l = jnp.sum(p, axis=-1)
    o = jnp.einsum('bhrnqk,bhrnkd->bhrnqd', p, vc.astype(jnp.float32))

    def from_blocks(t, trailing):
        t = t.reshape((B, H, dil, Lp) + trailing)[:, :, :, :L]
        t = jnp.moveaxis(t, 2, 3)
        return t.reshape((B, H, S) + trailing)

    return from_blocks(o, (Dh,)), from_blocks(m, ()), from_blocks(l, ())

def dilated_attention(q, k, v, slopes):
    outs = [dilated_branch(q, k, v, slopes, w, d) for (w, d) in DILATED_BRANCHES]
    m_all = jnp.stack([m for (_, m, _) in outs])
    m_max = jnp.max(m_all, axis=0)
    num = 0.0
    den = 0.0
    for (o, m, l) in outs:
        a = jnp.exp(m - m_max)
        num = num + a[..., None] * o
        den = den + a * l
    return num / den[..., None]

def conformer_conv(a, b, conv_w, conv_b, ln_g, ln_b):
    u = a * jax.nn.sigmoid(b)
    y = lax.conv_general_dilated(u, conv_w[:, None, :].astype(u.dtype), window_strides=(1,),
                                 padding=[(CONV_WIDTH - 1, 0)],
                                 dimension_numbers=('NWC', 'WIO', 'NWC'),
                                 feature_group_count=D_CONV) + conv_b
    return jax.nn.silu(layer_norm_2(y, ln_g, ln_b))

def hier_moe(h, w_rg, b_rg, w_re, b_re, w_gate, w_up, w_down):
    B, S, D = h.shape
    T = B * S
    hf = h.reshape(T, D)
    tix = jnp.arange(T)
    g_logits = (hf @ w_rg + b_rg).astype(jnp.float32)
    g_prob = jax.nn.softmax(g_logits, axis=-1)
    grp = jnp.argmax(g_logits, axis=-1)
    p_grp = g_prob[tix, grp]
    e_logits = (hf @ w_re + b_re).astype(jnp.float32).reshape(T, N_GROUPS, EXPERTS_PER_GROUP)
    e_logits = e_logits[tix, grp]
    top_val, top_idx = lax.top_k(e_logits, TOP_K_INNER)
    top_w = jax.nn.softmax(top_val, axis=-1) * p_grp[:, None]

    A = T * TOP_K_INNER
    eid = (grp[:, None] * EXPERTS_PER_GROUP + top_idx).reshape(A).astype(jnp.int32)
    tok = jnp.repeat(tix, TOP_K_INNER).astype(jnp.int32)
    wts = top_w.reshape(A)
    order = jnp.argsort(eid)
    s_eid, s_tok, s_w = eid[order], tok[order], wts[order]
    counts = jnp.bincount(eid, length=N_EXPERTS)
    start = jnp.cumsum(counts) - counts
    padded = ((counts + MOE_BLOCK - 1) // MOE_BLOCK) * MOE_BLOCK
    pad_end = jnp.cumsum(padded)
    pad_start = pad_end - padded
    dest = pad_start[s_eid] + (jnp.arange(A) - start[s_eid])
    P = (-(-A // MOE_BLOCK)) * MOE_BLOCK + N_EXPERTS * MOE_BLOCK
    nblk = P // MOE_BLOCK
    buf_tok = jnp.full((P,), T, dtype=jnp.int32).at[dest].set(s_tok)
    buf_w = jnp.zeros((P,), dtype=jnp.float32).at[dest].set(s_w)
    blk_eid = jnp.clip(jnp.searchsorted(pad_end, jnp.arange(nblk) * MOE_BLOCK, side='right'),
                       0, N_EXPERTS - 1)
    x_pad = jnp.concatenate([hf, jnp.zeros((1, D), hf.dtype)], axis=0)
    xb = x_pad[buf_tok].reshape(nblk, MOE_BLOCK, D)

    def expert_block(args):
        xblk, e = args
        return (jax.nn.silu(xblk @ w_gate[e]) * (xblk @ w_up[e])) @ w_down[e]

    yb = lax.map(expert_block, (xb, blk_eid)).reshape(P, D)
    out = jnp.zeros((T + 1, D), yb.dtype).at[buf_tok].add(yb * buf_w[:, None].astype(yb.dtype))[:T]
    return out.reshape(B, S, D).astype(h.dtype)

def second_inputs(seed: int = 0) -> dict:
    key = jax.random.key(seed)
    ks = jax.random.split(key, 24)
    f32 = jnp.float32
    nrm = lambda k, shape, s: jax.random.normal(k, shape, f32) * s
    L = DEPTH_2
    return {
        "x": nrm(ks[0], (BATCH, SEQ, D_MODEL), 1.0),
        "c": nrm(ks[1], (BATCH, D_MODEL), 1.0),
        "w_mod": nrm(ks[2], (L, D_MODEL, N_MOD * D_MODEL), 0.5 * D_MODEL ** -0.5),
        "b_mod": nrm(ks[3], (L, N_MOD * D_MODEL), 0.01),
        "g_norm1": 1.0 + nrm(ks[4], (L, D_MODEL), 0.02),
        "w_in": nrm(ks[5], (L, D_MODEL, D_IN), D_MODEL ** -0.5),
        "conv_w": nrm(ks[6], (L, CONV_WIDTH, D_CONV), CONV_WIDTH ** -0.5),
        "conv_b": nrm(ks[7], (L, D_CONV), 0.01),
        "conv_ln_g": 1.0 + nrm(ks[8], (L, D_CONV), 0.02),
        "conv_ln_b": nrm(ks[9], (L, D_CONV), 0.01),
        "w_out": nrm(ks[10], (L, D_MIX, D_MODEL), D_MIX ** -0.5),
        "g_norm2": 1.0 + nrm(ks[11], (L, D_MODEL), 0.02),
        "w_router_group": nrm(ks[12], (L, D_MODEL, N_GROUPS), D_MODEL ** -0.5),
        "b_router_group": nrm(ks[13], (L, N_GROUPS), 0.01),
        "w_router_expert": nrm(ks[14], (L, D_MODEL, N_EXPERTS), D_MODEL ** -0.5),
        "b_router_expert": nrm(ks[15], (L, N_EXPERTS), 0.01),
        "w_exp_gate": nrm(ks[16], (L, N_EXPERTS, D_MODEL, D_EXPERT), D_MODEL ** -0.5),
        "w_exp_up": nrm(ks[17], (L, N_EXPERTS, D_MODEL, D_EXPERT), D_MODEL ** -0.5),
        "w_exp_down": nrm(ks[18], (L, N_EXPERTS, D_EXPERT, D_MODEL), D_EXPERT ** -0.5),
        "g_final": 1.0 + nrm(ks[19], (D_MODEL,), 0.02),
    }

def second_block(x, c, w_mod, b_mod, g_norm1, w_in, conv_w, conv_b, conv_ln_g, conv_ln_b, w_out,
              g_norm2, w_router_group, b_router_group, w_router_expert, b_router_expert,
              w_exp_gate, w_exp_up, w_exp_down, g_final):
    B, S, D = x.shape
    slopes = alibi_slopes(N_HEADS_2)
    c_act = jax.nn.silu(c)

    def split_heads(t):
        return t.reshape(B, S, N_HEADS_2, HEAD_DIM).transpose(0, 2, 1, 3)

    for l in range(DEPTH_2):
        mod = c_act @ w_mod[l] + b_mod[l]
        sh1, sc1, gt1, sh2, sc2, gt2 = jnp.split(mod[:, None, :], N_MOD, axis=-1)

        h = rms_norm(x, g_norm1[l]) * (1.0 + sc1) + sh1
        u = h @ w_in[l]
        q, k, v, ga, gb = jnp.split(
            u, [D_ATTN, 2 * D_ATTN, 3 * D_ATTN, 3 * D_ATTN + D_CONV], axis=-1)
        attn = dilated_attention(split_heads(q), split_heads(k), split_heads(v), slopes)
        attn = attn.transpose(0, 2, 1, 3).reshape(B, S, D_ATTN).astype(x.dtype)
        conv = conformer_conv(ga, gb, conv_w[l], conv_b[l], conv_ln_g[l], conv_ln_b[l])
        mix = jnp.concatenate([attn, conv], axis=-1) @ w_out[l]
        x = x + gt1 * mix

        h2 = rms_norm(x, g_norm2[l]) * (1.0 + sc2) + sh2
        x = x + gt2 * hier_moe(h2, w_router_group[l], b_router_group[l], w_router_expert[l],
                               b_router_expert[l], w_exp_gate[l], w_exp_up[l], w_exp_down[l])

    return rms_norm(x, g_final)


def setup_inputs(seed=0):
    out = dict(first_inputs(seed))
    for name, value in second_inputs(seed + 1).items():
        if name != "x":
            out[name + "_2"] = value
    return out


def reference(
    x, c, ctx, c_ctx, w_ada, b_ada, ln_g, ln_b, a_w_in, a_w_out, a_sink, b_w_in, b_w_out,
    b_rel_bias, c_2, w_mod_2, b_mod_2, g_norm1_2, w_in_2, conv_w_2, conv_b_2, conv_ln_g_2,
    conv_ln_b_2, w_out_2, g_norm2_2, w_router_group_2, b_router_group_2, w_router_expert_2,
    b_router_expert_2, w_exp_gate_2, w_exp_up_2, w_exp_down_2, g_final_2,
):
    x = first_block(
        x, c, ctx, c_ctx, w_ada, b_ada, ln_g, ln_b, a_w_in, a_w_out, a_sink, b_w_in, b_w_out,
        b_rel_bias,
    )
    return second_block(
        x, c_2, w_mod_2, b_mod_2, g_norm1_2, w_in_2, conv_w_2, conv_b_2, conv_ln_g_2,
        conv_ln_b_2, w_out_2, g_norm2_2, w_router_group_2, b_router_group_2, w_router_expert_2,
        b_router_expert_2, w_exp_gate_2, w_exp_up_2, w_exp_down_2, g_final_2,
    )


_drawn_inputs = setup_inputs


def setup_inputs(seed=0):
    import zlib

    import numpy as np

    out = dict(_drawn_inputs(seed))
    spreads = {}
    factors = {'b_ada': 8.0,
     'a_sink': 8.0,
     'b_rel_bias': 4.073,
     'b_mod_2': 5.274,
     'g_norm1_2': 8.0,
     'conv_b_2': 6.868,
     'conv_ln_g_2': 8.0,
     'conv_ln_b_2': 8.0,
     'g_norm2_2': 4.923,
     'b_router_group_2': 8.0,
     'b_router_expert_2': 8.0}
    for name, (base, spread) in spreads.items():
        noise = np.random.default_rng([zlib.crc32(name.encode()), seed]).standard_normal(out[name].shape)
        drawn = base * np.exp(spread * noise) if base else spread * noise
        out[name] = __import__('jax').numpy.asarray(drawn.astype(out[name].dtype))
    for name, factor in factors.items():
        out[name] = (out[name] * factor).astype(out[name].dtype)
    return out
```

```python
from contextlib import ExitStack

import numpy as np
import concourse.bass as bass
from concourse import mybir

F32 = mybir.dt.float32
I32 = mybir.dt.int32
ACT = mybir.ActivationFunctionType
ALU = mybir.AluOpType
AX = mybir.AxisListType

P = 128
D = 1024
KT = D // P
S = 256
C = 256
T = S + C
NH = 16
HD = 64
KVH = 4
GRID_W = 64
KW = 16
REL_W, REL_H = 2 * KW - 1, 15
PADW = 2 * GRID_W - 1
BROWS = 6
NH2 = 8
CONV_W = 31
NG, EPG = 4, 8
NE = NG * EPG
HID = 512
CAP = 64
PAIRS = NE // 2
FIRST = 0
PASSES = -(-S // CAP)
COLS = 512
SLOTS = 6
ALPHA = 4.0 ** 0.25
BIG = 1e30


def const_layout():
    at, n = {}, 0
    for name, w in (("ident", P), ("mean", P), ("ones", P), ("rot", P), ("before", P), ("cos", S), ("sin", S),
                    ("band", 2 * P), ("dist", 2 * S), ("mult", 2 * S), ("col", GRID_W), ("slot", CAP),
                    ("desc", NE), ("eps", 2)):
        at[name] = (n, n + w)
        n += w
    return at, n


def constants():
    at, n = const_layout()
    out = np.zeros((P, n), np.float32)

    def put(name, a):
        out[:, at[name][0]:at[name][1]] = np.asarray(a, np.float32).reshape(a.shape[0], -1)

    p, q = np.arange(P)[:, None], np.arange(P)[None, :]
    put("ident", (p == q) * 1.0)
    put("mean", np.full((P, P), 1.0 / D))
    put("ones", np.ones((P, P)))
    rot = np.zeros((P, P), np.float32)
    for m in range(P):
        if m % 32 < 16:
            rot[m + 16, m] = -1.0
        else:
            rot[m - 16, m] = 1.0
    put("rot", rot)
    put("before", (p < q) * 1.0)
    t = np.arange(S)
    inv = np.float32(10000.0) ** (-np.arange(16, dtype=np.float32) / np.float32(16))
    sub = np.arange(P) % HD
    pos = np.where((sub < 32)[:, None], (t // GRID_W)[None, :], (t % GRID_W)[None, :]).astype(np.float32)
    ang = (pos * inv[sub % 16][:, None]).astype(np.float32)
    put("cos", np.cos(ang))
    put("sin", np.sin(ang))
    put("band", np.concatenate([np.where(q > p, -BIG, 0.0), np.where(p > q, -BIG, 0.0)], axis=1))
    d = (np.arange(2)[None, :, None] * P + np.arange(P)[:, None, None]) - np.arange(S)[None, None, :]
    mult = np.where(d >= 0, (d <= 128) * 1.0 + (d % 4 == 0) + (d % 16 == 0), 0.0)
    put("dist", np.where(mult > 0, d, BIG))
    put("mult", mult)
    qc, kc = np.arange(P)[:, None] % GRID_W, np.arange(GRID_W)[None, :]
    first = np.clip(qc - KW // 2, 0, GRID_W - KW)
    put("col", np.where((kc >= first) & (kc < first + KW), 0.0, -BIG)[:, ::-1])
    put("slot", np.tile(np.arange(CAP), (P, 1)))
    put("desc", np.tile(NE - np.arange(NE), (P, 1)))
    put("eps", np.tile(np.array([1e-5, 1e-6]), (P, 1)))
    return out


VEC = [("c", 8), ("c_ctx", 8), ("c_2", 8), ("b_ada", 48), ("ln_g", 16), ("ln_b", 16), ("g_norm1_2", 8),
       ("g_norm2_2", 8), ("g_final_2", 8), ("b_mod_2", 48), ("conv_b_2", 4), ("conv_ln_g_2", 4), ("conv_ln_b_2", 4)]
VAT = {}
for _name, _n in VEC:
    VAT[_name] = sum(VAT_n for _, VAT_n in VEC[:[v[0] for v in VEC].index(_name)])
NVEC = sum(n for _, n in VEC)
VROWS1 = NVEC - P


def chunk_plan():
    plan = [("ada0", "w_ada", 0, c) for c in range(6)]
    plan += [("a_in", "a_w_in", 0, c) for c in range(5)]
    plan += [("a_out", "a_w_out", 0, c) for c in range(2)]
    plan += [("ada1", "w_ada", 1, c) for c in range(6)]
    plan += [("b_in", "b_w_in", 0, c) for c in range(8)]
    plan += [("b_out", "b_w_out", 0, c) for c in range(2)]
    plan += [("mod_a", "w_mod_2", 0, c) for c in range(6)]
    plan += [("c_in", "w_in_2", 0, c) for c in (4, 3, 0, 1, 2)]
    plan += [("c_out", "w_out_2", 0, c) for c in range(2)]
    plan += [("mod_b", "w_mod_2", 0, c) for c in range(6, 12)]
    return plan


PLAN = chunk_plan()
ROUNDS = len(PLAN) // SLOTS
STAGE_AT = {}
for _i, _c in enumerate(PLAN):
    STAGE_AT.setdefault(_c[0], _i)


def in_jobs(stage):
    if stage == "a_in":
        jobs = [("q", m, m // 4, (m % 4) * P, "act") for m in range(8)]
        jobs += [("k", m, 2, m * P, "act") for m in range(2)]
        jobs += [("v", t, 2, 2 * P, "dve") for t in range(4)]
        jobs += [("g", m, 3 + m // 4, (m % 4) * P, "act") for m in range(8)]
    elif stage == "b_in":
        jobs = [("q", m, m // 4, (m % 4) * P, "act") for m in range(8)]
        jobs += [("k", m, 2 + m // 4, (m % 4) * P, "dve" if m % 2 else "act") for m in range(8)]
        jobs += [("v", (h, t), 4 + h, 0, "dve" if t % 2 else "act") for h in range(2) for t in range(4)]
        jobs += [("g", m, 6 + m // 4, (m % 4) * P, "act") for m in range(8)]
    else:
        jobs = [("b", m, 0, m * P, "act") for m in range(4)]
        jobs += [("a", m, 1, m * P, "dve") for m in range(4)]
        jobs += [("q", m, 2, m * P, "act") for m in range(4)]
        jobs += [("k", m, 3, m * P, "act") for m in range(4)]
        jobs += [("v", t, 4, 0, "act") for t in range(2)]
    return jobs


def taken_by(jobs, i):
    eng = jobs[i][4]
    return eng, sum(1 for j in jobs[:i + 1] if j[4] == eng)


def units(layer):
    if layer == "a":
        return [(2 * p + x, kind, kts, x == 1) for p in range(NH // 2)
                for kind, kts in (("lat", (0, 1, 2, 3)), ("ctx", (2, 3))) for x in range(2)]
    if layer == "b":
        return [(h, "lat", (0, 1, 2, 3), h % 2 == 1) for h in range(NH)]
    return [(h, "lat", (0, 1), h % 2 == 1) for h in range(NH2)]


def build(nc, IN, consts_dram, relpad, out):
    CA, CN = const_layout()
    with ExitStack() as ctx:
        def sb(name, shape, dt=F32):
            return ctx.enter_context(nc.sbuf_tensor(name, shape, dt))

        def sem(name):
            return ctx.enter_context(nc.semaphore(name))

        ring = sb("ring", [P, SLOTS, KT * COLS])
        cst = sb("cst", [P, CN])
        H = sb("H", [P, KT, T])
        U = sb("U", [P, KT * T])
        Q = sb("Q", [P, KT * T])
        G = sb("G", [P, KT * T])
        K = sb("K", [P, KT * T])
        prob = sb("prob", [P, 2, 2 * T])
        probT = sb("probT", [P, 2, 2 * T])
        bias = sb("bias", [P, 2, BROWS * GRID_W])
        vec = sb("vec", [P, NVEC])
        conv_taps = sb("conv_taps", [P, 4, CONV_W])
        sil = sb("sil", [P, 3, KT])
        mod = sb("mod", [P, 2, 24, 2])
        mod2 = sb("mod2", [P, 48])
        gain = sb("gain", [P, 2, KT])
        sink = sb("sink", [P, NH])
        soft = sb("soft", [P, 2, 5, 2])
        peak = sb("peak", [1, 1], I32)
        peakf = sb("peakf", [P, 1])
        ps = ctx.enter_context(nc.psum_tensor("ps", [P, 8, 512], F32))

        def cs(name):
            return cst[:, CA[name][0]:CA[name][1]]

        def vc(name, j=0):
            return vec[:, VAT[name] + j:VAT[name] + j + 1]

        ident, ones, meanm, rotm, before = cs("ident"), cs("ones"), cs("mean"), cs("rot"), cs("before")
        eps_ln, eps_rms = cs("eps")[:, 0:1], cs("eps")[:, 1:2]

        xrows = Q[:, :].rearrange("p (t f) -> p t f", t=4)
        vrows = K[:, 0:2 * P].rearrange("p (t f) -> p t f", t=2)
        crows = K[0:CONV_W, 512:512 + HID]
        uT = U[:, :].rearrange("p (j t) -> p j t", j=KT)
        oT = uT
        qT = Q[:, :].rearrange("p (j t) -> p j t", j=KT)
        gT = G[:, :].rearrange("p (j t) -> p j t", j=KT)
        kTa = K[:, 0:1024].rearrange("p (j t) -> p j t", j=2)
        kSa = K[:, 1024:2048].rearrange("p (j t) -> p j t", j=2)
        va = K[:, 2048:3072].rearrange("p (t f) -> p t f", t=4)
        qTb = Q[:, 0:2048].rearrange("p (j t) -> p j t", j=KT)
        gTb = Q[:, 2048:4096].rearrange("p (j t) -> p j t", j=KT)
        kTb = K[:, :].rearrange("p (j t) -> p j t", j=KT)
        vb = G[:, :].rearrange("p (t f) -> p t f", t=4)
        sq = Q[:, :].rearrange("p (j t) -> p j t", j=KT)
        rstd = prob[:, 0, 0:512]
        mixT = U[:, 0:2048].rearrange("p (j t) -> p j t", j=KT)
        h1T = U[:, 2048:4096].rearrange("p (j t) -> p j t", j=KT)
        qTc = K[:, 0:1024].rearrange("p (j t) -> p j t", j=4)
        kTc = K[:, 1024:2048].rearrange("p (j t) -> p j t", j=4)
        vcr = K[:, 2048:3072].rearrange("p (t f) -> p t f", t=2)
        sigb = K[:, 3072:4096].rearrange("p (j t) -> p j t", j=4)
        GLU_W = CONV_W - 1 + S
        glu = G[:, 0:4 * GLU_W].rearrange("p (j t) -> p j t", j=4)
        convo = G[:, 2048:3072].rearrange("p (j t) -> p j t", j=4)
        csq = G[:, 3072:4096].rearrange("p (j t) -> p j t", j=4)
        sq2 = Q[:, 0:2048].rearrange("p (j t) -> p j t", j=KT)
        h2T = Q[:, 2048:4096].rearrange("p (j t) -> p j t", j=KT)
        yacc = U[:, 0:2048]
        h2rows = U[:, 2048:4096].rearrange("p (t f) -> p t f", t=2)
        pick = Q[:, :].rearrange("p (t s) -> p t s", t=2)
        wpick = G[:, :].rearrange("p (t s) -> p t s", t=2)
        wpickT = K[:, :]
        xg = prob[:, 0, :].rearrange("p (j s) -> p j s", j=KT)
        yT = prob[:, 1, :].rearrange("p (j s) -> p j s", j=KT)
        yrows = probT[:, 0, :]
        hidT = probT[:, 1, 0:512].rearrange("p (x k s) -> p x k s", x=2, k=4)
        sgl = probT[:, 1, 512:1024].rearrange("p (x n) -> p x n", x=2)
        route = K[:, 0:1024].rearrange("p (r n) -> p r n", n=2 * 32)
        outrows = Q[:, 0:2048].rearrange("p (t f) -> p t f", t=2)
        wr = prob[:, 1, 0:KT * 36].rearrange("p (j n) -> p j n", j=KT)
        rbias = prob[:, 1, 512:548]
        keysel = sb("keysel", [P, 2, NE])
        wsel = sb("wsel", [P, 2, NE])

        cst_in, vec_in, x_in, sink_in = sem("cst_in"), sem("vec_in"), sem("x_in"), sem("sink_in")
        rel_in, rel_out, rel_zero = sem("rel_in"), sem("rel_out"), sem("rel_zero")
        full = [sem(f"full{i}") for i in range(SLOTS)]
        pe_vec, vec_ok = sem("pe_vec"), sem("vec_ok")
        pe_x, x_ok = sem("pe_x"), sem("x_ok")
        sil_ok = sem("sil_ok")
        st = {n: sem(n + "_done") for n in ("ada0", "a_in", "a_out", "ada1", "b_in", "b_out", "mod_a", "c_in",
                                            "c_out", "mod_b")}
        tk = {(n, e): sem(f"{n}_taken_{e}") for n in ("a_in", "b_in", "c_in") for e in ("act", "dve")}
        tk.update({(n, "dve"): sem(f"{n}_taken_dve") for n in ("a_out", "b_out", "c_out")})
        mod_ok, u_ok, alpha_ok = sem("mod_ok"), sem("u_ok"), sem("alpha_ok")
        rot_done, rope_ok, swap_ok = sem("rot_done"), sem("rope_ok"), sem("swap_ok")
        dve_step, over_step = sem("dve_step"), sem("over_step")
        at = {}
        for L in "abc":
            for n in ("scores", "max", "exp", "prob", "turned", "turn_act", "turn_dve", "pv", "o"):
                at[L, n] = sem(f"{L}_{n}")
        bias_in, bias_ok, bias_used = [sem("bias_in0"), sem("bias_in1")], sem("bias_ok"), sem("bias_used")
        nm = {}
        for N in ("lna", "lnb", "rms1", "lnc", "rms2", "rmsf"):
            for n in ("mean", "cent", "sq", "var", "std", "rs", "out"):
                nm[N, n] = sem(f"{N}_{n}")
        glu_ok, conv_ok, zero_ok = sem("glu_ok"), sem("conv_ok"), sem("zero_ok")
        rt_in, logits, h2r_turn, h2r_ok = sem("rt_in"), sem("logits"), sem("h2r_turn"), sem("h2r_ok")
        gsub, gexp, tdif, texp, sel_ok, ranks = (sem(n) for n in ("gsub", "gexp", "tdif", "texp", "sel_ok", "ranks"))
        peak_ok, pick_ok, wpick_ok = sem("peak_ok"), sem("pick_ok"), sem("wpick_ok")
        wturn, wturn_ok = sem("wturn"), sem("wturn_ok")
        gath, xg_act, xg_dve = sem("gath"), sem("xg_act"), sem("xg_dve")
        gu, sg_ok, hid_ok = sem("gu"), sem("sg_ok"), sem("hid_ok")
        down, y_act, y_dve = sem("down"), sem("y_act"), sem("y_dve")
        yturn, yr_act, yr_dve = sem("yturn"), sem("yr_act"), sem("yr_dve")
        scat, acc_ok, acc_zero = sem("scat"), sem("acc_ok"), sem("acc_zero")
        oturn, orow_ok, out_done = sem("oturn"), sem("orow_ok"), sem("out_done")
        acc2_ok = sem("acc2_ok")

        UN = {L: units(L) for L in "abc"}
        JOBS = {s: in_jobs(s) for s in ("a_in", "b_in", "c_in")}
        used = {}
        for s in JOBS:
            used[s] = [sum(1 for j in JOBS[s] if j[2] <= c) for c in range(1 + max(j[2] for j in JOBS[s]))]
        for s in ("a_out", "b_out", "c_out"):
            used[s] = [4, 8]
        for s in ("ada0", "ada1", "mod_a", "mod_b"):
            used[s] = [c + 1 for c in range(6)]

        def slot(n):
            return ring[:, n % SLOTS, :].rearrange("p (k n) -> p k n", k=KT)

        def turned_by_dve(L, n):
            return sum(1 for u in UN[L][:n] if len(u[2]) == 4)

        def dslot(n):
            return ring[:, n, :].rearrange("p (k n) -> p k n", k=4)

        block = ctx.enter_context(nc.Block())

        @block.sync
        def _(sp):
            sp.dma_start(cst[:, :], consts_dram).then_inc(cst_in, 16)
            sp.dma_start(xrows[:, 0:2, :], IN["x"][0].rearrange("(t p) f -> p t f", p=P)).then_inc(x_in, 16)
            sp.dma_start(xrows[:, 2:4, :], IN["ctx"][0].rearrange("(t p) f -> p t f", p=P)).then_inc(x_in, 16)
            for n, (stage, src, l, c) in enumerate(PLAN):
                if n >= SLOTS:
                    was = PLAN[n - SLOTS][0]
                    sp.wait_ge(st[was], used[was][n - SLOTS - STAGE_AT[was]])
                w = IN[src][l, :, c * COLS:(c + 1) * COLS].rearrange("(k p) n -> p k n", p=P)
                sp.dma_start(slot(n), w).then_inc(full[n % SLOTS], 16)

            wg, wu, wd = (IN[f"w_exp_{n}_2"][0] for n in ("gate", "up", "down"))

            def load_expert(x, e):
                yield 3 * x, wg[bass.ds(e, 1)].rearrange("e (k p) n -> p (e k) n", p=P), slot
                yield 3 * x + 1, wu[bass.ds(e, 1)].rearrange("e (k p) n -> p (e k) n", p=P), slot
                yield 3 * x + 2, wd[bass.ds(e, 1)].rearrange("e (k p) n -> p (e k) n", p=P), dslot

            for x in range(2):
                for s, w, view in load_expert(x, x):
                    sp.wait_ge(st["mod_b"], s + 1)
                    sp.dma_start(view(s), w).then_inc(full[s], 16)

            def stream(r, pair):
                n = r * PAIRS + pair
                for x in range(2):
                    for i, (s, w, view) in enumerate(load_expert(x, pair * 2 + x)):
                        sp.wait_ge(down if i == 2 else gu, (n - 1) * 2 + x + 1)
                        sp.dma_start(view(s), w).then_inc(full[s], 16)

            with sp.Fori(1, PAIRS) as pair:
                stream(0, pair)
            sp.wait_ge(peak_ok, 1)
            most = sp.value_load(peak[:, :], min_val=0, max_val=S)
            for r in range(1, PASSES):
                with sp.If(most > CAP * r):
                    with sp.Fori(0, PAIRS) as pair:
                        stream(r, pair)
            sp.wait_ge(orow_ok, 4)
            sp.dma_start(out[0].rearrange("(t p) f -> p t f", p=P), outrows).then_inc(out_done, 16)
            sp.wait_ge(out_done, 16)

        @block.gpsimd
        def _(pool):
            pool.wait_ge(cst_in, 16)
            padr = probT[0:120, 0, 0:2 * PADW].rearrange("p (a w) -> p a w", a=2)
            pool.memset(padr, 0.0).then_inc(rel_zero, 1)
            pool.wait_ge(rel_zero, 1)
            relr = probT[0:120, 1, 0:2 * REL_W].rearrange("p (a w) -> p a w", a=2)
            pool.dma_start(relr, IN["b_rel_bias"][0].rearrange("h d w -> (h d) w").rearrange("(a p) w -> p a w", a=2)
                           ).then_inc(rel_in, 16)
            pool.wait_ge(rel_in, 16)
            backwards = bass.AP(relr.tensor, relr.offset + REL_W - 1,
                                [list(relr.ap[0]), [REL_W, 2], [-1, REL_W]])
            pool.tensor_copy(padr[:, :, GRID_W - KW:GRID_W - KW + REL_W], backwards).then_inc(rel_zero, 1)
            pool.wait_ge(rel_zero, 2)
            pool.dma_start(relpad.rearrange("(a p) w -> p a w", a=2), padr).then_inc(rel_out, 16)
            pool.wait_ge(rel_out, 16)
            for h in range(NH):
                if h >= 2:
                    pool.wait_ge(bias_used, h - 1)
                for half in range(2):
                    first = (h * REL_H + BROWS - 1 - half) * PADW
                    src = bass.AP(relpad.tensor, first, [[1, GRID_W], [PADW, BROWS], [1, GRID_W]])
                    pool.dma_start(bias[half * 64:half * 64 + 64, h % 2].rearrange("p (r c) -> p r c", r=BROWS),
                                   src).then_inc(bias_in[h % 2], 16)
                pool.wait_ge(bias_in[h % 2], 32 * (h // 2 + 1))
                tile = bias[:, h % 2].rearrange("p (r c) -> p r c", r=BROWS)
                pool.tensor_tensor(tile, tile, cs("col").unsqueeze(1).broadcast_to([P, BROWS, GRID_W]),
                                   ALU.add).then_inc(bias_ok, 1)
            pool.wait_ge(at["b", "pv"], NH)
            pool.memset(glu[:, :, 0:CONV_W - 1], 0.0).then_inc(zero_ok, 1)
            pool.wait_ge(tk["c_out", "dve"], KT)
            pool.memset(yacc, 0.0).then_inc(acc_zero, 1)

        @block.tensor
        def _(pe):
            mm, tr = nc.tensor.matmul, nc.tensor.transpose

            def landed(n):
                pe.wait_ge(full[n % SLOTS], 16 * (n // SLOTS + 1))

            pe.wait_ge(cst_in, 16)
            pe.wait_ge(vec_in, 16 * (len(VEC) + 1))
            tr(ps[:, 0, 0:P], vrows[:, 0, :], ident)
            tr(ps[:, 0, P:P + VROWS1], vrows[0:VROWS1, 1, :], ident[0:VROWS1, 0:VROWS1])
            for c in range(4):
                last = tr(ps[:, 0, 256 + 32 * c:256 + 32 * c + CONV_W], crows[:, c * P:(c + 1) * P],
                          ident[0:CONV_W, 0:CONV_W])
            last.then_inc(pe_vec, 1)
            pe.wait_ge(x_in, 32)
            for j in range(KT):
                if j >= 4:
                    pe.wait_ge(x_ok, j - 3)
                for t in range(4):
                    last = tr(ps[:, 1 + j % 4, t * P:(t + 1) * P], xrows[:, t, j * P:(j + 1) * P], ident)
                last.then_inc(pe_x, 1)

            def modulation(stage, chunks, vecs):
                nv = len(vecs)
                for c in chunks:
                    n = STAGE_AT[stage] + c
                    landed(n)
                    for m in range(4):
                        col = (4 * c + m) * nv
                        for k in range(KT):
                            last = mm(ps[:, 7, col:col + nv], slot(n)[:, k, m * P:(m + 1) * P],
                                      sil[:, vecs[0]:vecs[-1] + 1, k], start=(k == 0), stop=(k == KT - 1))
                    last.then_inc(st[stage], 1)

            pe.wait_ge(sil_ok, 1)
            modulation("ada0", range(6), (0, 1))

            def in_proj(stage, src, widths, after=None):
                jobs = JOBS[stage]
                seen = -1
                for i, (kind, m, c, col, _) in enumerate(jobs):
                    n = STAGE_AT[stage] + c
                    if c != seen:
                        landed(n)
                        seen = c
                    if i >= 4:
                        e, cnt = taken_by(jobs, i - 4)
                        pe.wait_ge(tk[stage, e], cnt)
                    b = i % 4
                    for k in range(KT):
                        if i == 0:
                            pe.wait_ge(*src_ready(stage, k))
                        w = slot(n)[:, k, :]
                        if kind == "v":
                            t = m[1] if stage == "b_in" else m
                            wid = 256 if stage == "a_in" else 512
                            last = mm(ps[:, b, 0:wid], src[:, k, t * P:(t + 1) * P], w[:, col:col + wid],
                                      start=(k == 0), stop=(k == KT - 1))
                        else:
                            wid = widths[kind]
                            last = mm(ps[:, b, 0:wid], w[:, col:col + P], src[:, k, 0:wid],
                                      start=(k == 0), stop=(k == KT - 1))
                    last.then_inc(st[stage], 1)
                    if after:
                        after(i)

            def src_ready(stage, k):
                if stage == "a_in":
                    return u_ok, k + 1
                if stage == "b_in":
                    return u_ok, KT + k + 1
                return nm["rms1", "out"], k + 1

            def rotate(i):
                if 1 <= i <= 10:
                    r = i - 1
                    pe.wait_ge(tk["a_in", "act"], r + 1)
                    if r >= 2:
                        pe.wait_ge(rope_ok, r - 1)
                    src = qT[:, r, 0:S] if r < 8 else kTa[:, r - 8, 0:S]
                    mm(ps[:, 4 + r % 2, 0:S], rotm, src, start=True, stop=True).then_inc(rot_done, 1)

            in_proj("a_in", uT, {"q": T, "k": T, "g": T}, rotate)

            def attention(L, q_of, k_of, v_of):
                un = UN[L]

                def scores(n):
                    h, kind, kts, _ = un[n]
                    for qb in range(2):
                        last = mm(ps[:, 2 * (n % 2) + qb, 0:len(kts) * P], q_of(h, kind, qb), k_of(h, kts),
                                  start=True, stop=True)
                    last.then_inc(at[L, "scores"], 1)

                scores(0)
                scores(1)
                for n, (h, kind, kts, closes) in enumerate(un):
                    pe.wait_ge(at[L, "prob"], n + 1)
                    for i in range(len(kts)):
                        for qb in range(2):
                            last = tr(ps[:, 4 + i // 2, (i % 2) * S + qb * P:(i % 2) * S + (qb + 1) * P],
                                      prob[:, n % 2, qb * T + i * P:qb * T + (i + 1) * P], ident)
                    last.then_inc(at[L, "turned"], 1)
                    if n + 2 < len(un):
                        scores(n + 2)
                    pe.wait_ge(at[L, "turn_act"], n + 1)
                    if len(kts) == 4:
                        pe.wait_ge(at[L, "turn_dve"], turned_by_dve(L, n + 1))
                    g = n // 2
                    if n % 2 == 0 and g >= 2:
                        pe.wait_ge(at[L, "o"], g - 1)
                    r0 = (h % 2) * HD
                    for i, kt in enumerate(kts):
                        last = mm(ps[r0:r0 + HD, 6 + g % 2, 0:S], v_of(h, kt),
                                  probT[:, n % 2, i * S:(i + 1) * S], start=(i == 0), stop=(i == len(kts) - 1))
                    last.then_inc(at[L, "pv"], 1)

            def half(h):
                return slice((h % 2) * HD, (h % 2) * HD + HD)

            def q_a(h, kind, qb):
                c0 = (0 if kind == "lat" else S) + qb * P
                return qT[half(h), h // 2, c0:c0 + P]

            def k_a(h, kts):
                kv = h // (NH // KVH)
                src = kTa if kv % 2 == h % 2 else kSa
                return src[half(h), kv // 2, kts[0] * P:(kts[-1] + 1) * P]

            def v_a(h, kt):
                kv = h // (NH // KVH)
                return va[:, kt, kv * HD:(kv + 1) * HD]

            pe.wait_ge(rope_ok, 10)
            pe.wait_ge(swap_ok, 2)
            pe.wait_ge(tk["a_in", "dve"], 4)
            pe.wait_ge(tk["a_in", "act"], 18)
            attention("a", q_a, k_a, v_a)

            def out_proj(stage, src, width):
                for m in range(KT):
                    n = STAGE_AT[stage] + m // 4
                    if m % 4 == 0:
                        landed(n)
                    if m >= 4:
                        pe.wait_ge(tk[stage, "dve"], m - 3)
                    for k in range(KT):
                        last = mm(ps[:, m % 4, 0:width], slot(n)[:, k, (m % 4) * P:(m % 4 + 1) * P], src[:, k, 0:width],
                                  start=(k == 0), stop=(k == KT - 1))
                    last.then_inc(st[stage], 1)

            def feature_sum(bank, mat, src, n, width, ready, done):
                for j in range(n):
                    pe.wait_ge(ready, j + 1)
                    last = mm(ps[:, bank, 0:width], mat, src[:, j, 0:width], start=(j == 0), stop=(j == n - 1))
                last.then_inc(done, 1)

            pe.wait_ge(at["a", "o"], NH)
            out_proj("a_out", oT, T)
            feature_sum(4, meanm, H, KT, T, tk["a_out", "dve"], nm["lna", "mean"])
            modulation("ada1", range(3), (0, 1))
            feature_sum(5, meanm, sq, KT, T, nm["lna", "sq"], nm["lna", "var"])
            modulation("ada1", range(3, 6), (0, 1))

            in_proj("b_in", uT, {"q": S, "k": T, "g": S})
            pe.wait_ge(tk["b_in", "dve"], sum(j[4] == "dve" for j in JOBS["b_in"]))
            pe.wait_ge(tk["b_in", "act"], sum(j[4] == "act" for j in JOBS["b_in"]))
            attention("b", lambda h, kind, qb: qTb[half(h), h // 2, qb * P:(qb + 1) * P],
                      lambda h, kts: kTb[half(h), h // 2, :],
                      lambda h, kt: vb[:, kt, h * HD:(h + 1) * HD])
            pe.wait_ge(at["b", "o"], NH // 2)
            out_proj("b_out", oT, S)
            feature_sum(4, meanm, H, KT, S, tk["b_out", "dve"], nm["lnb", "mean"])
            modulation("mod_a", range(3), (2,))
            feature_sum(5, meanm, sq, KT, S, nm["lnb", "sq"], nm["lnb", "var"])
            modulation("mod_a", range(3, 6), (2,))
            feature_sum(4, meanm, sq2, KT, S, nm["rms1", "sq"], nm["rms1", "var"])

            in_proj("c_in", h1T, {"a": S, "b": S, "q": S, "k": S})
            pe.wait_ge(tk["c_in", "act"], sum(j[4] == "act" for j in JOBS["c_in"]))
            pe.wait_ge(tk["c_in", "dve"], 4)
            attention("c", lambda h, kind, qb: qTc[half(h), h // 2, qb * P:(qb + 1) * P],
                      lambda h, kts: kTc[half(h), h // 2, :],
                      lambda h, kt: vcr[:, kt, h * HD:(h + 1) * HD])
            feature_sum(4, ones, convo, 4, S, conv_ok, nm["lnc", "mean"])
            feature_sum(5, ones, csq, 4, S, nm["lnc", "sq"], nm["lnc", "var"])
            pe.wait_ge(at["c", "o"], NH2 // 2)
            pe.wait_ge(nm["lnc", "out"], 4)
            out_proj("c_out", mixT, S)
            feature_sum(4, meanm, sq2, KT, S, nm["rms2", "sq"], nm["rms2", "var"])
            pe.wait_ge(mod_ok, 3)
            for c in range(6):
                n = STAGE_AT["mod_b"] + c
                landed(n)
                for m in range(4):
                    for k in range(KT):
                        last = mm(ps[:, 7, 4 * c + m:4 * c + m + 1], slot(n)[:, k, m * P:(m + 1) * P],
                                  sil[:, 2:3, k], start=(k == 0), stop=(k == KT - 1))
                last.then_inc(st["mod_b"], 1)

            pe.wait_ge(rt_in, 64)
            pe.wait_ge(nm["rms2", "out"], KT)
            for t in range(2):
                for k in range(KT):
                    last = mm(ps[:, 0, t * 64:t * 64 + 36], h2T[:, k, t * P:(t + 1) * P], wr[:, k, :],
                              start=(k == 0), stop=(k == KT - 1))
            last.then_inc(logits, 1)
            for b in range(4):
                t, f0 = b // 2, (b % 2) * 4
                for f in range(4):
                    last = tr(ps[:, 1 + b, f * P:(f + 1) * P], h2T[:, f0 + f, t * P:(t + 1) * P], ident)
                last.then_inc(h2r_turn, 1)
            sel = route[:, 14, :].rearrange("p (t e) -> p t e", t=2)
            pe.wait_ge(sel_ok, 1)
            mm(ps[:, 5, 0:NE], before, sel[:, 0, :], start=True, stop=True)
            mm(ps[:, 5, NE:2 * NE], ones, sel[:, 0, :], start=True, stop=False)
            mm(ps[:, 5, NE:2 * NE], before, sel[:, 1, :], start=False, stop=True)
            mm(ps[:, 5, 64:64 + NE], ones, sel[:, 0, :], start=True, stop=False)
            mm(ps[:, 5, 64:64 + NE], ones, sel[:, 1, :], start=False, stop=True).then_inc(ranks, 1)

            def turn_weights(r):
                pe.wait_ge(wpick_ok, r + 1)
                for i in range(PAIRS // 2):
                    if i >= 4:
                        pe.wait_ge(wturn_ok, r * PAIRS // 2 + i - 3)
                    for x in range(2):
                        for t in range(2):
                            last = tr(ps[:, 4 + i % 4, (2 * x + t) * P:(2 * x + t + 1) * P],
                                      wpick[:, t, (2 * i + x) * P:(2 * i + x + 1) * P], ident)
                    last.then_inc(wturn, 1)
                pe.wait_ge(wturn_ok, (r + 1) * PAIRS // 2)

            def experts(r, pair):
                n = r * PAIRS + pair
                if not isinstance(pair, int):
                    pe.wait_ge(acc_ok, n * 4)
                for j in range(KT):
                    for t in range(2):
                        last = mm(ps[:, j // 4, (j % 4) * P:(j % 4 + 1) * P], h2rows[:, t, j * P:(j + 1) * P],
                                  pick[:, t, bass.ds(pair * P, P)], start=(t == 0), stop=(t == 1))
                    if j % 4 == 3:
                        last.then_inc(gath, 1)
                pe.wait_ge(xg_act, n + 1)
                pe.wait_ge(xg_dve, n + 1)
                for x in range(2):
                    for i in range(2):
                        s = 3 * x + i
                        pe.wait_ge(full[s], (n + ROUNDS + 1) * 16)
                        for m in range(4):
                            for k in range(KT):
                                last = mm(ps[:, 2 + x, i * 256 + m * CAP:i * 256 + (m + 1) * CAP],
                                          slot(s)[:, k, m * P:(m + 1) * P], xg[:, k, x * CAP:(x + 1) * CAP],
                                          start=(k == 0), stop=(k == KT - 1))
                    last.then_inc(gu, 1)
                for x in range(2):
                    s = 3 * x + 2
                    pe.wait_ge(full[s], (n + ROUNDS + 1) * 16)
                    pe.wait_ge(hid_ok, n * 2 + x + 1)
                    for m in range(KT):
                        for k in range(4):
                            last = mm(ps[:, 4 + m // 4, (m % 4) * P + x * CAP:(m % 4) * P + (x + 1) * CAP],
                                      dslot(s)[:, k, m * P:(m + 1) * P], hidT[:, x, k, :],
                                      start=(k == 0), stop=(k == 3))
                    last.then_inc(down, 1)
                pe.wait_ge(y_act, n + 1)
                pe.wait_ge(y_dve, n + 1)
                for m in range(KT):
                    last = tr(ps[:, 6 + m // 4, (m % 4) * P:(m % 4 + 1) * P], yT[:, m, :], ident)
                    if m % 4 == 3:
                        last.then_inc(yturn, 1)
                pe.wait_ge(yr_act, n + 1)
                pe.wait_ge(yr_dve, n + 1)
                for m in range(KT):
                    last = mm(ps[:, m // 2, (m % 2) * S:(m % 2 + 1) * S], yrows[:, m * P:(m + 1) * P],
                              wpickT[:, bass.ds(pair * S, S)], start=True, stop=True)
                    if m % 2 == 1:
                        last.then_inc(scat, 1)

            turn_weights(0)
            pe.wait_ge(pick_ok, 1)
            pe.wait_ge(h2r_ok, 4)
            experts(0, FIRST)
            with pe.Fori(1, PAIRS) as pair:
                experts(0, pair)
            pe.wait_ge(peak_ok, 1)
            most = pe.value_load(peak[:, :], min_val=0, max_val=S)
            for r in range(1, PASSES):
                with pe.If(most > CAP * r):
                    turn_weights(r)
                    pe.wait_ge(pick_ok, r + 1)
                    with pe.Fori(0, PAIRS) as pair:
                        experts(r, pair)

            feature_sum(4, meanm, sq2, KT, S, nm["rmsf", "sq"], nm["rmsf", "var"])
            pe.wait_ge(nm["rmsf", "out"], KT)
            for b in range(4):
                t, f0 = b // 2, (b % 2) * 4
                for f in range(4):
                    last = tr(ps[:, b, f * P:(f + 1) * P], H[:, f0 + f, t * P:(t + 1) * P], ident)
                last.then_inc(oturn, 1)

        @block.scalar
        def _(act):
            a = nc.scalar.activation
            row = 0
            for name, n in VEC:
                src = IN[name]
                names = "a b" if len(src.shape) == 2 else "b"
                flat = src.rearrange("a b -> (a b)") if len(src.shape) == 2 else src
                r, t = row % P, row // P
                act.dma_start(vrows[r:r + n, t, :], flat.rearrange("(r f) -> r f", f=P)).then_inc(vec_in, 16)
                row += n
            act.dma_start(crows, IN["conv_w_2"][0]).then_inc(vec_in, 16)
            act.dma_start(sink[:, :], IN["a_sink"].broadcast_to([P, NH])).then_inc(sink_in, 16)

            act.wait_ge(cst_in, 16)
            act.wait_ge(vec_ok, 1)
            a(sil[:, :, :], vec[:, 0:3 * KT].rearrange("p (v k) -> p v k", v=3), ACT.Silu).then_inc(sil_ok, 1)

            def evac_in(stage, how):
                jobs = JOBS[stage]
                for i, (kind, m, _, _, eng) in enumerate(jobs):
                    if eng == "act":
                        act.wait_ge(st[stage], i + 1)
                        how(kind, m, i % 4).then_inc(tk[stage, "act"], 1)

            def from_a(kind, m, b):
                if kind == "q":
                    return a(qT[:, m, :], ps[:, b, :], ACT.Copy, scale=HD ** -0.5)
                if kind == "k":
                    return a(kTa[:, m, :], ps[:, b, :], ACT.Copy)
                return a(gT[:, m, :], ps[:, b, :], ACT.Silu)

            evac_in("a_in", from_a)
            for j in range(KT):
                act.wait_ge(u_ok, j + 1)
                a(H[:, j, :], H[:, j, :], ACT.Copy, scale=ALPHA).then_inc(alpha_ok, 1)

            def attention(L):
                un = UN[L]

                def exps(n):
                    h, kind, kts, _ = un[n]
                    w = len(kts) * P
                    act.wait_ge(at[L, "max"], n + 1)
                    if n >= 2:
                        act.wait_ge(at[L, "turned"], n - 1)
                    if n == 0 and L == "a":
                        act.wait_ge(sink_in, 16)
                    s = soft[:, n % 2]
                    for qb in range(2):
                        last = a(prob[:, n % 2, qb * T:qb * T + w], ps[:, 2 * (n % 2) + qb, 0:w], ACT.Exp,
                                 bias=s[:, 1, qb:qb + 1], accum_out=None if L == "c" else s[:, 2, qb:qb + 1])
                    if L == "a":
                        last = a(s[:, 3, :], s[:, 1, :], ACT.Exp, bias=sink[:, h:h + 1])
                    last.then_inc(at[L, "exp"], 1)

                exps(0)
                for n in range(len(un)):
                    act.wait_ge(at[L, "turned"], n + 1)
                    if n >= 2:
                        act.wait_ge(at[L, "pv"], n - 1)
                    a(probT[:, n % 2, 0:512], ps[:, 4, :], ACT.Copy).then_inc(at[L, "turn_act"], 1)
                    if n + 1 < len(un):
                        exps(n + 1)

            attention("a")

            def squares(N, src, dst, n, width, ready, base=0):
                for j in range(n):
                    act.wait_ge(ready, base + j + 1)
                    a(dst[:, j, 0:width], src[:, j, 0:width], ACT.Square).then_inc(nm[N, "sq"], 1)

            def root(N, bank, width, eps, scale=1.0):
                act.wait_ge(nm[N, "var"], 1)
                a(rstd[:, 0:width], ps[:, bank, 0:width], ACT.Sqrt, bias=eps, scale=scale).then_inc(nm[N, "std"], 1)

            squares("lna", H, sq, KT, T, nm["lna", "cent"])
            root("lna", 5, T, eps_ln)

            def from_b(kind, m, b):
                if kind == "q":
                    return a(qTb[:, m, :], ps[:, b, 0:S], ACT.Copy, scale=HD ** -0.5)
                if kind == "k":
                    return a(kTb[:, m, :], ps[:, b, :], ACT.Copy)
                if kind == "v":
                    return a(vb[:, m[1], m[0] * 512:(m[0] + 1) * 512], ps[:, b, :], ACT.Copy)
                return a(gTb[:, m, :], ps[:, b, 0:S], ACT.Silu)

            evac_in("b_in", from_b)
            for j in range(KT):
                act.wait_ge(u_ok, KT + j + 1)
                a(H[:, j, 0:S], H[:, j, 0:S], ACT.Copy, scale=ALPHA).then_inc(alpha_ok, 1)
            attention("b")
            squares("lnb", H, sq, KT, S, nm["lnb", "cent"])
            root("lnb", 5, S, eps_ln)
            squares("rms1", H, sq2, KT, S, nm["lnb", "out"])
            root("rms1", 4, S, eps_rms)

            def from_c(kind, m, b):
                if kind == "b":
                    return a(sigb[:, m, :], ps[:, b, 0:S], ACT.Sigmoid)
                if kind == "q":
                    return a(qTc[:, m, :], ps[:, b, 0:S], ACT.Copy, scale=HD ** -0.5)
                if kind == "k":
                    return a(kTc[:, m, :], ps[:, b, 0:S], ACT.Copy)
                return a(vcr[:, m, :], ps[:, b, :], ACT.Copy)

            evac_in("c_in", from_c)
            attention("c")
            squares("lnc", convo, csq, 4, S, nm["lnc", "cent"])
            root("lnc", 5, S, eps_rms, scale=1.0 / HID)
            for j in range(4):
                act.wait_ge(acc2_ok, j + 1)
                a(mixT[:, 4 + j, :], convo[:, j, :], ACT.Silu, scale=vc("conv_ln_g_2", j),
                  bias=vc("conv_ln_b_2", j)).then_inc(nm["lnc", "out"], 1)
            squares("rms2", H, sq2, KT, S, tk["c_out", "dve"])
            act.dma_start(wr[:, :, 0:NG], IN["w_router_group_2"][0].rearrange("(k p) n -> p k n", p=P)
                          ).then_inc(rt_in, 16)
            act.dma_start(wr[:, :, NG:NG + NE], IN["w_router_expert_2"][0].rearrange("(k p) n -> p k n", p=P)
                          ).then_inc(rt_in, 16)
            act.dma_start(rbias[:, 0:NG], IN["b_router_group_2"].broadcast_to([P, NG])).then_inc(rt_in, 16)
            act.dma_start(rbias[:, NG:NG + NE], IN["b_router_expert_2"].broadcast_to([P, NE])).then_inc(rt_in, 16)
            root("rms2", 4, S, eps_rms)

            for b in range(0, 4, 2):
                act.wait_ge(h2r_turn, b + 1)
                a(h2rows[:, b // 2, 0:512], ps[:, 1 + b, :], ACT.Copy).then_inc(h2r_ok, 1)
            act.wait_ge(gsub, 1)
            a(route[:, 2, 0:8], route[:, 1, 0:8], ACT.Exp).then_inc(gexp, 1)
            act.wait_ge(tdif, 1)
            a(route[:, 11, 2:4], route[:, 11, 0:2], ACT.Exp).then_inc(texp, 1)

            def turn_weights(r):
                for i in range(PAIRS // 2):
                    act.wait_ge(wturn, r * PAIRS // 2 + i + 1)
                    a(wpickT[:, i * 512:(i + 1) * 512], ps[:, 4 + i % 4, :], ACT.Copy).then_inc(wturn_ok, 1)

            def experts(r, pair):
                n = r * PAIRS + pair
                act.wait_ge(gath, n * 2 + 1)
                a(xg[:, 0:4, :], ps[:, 0, :], ACT.Copy).then_inc(xg_act, 1)
                for x in range(2):
                    act.wait_ge(gu, n * 2 + x + 1)
                    a(sgl[:, x, :], ps[:, 2 + x, 0:256], ACT.Silu).then_inc(sg_ok, 1)
                act.wait_ge(down, n * 2 + 2)
                a(yT[:, 0:4, :], ps[:, 4, :], ACT.Copy).then_inc(y_act, 1)
                act.wait_ge(yturn, n * 2 + 1)
                a(yrows[:, 0:512], ps[:, 6, :], ACT.Copy).then_inc(yr_act, 1)

            turn_weights(0)
            with act.Fori(0, PAIRS) as pair:
                experts(0, pair)
            act.wait_ge(peak_ok, 1)
            most = act.value_load(peak[:, :], min_val=0, max_val=S)
            for r in range(1, PASSES):
                with act.If(most > CAP * r):
                    turn_weights(r)
                    with act.Fori(0, PAIRS) as pair:
                        experts(r, pair)

            squares("rmsf", H, sq2, KT, S, nm["rmsf", "cent"])
            root("rmsf", 4, S, eps_rms)
            for b in range(0, 4, 2):
                act.wait_ge(oturn, b + 1)
                a(outrows[:, b // 2, 0:512], ps[:, b, :], ACT.Copy).then_inc(orow_ok, 1)

        @block.vector
        def _(dve):
            v = nc.vector
            steps = [0]

            def step(ins):
                steps[0] += 1
                ins.then_inc(dve_step, 1)

            def settle():
                dve.wait_ge(dve_step, steps[0])

            over = [0]

            def do_over(ins):
                over[0] += 1
                ins.then_inc(over_step, 1)
                dve.wait_ge(over_step, over[0])

            dve.wait_ge(cst_in, 16)
            dve.wait_ge(pe_vec, 1)
            step(v.tensor_copy(conv_taps[:, :, :],
                               ps[:, 0, 256:384].rearrange("p (c k) -> p c k", c=4)[:, :, 0:CONV_W]))
            v.tensor_copy(vec[:, :], ps[:, 0, 0:NVEC]).then_inc(vec_ok, 1)
            for j in range(KT):
                dve.wait_ge(pe_x, j + 1)
                v.tensor_copy(H[:, j, :], ps[:, 1 + j % 4, :]).then_inc(x_ok, 1)

            def take_modulation(l):
                stage = f"ada{l}"
                dve.wait_ge(st[stage], 6)
                if l == 0:
                    dve.wait_ge(vec_ok, 1)
                b = vec[:, VAT["b_ada"] + 24 * l:VAT["b_ada"] + 24 * (l + 1)]
                step(v.tensor_tensor(mod[:, l], ps[:, 7, 0:48].rearrange("p (m c) -> p m c", c=2),
                                     b.unsqueeze(2).broadcast_to([P, 24, 2]), ALU.add))
                settle()
                v.tensor_scalar(mod[:, l, 8:16, :], mod[:, l, 8:16, :], 1.0, None, ALU.add).then_inc(mod_ok, 1)
                dve.wait_ge(mod_ok, l + 1)

            def modulate(l):
                for j in range(KT):
                    step(v.tensor_scalar(uT[:, j, 0:S], H[:, j, 0:S], mod[:, l, 8 + j, 0:1], mod[:, l, j, 0:1],
                                         ALU.mult, ALU.add))
                    v.tensor_scalar(uT[:, j, S:T], H[:, j, S:T], mod[:, l, 8 + j, 1:2], mod[:, l, j, 1:2],
                                    ALU.mult, ALU.add).then_inc(u_ok, 1)

            take_modulation(0)
            dve.wait_ge(x_ok, KT)
            modulate(0)

            tmp = probT[:, 0, 0:512].rearrange("p (a t) -> p a t", a=2)
            dve.wait_ge(rel_out, 16)

            def rope(r):
                x = qT[:, r, 0:S] if r < 8 else kTa[:, r - 8, 0:S]
                dve.wait_ge(tk["a_in", "act"], r + 1)
                if r >= 1:
                    dve.wait_ge(rope_ok, r)
                step(v.tensor_tensor(tmp[:, 0, :], x, cs("cos"), ALU.mult))
                dve.wait_ge(rot_done, r + 1)
                step(v.tensor_tensor(tmp[:, 1, :], ps[:, 4 + r % 2, 0:S], cs("sin"), ALU.mult))
                settle()
                v.tensor_tensor(x, tmp[:, 0, :], tmp[:, 1, :], ALU.add).then_inc(rope_ok, 1)

            for r in range(10):
                rope(r)
                if r == 9:
                    for t in range(4):
                        dve.wait_ge(st["a_in"], 10 + t + 1)
                        v.tensor_copy(va[:, t, :], ps[:, (10 + t) % 4, 0:256]).then_inc(tk["a_in", "dve"], 1)
            dve.wait_ge(rope_ok, 10)
            for x in range(2):
                v.tensor_copy(kSa[64 * x:64 * x + 64], kTa[64 * (1 - x):64 * (1 - x) + 64]).then_inc(swap_ok, 1)

            def attention(L, prepare):
                un = UN[L]

                def row_max(n):
                    h, kind, kts, _ = un[n]
                    w = len(kts) * P
                    dve.wait_ge(at[L, "scores"], n + 1)
                    prepare(n, h, kind)
                    sc = ps[:, 2 * (n % 2):2 * (n % 2) + 2, 0:w]
                    s = soft[:, n % 2]
                    if n >= 2:
                        dve.wait_ge(at[L, "prob"], n - 1)
                    if L == "a":
                        step(v.tensor_reduce(s[:, 0, :], sc, AX.X, ALU.max))
                        settle()
                        v.tensor_scalar(s[:, 1, :], s[:, 0, :], sink[:, h:h + 1], -1.0, ALU.max, ALU.mult
                                        ).then_inc(at[L, "max"], 1)
                    else:
                        v.tensor_reduce(s[:, 1, :], sc, AX.X, ALU.max, negate=True).then_inc(at[L, "max"], 1)

                def normalise(n):
                    h, kind, kts, _ = un[n]
                    w = len(kts) * P
                    s = soft[:, n % 2]
                    dve.wait_ge(at[L, "exp"], n + 1)
                    if L == "a":
                        step(v.tensor_tensor(s[:, 2, :], s[:, 2, :], s[:, 3, :], ALU.add))
                        settle()
                    if L == "c":
                        mult = cs("mult").rearrange("p (q k) -> p q k", q=2)
                        for qb in range(2):
                            pr = prob[:, n % 2, qb * T:qb * T + w]
                            step(v.scalar_tensor_tensor(pr, pr, 1.0, mult[:, qb, :], ALU.mult, ALU.mult,
                                                        accum_out=s[:, 2, qb:qb + 1]))
                        settle()
                    step(v.reciprocal(s[:, 4, :], s[:, 2, :]))
                    settle()
                    for qb in range(2):
                        pr = prob[:, n % 2, qb * T:qb * T + w]
                        last = v.tensor_scalar(pr, pr, s[:, 4, qb:qb + 1], None, ALU.mult)
                    last.then_inc(at[L, "prob"], 1)

                def take_out(n):
                    g = n // 2
                    h, kind = un[n][0], un[n][1]
                    dve.wait_ge(at[L, "pv"], n + 1)
                    src = ps[:, 6 + g % 2, 0:S]
                    j, c0 = h // 2, 0 if kind == "lat" else S
                    if L == "a":
                        o = v.tensor_tensor(oT[:, j, c0:c0 + S], src, gT[:, j, c0:c0 + S], ALU.mult)
                    elif L == "b":
                        o = v.tensor_tensor(oT[:, j, 0:S], src, gTb[:, j, :], ALU.mult)
                    else:
                        o = v.tensor_copy(mixT[:, j, :], src)
                    o.then_inc(at[L, "o"], 1)

                row_max(0)
                normalise(0)
                row_max(1)
                for n in range(len(un)):
                    if len(un[n][2]) == 4:
                        dve.wait_ge(at[L, "turned"], n + 1)
                        if n >= 2:
                            dve.wait_ge(at[L, "pv"], n - 1)
                        v.tensor_copy(probT[:, n % 2, 512:1024], ps[:, 5, :]).then_inc(at[L, "turn_dve"], 1)
                    if n >= 1 and un[n - 1][3]:
                        take_out(n - 1)
                    if n + 1 < len(un):
                        normalise(n + 1)
                    if n + 2 < len(un):
                        row_max(n + 2)
                take_out(len(un) - 1)

            def mask_a(n, h, kind):
                if kind == "lat":
                    band = cs("band").rearrange("p (q k) -> p q k", q=2)
                    s0 = ps[:, 2 * (n % 2), P:2 * P]
                    s1 = ps[:, 2 * (n % 2) + 1, 0:P]
                    step(v.tensor_tensor(s0, s0, band[:, 0, :], ALU.add))
                    step(v.tensor_tensor(s1, s1, band[:, 1, :], ALU.add))
                    settle()

            def bias_b(n, h, kind):
                dve.wait_ge(bias_ok, h + 1)
                for qb in range(2):
                    sc = ps[:, 2 * (n % 2) + qb, 0:S].rearrange("p (r c) -> p r c", r=4)
                    b = bias[:, h % 2, (2 - 2 * qb) * GRID_W:(6 - 2 * qb) * GRID_W]
                    forwards = bass.AP(b.tensor, b.offset + GRID_W - 1,
                                       [list(b.ap[0]), [GRID_W, 4], [-1, GRID_W]])
                    ins = v.tensor_tensor(sc, sc, forwards, ALU.add)
                    if qb == 0:
                        step(ins)
                    else:
                        ins.then_inc(bias_used, 1)
                settle()
                dve.wait_ge(bias_used, h + 1)

            def bias_c(n, h, kind):
                slope = 2.0 ** (-8.0 * (h + 1) / NH2)
                dist = cs("dist").rearrange("p (q k) -> p q k", q=2)
                for qb in range(2):
                    sc = ps[:, 2 * (n % 2) + qb, 0:S]
                    step(v.scalar_tensor_tensor(sc, dist[:, qb, :], -slope, sc, ALU.mult, ALU.add))
                settle()

            dve.wait_ge(sink_in, 16)
            attention("a", mask_a)

            def residual(stage, l, parts, base):
                for m in range(KT):
                    dve.wait_ge(st[stage], m + 1)
                    dve.wait_ge(alpha_ok, base + m + 1)
                    for i, (c0, c1) in enumerate(parts):
                        ins = v.scalar_tensor_tensor(H[:, m, c0:c1], ps[:, m % 4, c0:c1], mod[:, l, 16 + m, i:i + 1],
                                                     H[:, m, c0:c1], ALU.mult, ALU.add)
                        if i < len(parts) - 1:
                            step(ins)
                            settle()
                    ins.then_inc(tk[stage, "dve"], 1)

            def layer_norm(N, l, w):
                dve.wait_ge(nm[N, "mean"], 1)
                for j in range(KT):
                    v.tensor_tensor(H[:, j, 0:w], H[:, j, 0:w], ps[:, 4, 0:w], ALU.subtract).then_inc(nm[N, "cent"], 1)
                dve.wait_ge(nm[N, "std"], 1)
                v.reciprocal(rstd[:, 0:w], rstd[:, 0:w]).then_inc(nm[N, "rs"], 1)
                dve.wait_ge(nm[N, "rs"], 1)
                dve.wait_ge(nm[N, "sq"], KT)
                for j in range(KT):
                    step(v.tensor_tensor(H[:, j, 0:w], H[:, j, 0:w], rstd[:, 0:w], ALU.mult))
                    settle()
                    v.tensor_scalar(H[:, j, 0:w], H[:, j, 0:w], vc("ln_g", 8 * l + j), vc("ln_b", 8 * l + j),
                                    ALU.mult, ALU.add).then_inc(nm[N, "out"], 1)
                    if j == KT - 1:
                        dve.wait_ge(nm[N, "out"], KT)

            residual("a_out", 0, ((0, S), (S, T)), 0)
            layer_norm("lna", 0, T)
            take_modulation(1)
            modulate(1)

            jobs = JOBS["b_in"]
            for i, (kind, m, _, _, eng) in enumerate(jobs):
                if eng == "dve":
                    dve.wait_ge(st["b_in"], i + 1)
                    dst = kTb[:, m, :] if kind == "k" else vb[:, m[1], m[0] * 512:(m[0] + 1) * 512]
                    v.tensor_copy(dst, ps[:, i % 4, :]).then_inc(tk["b_in", "dve"], 1)
            attention("b", bias_b)
            residual("b_out", 1, ((0, S),), KT)
            layer_norm("lnb", 1, S)

            def gains(i, name, col):
                step(v.scalar_tensor_tensor(gain[:, i, :], mod2[:, col:col + KT], 1.0,
                                            vec[:, VAT[name]:VAT[name] + KT], ALU.add, ALU.mult))
                settle()

            def rms_norm(N, dst, gain_of, shift_of, sem_out):
                dve.wait_ge(nm[N, "std"], 1)
                v.reciprocal(rstd[:, 0:S], rstd[:, 0:S]).then_inc(nm[N, "rs"], 1)
                dve.wait_ge(nm[N, "rs"], 1)
                for j in range(KT):
                    step(v.tensor_tensor(dst[:, j, 0:S], H[:, j, 0:S], rstd[:, 0:S], ALU.mult))
                    settle()
                    v.tensor_scalar(dst[:, j, 0:S], dst[:, j, 0:S], gain_of(j), shift_of(j), ALU.mult,
                                    ALU.add if shift_of(j) is not None else ALU.bypass).then_inc(sem_out, 1)

            dve.wait_ge(st["mod_a"], 6)
            v.tensor_tensor(mod2[:, 0:24], ps[:, 7, 0:24], vec[:, VAT["b_mod_2"]:VAT["b_mod_2"] + 24],
                            ALU.add).then_inc(mod_ok, 1)
            dve.wait_ge(mod_ok, 3)
            gains(0, "g_norm1_2", 8)
            rms_norm("rms1", h1T, lambda j: gain[:, 0, j:j + 1], lambda j: mod2[:, j:j + 1], nm["rms1", "out"])

            dve.wait_ge(zero_ok, 1)
            for m in range(4):
                dve.wait_ge(st["c_in"], 4 + m + 1)
                dve.wait_ge(tk["c_in", "act"], 4)
                v.tensor_tensor(glu[:, m, CONV_W - 1:], ps[:, m, 0:S], sigb[:, m, :], ALU.mult
                                ).then_inc(tk["c_in", "dve"], 1)
            dve.wait_ge(tk["c_in", "dve"], 4)
            base = steps[0]
            for j in range(4):
                step(v.tensor_scalar(convo[:, j, :], glu[:, j, 0:S], conv_taps[:, j, 0:1], vc("conv_b_2", j),
                                     ALU.mult, ALU.add))
            for k in range(1, CONV_W):
                for j in range(4):
                    dve.wait_ge(dve_step, base + 4 * (k - 1) + j + 1)
                    ins = v.scalar_tensor_tensor(convo[:, j, :], glu[:, j, k:k + S], conv_taps[:, j, k:k + 1],
                                                 convo[:, j, :], ALU.mult, ALU.add)
                    if k < CONV_W - 1:
                        step(ins)
                    else:
                        ins.then_inc(conv_ok, 1)
            attention("c", bias_c)
            dve.wait_ge(nm["lnc", "mean"], 1)
            step(v.tensor_scalar(probT[:, 0, 0:S], ps[:, 4, 0:S], 1.0 / HID, None, ALU.mult))
            settle()
            dve.wait_ge(conv_ok, 4)
            for j in range(4):
                v.tensor_tensor(convo[:, j, :], convo[:, j, :], probT[:, 0, 0:S], ALU.subtract
                                ).then_inc(nm["lnc", "cent"], 1)
            dve.wait_ge(nm["lnc", "std"], 1)
            v.reciprocal(rstd[:, 0:S], rstd[:, 0:S]).then_inc(nm["lnc", "rs"], 1)
            dve.wait_ge(nm["lnc", "rs"], 1)
            for j in range(4):
                v.tensor_tensor(convo[:, j, :], convo[:, j, :], rstd[:, 0:S], ALU.mult).then_inc(acc2_ok, 1)

            for m in range(KT):
                dve.wait_ge(st["c_out"], m + 1)
                v.scalar_tensor_tensor(H[:, m, 0:S], ps[:, m % 4, 0:S], mod2[:, 16 + m:17 + m], H[:, m, 0:S],
                                       ALU.mult, ALU.add).then_inc(tk["c_out", "dve"], 1)
            dve.wait_ge(st["mod_b"], 6)
            v.tensor_tensor(mod2[:, 24:48], ps[:, 7, 0:24], vec[:, VAT["b_mod_2"] + 24:VAT["b_mod_2"] + 48],
                            ALU.add).then_inc(mod_ok, 1)
            dve.wait_ge(mod_ok, 4)
            dve.wait_ge(tk["c_out", "dve"], KT)
            gains(1, "g_norm2_2", 32)
            rms_norm("rms2", h2T, lambda j: gain[:, 1, j:j + 1], lambda j: mod2[:, 24 + j:25 + j], nm["rms2", "out"])

            def rr(i):
                return route[:, i, :].rearrange("p (t e) -> p t e", t=2)

            def r8(i):
                return route[:, i, 0:8].rearrange("p (t g) -> p t g", t=2)

            def r2(i, a=0):
                return route[:, i, a:a + 2]

            def bc(x, n):
                return x.unsqueeze(2).broadcast_to([P, 2, n])

            def do(ins):
                step(ins)
                settle()

            dve.wait_ge(logits, 1)
            dve.wait_ge(rt_in, 64)
            lg = ps[:, 0, 0:128].rearrange("p (t e) -> p t e", t=2)
            do(v.tensor_tensor(r8(0), lg[:, :, 0:NG], rbias[:, 0:NG].unsqueeze(1).broadcast_to([P, 2, NG]), ALU.add))
            do(v.tensor_tensor(rr(3), lg[:, :, NG:NG + NE], rbias[:, NG:NG + NE].unsqueeze(1).broadcast_to([P, 2, NE]),
                               ALU.add))
            do(v.tensor_reduce(r2(4), r8(0), AX.X, ALU.max))
            v.tensor_tensor(r8(1), r8(0), bc(r2(4), NG), ALU.subtract).then_inc(gsub, 1)

            def first_max(onehot, score, x, top, n, desc):
                do(v.tensor_tensor(score, x, bc(top, n), ALU.is_equal))
                do(v.tensor_tensor(score, score, desc.unsqueeze(1).broadcast_to([P, 2, n]), ALU.mult))
                do(v.tensor_reduce(r2(5), score, AX.X, ALU.max))
                do(v.tensor_tensor(onehot, score, bc(r2(5), n), ALU.is_equal))

            first_max(r8(6), r8(7), r8(0), r2(4), NG, cs("desc")[:, NE - NG:NE])
            do(v.tensor_scalar(r8(6), r8(6), BIG, -BIG, ALU.mult, ALU.add))
            for t in range(2):
                e3 = route[:, 3, t * NE:(t + 1) * NE].rearrange("p (g e) -> p g e", g=NG)
                pen = route[:, 6, t * NG:(t + 1) * NG].unsqueeze(2).broadcast_to([P, NG, EPG])
                do(v.tensor_tensor(e3, e3, pen, ALU.add))
            do(v.tensor_reduce(r2(8), rr(3), AX.X, ALU.max))
            first_max(rr(12), rr(9), rr(3), r2(8), NE, cs("desc"))
            do(v.scalar_tensor_tensor(rr(3), rr(12), -3 * BIG, rr(3), ALU.mult, ALU.add))
            do(v.tensor_reduce(r2(10), rr(3), AX.X, ALU.max))
            first_max(rr(13), rr(9), rr(3), r2(10), NE, cs("desc"))
            sel = rr(14)
            v.tensor_tensor(sel, rr(12), rr(13), ALU.add).then_inc(sel_ok, 1)
            v.tensor_tensor(r2(11), r2(10), r2(8), ALU.subtract).then_inc(tdif, 1)
            dve.wait_ge(gexp, 1)
            do(v.tensor_reduce(r2(15), r8(2), AX.X, ALU.add))
            dve.wait_ge(texp, 1)
            do(v.tensor_scalar(r2(15, 2), r2(11, 2), 1.0, None, ALU.add))
            do(v.tensor_tensor(r2(15, 4), r2(15, 0), r2(15, 2), ALU.mult))
            do(v.reciprocal(r2(15, 6), r2(15, 4)))
            do(v.tensor_tensor(r2(15, 8), r2(15, 6), r2(11, 2), ALU.mult))
            do(v.tensor_tensor(rr(12), rr(12), bc(r2(15, 6), NE), ALU.mult))
            do(v.tensor_tensor(rr(13), rr(13), bc(r2(15, 8), NE), ALU.mult))
            do(v.tensor_tensor(wsel[:, :, :], rr(12), rr(13), ALU.add))
            dve.wait_ge(ranks, 1)
            dve.wait_ge(sel_ok, 1)
            rk = ps[:, 5, 0:2 * NE].rearrange("p (t e) -> p t e", t=2)
            do(v.scalar_tensor_tensor(keysel[:, :, :], rk, 1.0, sel, ALU.add, ALU.mult))
            do(v.tensor_scalar(keysel[:, :, :], keysel[:, :, :], -1.0, None, ALU.add))
            do(v.tensor_reduce(peakf[:, :], ps[:, 5, 64:64 + NE], AX.X, ALU.max))
            v.tensor_copy(peak[:, :], peakf[0:1, :]).then_inc(peak_ok, 1)
            for b in range(1, 4, 2):
                dve.wait_ge(h2r_turn, b + 1)
                v.tensor_copy(h2rows[:, b // 2, 512:1024], ps[:, 1 + b, :]).then_inc(h2r_ok, 1)

            def slots(r, do):
                if r:
                    do(v.tensor_scalar(keysel[:, :, :], keysel[:, :, :], -1.0 * CAP, None, ALU.add))
                for t in range(2):
                    ins = v.tensor_tensor(pick[:, t, :].rearrange("p (e s) -> p e s", e=NE),
                                          keysel[:, t, :].unsqueeze(2).broadcast_to([P, NE, CAP]),
                                          cs("slot").unsqueeze(1).broadcast_to([P, NE, CAP]), ALU.is_equal)
                ins.then_inc(pick_ok, 1)
                dve.wait_ge(pick_ok, r + 1)
                for t in range(2):
                    ins = v.tensor_tensor(wpick[:, t, :].rearrange("p (e s) -> p e s", e=NE),
                                          pick[:, t, :].rearrange("p (e s) -> p e s", e=NE),
                                          wsel[:, t, :].unsqueeze(2).broadcast_to([P, NE, CAP]), ALU.mult)
                ins.then_inc(wpick_ok, 1)

            def experts(r, pair):
                n = r * PAIRS + pair
                dve.wait_ge(gath, n * 2 + 2)
                v.tensor_copy(xg[:, 4:8, :], ps[:, 1, :]).then_inc(xg_dve, 1)
                for x in range(2):
                    dve.wait_ge(sg_ok, n * 2 + x + 1)
                    v.tensor_tensor(hidT[:, x].rearrange("p k s -> p (k s)"), ps[:, 2 + x, 256:512], sgl[:, x, :],
                                    ALU.mult).then_inc(hid_ok, 1)
                dve.wait_ge(down, n * 2 + 2)
                v.tensor_copy(yT[:, 4:8, :], ps[:, 5, :]).then_inc(y_dve, 1)
                dve.wait_ge(yturn, n * 2 + 2)
                v.tensor_copy(yrows[:, 512:1024], ps[:, 7, :]).then_inc(yr_dve, 1)
                for b in range(4):
                    dve.wait_ge(scat, n * 4 + b + 1)
                    y = yacc[:, b * 512:(b + 1) * 512]
                    v.tensor_tensor(y, ps[:, b, :], y, ALU.add).then_inc(acc_ok, 1)

            slots(0, do)
            dve.wait_ge(acc_zero, 1)
            with dve.Fori(0, PAIRS) as pair:
                experts(0, pair)
            dve.wait_ge(peak_ok, 1)
            most = dve.value_load(peak[:, :], min_val=0, max_val=S)
            for r in range(1, PASSES):
                with dve.If(most > CAP * r):
                    slots(r, do_over)
                    with dve.Fori(0, PAIRS) as pair:
                        experts(r, pair)
                    dve.wait_ge(acc_ok, 4 * PAIRS * (r + 1))

            dve.wait_ge(acc_ok, 4 * PAIRS)
            for m in range(KT):
                v.scalar_tensor_tensor(H[:, m, 0:S], yacc[:, m * S:(m + 1) * S], mod2[:, 40 + m:41 + m],
                                       H[:, m, 0:S], ALU.mult, ALU.add).then_inc(nm["rmsf", "cent"], 1)
            dve.wait_ge(nm["rmsf", "cent"], KT)
            dve.wait_ge(nm["rmsf", "sq"], KT)
            rms_norm("rmsf", H, lambda j: vc("g_final_2", j), lambda j: None, nm["rmsf", "out"])
            for b in range(1, 4, 2):
                dve.wait_ge(oturn, b + 1)
                v.tensor_copy(outrows[:, b // 2, 512:1024], ps[:, b, :]).then_inc(orow_ok, 1)


_INS = ["x", "c", "ctx", "c_ctx", "w_ada", "b_ada", "ln_g", "ln_b", "a_w_in", "a_w_out", "a_sink", "b_w_in",
        "b_w_out", "b_rel_bias", "c_2", "w_mod_2", "b_mod_2", "g_norm1_2", "w_in_2", "conv_w_2", "conv_b_2",
        "conv_ln_g_2", "conv_ln_b_2", "w_out_2", "g_norm2_2", "w_router_group_2", "b_router_group_2",
        "w_router_expert_2", "b_router_expert_2", "w_exp_gate_2", "w_exp_up_2", "w_exp_down_2", "g_final_2"]


def kernel(**inputs):
    import numpy as _np
    import concourse.bacc as _bacc
    from concourse import mybir as _mybir
    from concourse.bass_utils import run_bass_kernel_spmd as _run

    nc = _bacc.Bacc("TRN2", target_bir_lowering=False, num_devices=1)
    arrays, aps = {}, {}
    for name in _INS:
        a = _np.ascontiguousarray(inputs[name])
        arrays[f"in_{name}"] = a
        aps[name] = nc.dram_tensor(f"in_{name}", a.shape, _mybir.dt.from_np(a.dtype), kind="ExternalInput").ap()
    arrays["in_consts"] = constants()
    consts = nc.dram_tensor("in_consts", arrays["in_consts"].shape, _mybir.dt.float32, kind="ExternalInput").ap()
    relpad = nc.dram_tensor("relpad", (NH * REL_H, PADW), _mybir.dt.float32, kind="Internal").ap()
    out = nc.dram_tensor("out_0", (1, S, D), _mybir.dt.float32, kind="ExternalOutput").ap()
    build(nc, aps, consts, relpad, out)
    r = _run(nc, [arrays], core_ids=[0])
    return r.results[0]["out_0"]
```

```python
from contextlib import ExitStack

import numpy as np
import concourse.bass as bass
from concourse import mybir

F32 = mybir.dt.float32
I32 = mybir.dt.int32
ACT = mybir.ActivationFunctionType
ALU = mybir.AluOpType
AX = mybir.AxisListType

P = 128
D = 1024
KT = D // P
S = 256
C = 256
T = S + C
NH = 16
HD = 64
KVH = 4
GRID_W = 64
KW = 16
REL_W, REL_H = 2 * KW - 1, 15
PADW = 2 * GRID_W - 1
BROWS = 6
NH2 = 8
CONV_W = 31
NG, EPG = 4, 8
NE = NG * EPG
HID = 512
CAP = 64
PAIRS = NE // 2
PASSES = -(-S // CAP)
COLS = 512
SLOTS = 6
ALPHA = 4.0 ** 0.25
BIG = 1e30


def const_layout():
    at, n = {}, 0
    for name, w in (("ident", P), ("mean", P), ("ones", P), ("rot", P), ("before", P), ("band", 2 * P), ("dist", 2 * S), ("mult", 2 * S), ("col", GRID_W), ("slot", CAP),
                    ("desc", NE), ("fold", 3), ("eps", 2), ("cos", S), ("sin", S)):
        at[name] = (n, n + w)
        n += w
    return at, n


def constants():
    at, n = const_layout()
    out = np.zeros((P, n), np.float32)

    def put(name, a):
        out[:, at[name][0]:at[name][1]] = np.asarray(a, np.float32).reshape(a.shape[0], -1)

    p, q = np.arange(P)[:, None], np.arange(P)[None, :]
    put("ident", (p == q) * 1.0)
    put("mean", np.full((P, P), 1.0 / D))
    put("ones", np.ones((P, P)))
    rot = np.zeros((P, P), np.float32)
    for m in range(P):
        if m % 32 < 16:
            rot[m + 16, m] = -1.0
        else:
            rot[m - 16, m] = 1.0
    put("rot", rot)
    put("before", (p < q) * 1.0)
    t = np.arange(S)
    inv = np.float32(10000.0) ** (-np.arange(16, dtype=np.float32) / np.float32(16))
    sub = np.arange(P) % HD
    pos = np.where((sub < 32)[:, None], (t // GRID_W)[None, :], (t % GRID_W)[None, :]).astype(np.float32)
    ang = (pos * inv[sub % 16][:, None]).astype(np.float32)
    put("cos", np.cos(ang))
    put("sin", np.sin(ang))
    put("band", np.concatenate([np.where(q > p, -BIG, 0.0), np.where(p > q, -BIG, 0.0)], axis=1))
    d = (np.arange(2)[None, :, None] * P + np.arange(P)[:, None, None]) - np.arange(S)[None, None, :]
    mult = np.where(d >= 0, (d <= 128) * 1.0 + (d % 4 == 0) + (d % 16 == 0), 0.0)
    put("dist", np.where(mult > 0, d, BIG))
    put("mult", mult)
    qc, kc = np.arange(P)[:, None] % GRID_W, np.arange(GRID_W)[None, :]
    first = np.clip(qc - KW // 2, 0, GRID_W - KW)
    put("col", np.where((kc >= first) & (kc < first + KW), 0.0, -BIG)[:, ::-1])
    put("slot", np.tile(np.arange(CAP), (P, 1)))
    put("desc", np.tile(NE - np.arange(NE), (P, 1)))
    put("fold", np.arange(P)[:, None] % 32 == np.arange(3)[None, :])
    put("eps", np.tile(np.array([1e-5, 1e-6]), (P, 1)))
    return out


VEC = [("c", 8), ("c_ctx", 8), ("c_2", 8), ("b_ada", 48), ("ln_g", 16), ("ln_b", 16), ("g_norm1_2", 8),
       ("g_norm2_2", 8), ("g_final_2", 8), ("b_mod_2", 48), ("conv_b_2", 4), ("conv_ln_g_2", 4), ("conv_ln_b_2", 4)]
VAT = {}
for _name, _n in VEC:
    VAT[_name] = sum(VAT_n for _, VAT_n in VEC[:[v[0] for v in VEC].index(_name)])
NVEC = sum(n for _, n in VEC)
VROWS1 = NVEC - P


def chunk_plan():
    plan = [("ada0", "w_ada", 0, c) for c in range(6)]
    plan += [("a_in", "a_w_in", 0, c) for c in range(5)]
    plan += [("a_out", "a_w_out", 0, c) for c in range(2)]
    plan += [("ada1", "w_ada", 1, c) for c in range(6)]
    plan += [("b_in", "b_w_in", 0, c) for c in range(8)]
    plan += [("b_out", "b_w_out", 0, c) for c in range(2)]
    plan += [("mod_a", "w_mod_2", 0, c) for c in range(6)]
    plan += [("c_in", "w_in_2", 0, c) for c in (4, 3, 0, 1, 2)]
    plan += [("mod_b", "w_mod_2", 0, c) for c in range(6, 12)]
    plan += [("c_out", "w_out_2", 0, c) for c in range(2)]
    return plan


PLAN = chunk_plan()
ROUNDS = len(PLAN) // SLOTS
STAGE_AT = {}
for _i, _c in enumerate(PLAN):
    STAGE_AT.setdefault(_c[0], _i)


def in_jobs(stage):
    if stage == "a_in":
        jobs = [("q", m, m // 4, (m % 4) * P, "act") for m in range(8)]
        jobs += [("k", m, 2, m * P, "act") for m in range(2)]
        jobs += [("v", t, 2, 2 * P, "dve") for t in range(4)]
        jobs += [("g", m, 3 + m // 4, (m % 4) * P, "act") for m in range(8)]
    elif stage == "b_in":
        jobs = [("q", m, m // 4, (m % 4) * P, "act") for m in range(8)]
        jobs += [("k", m, 2 + m // 4, (m % 4) * P, "dve" if m % 2 else "act") for m in range(8)]
        jobs += [("v", (h, t), 4 + h, 0, "dve" if t % 2 else "act") for h in range(2) for t in range(4)]
        jobs += [("g", m, 6 + m // 4, (m % 4) * P, "act") for m in range(8)]
    else:
        jobs = [("b", m, 0, m * P, "act") for m in range(4)]
        jobs += [("a", m, 1, m * P, "dve") for m in range(4)]
        jobs += [("q", m, 2, m * P, "act") for m in range(4)]
        jobs += [("k", m, 3, m * P, "act") for m in range(4)]
        jobs += [("v", t, 4, 0, "act") for t in range(2)]
    return jobs


def taken_by(jobs, i):
    eng = jobs[i][4]
    return eng, sum(1 for j in jobs[:i + 1] if j[4] == eng)


def units(layer):
    if layer == "a":
        return [(2 * p + x, kind, kts, x == 1) for p in range(NH // 2)
                for kind, kts in (("lat", (0, 1, 2, 3)), ("ctx", (2, 3))) for x in range(2)]
    if layer == "b":
        return [(h, "lat", (0, 1, 2, 3), h % 2 == 1) for h in range(NH)]
    return [(h, "lat", (0, 1), h % 2 == 1) for h in range(NH2)]


def build(nc, IN, consts_dram, relpad, out):
    CA, CN = const_layout()
    with ExitStack() as ctx:
        def sb(name, shape, dt=F32):
            return ctx.enter_context(nc.sbuf_tensor(name, shape, dt))

        def sem(name):
            return ctx.enter_context(nc.semaphore(name))

        ring = sb("ring", [P, SLOTS, KT * COLS])
        CR = CN - 2 * S
        cst = sb("cst", [P, CR])
        H = sb("H", [P, KT, T])
        U = sb("U", [P, KT * T])
        Q = sb("Q", [P, KT * T])
        G = sb("G", [P, KT * T])
        K = sb("K", [P, KT * T])
        prob = sb("prob", [P, 2, 2 * T])
        probT = sb("probT", [P, 2, 2 * T])
        bias = sb("bias", [P, 2, BROWS * GRID_W])
        vec = sb("vec", [P, NVEC])
        conv_taps = sb("conv_taps", [P, 4, CONV_W])
        sil = sb("sil", [P, KT, 32])
        mod = sb("mod", [P, 2, 24, 2])
        mod2 = sb("mod2", [P, 48])
        gain = sb("gain", [P, 2, KT])
        sink = sb("sink", [P, NH])
        soft = sb("soft", [P, 2, 5, 2])
        peak = sb("peak", [1, 1], I32)
        peakf = sb("peakf", [P, 1])
        ps = ctx.enter_context(nc.psum_tensor("ps", [P, 8, 512], F32))

        def cs(name):
            return cst[:, CA[name][0]:CA[name][1]]

        cos, sin = bias[:, 0, 0:S], bias[:, 1, 0:S]

        def vc(name, j=0):
            return vec[:, VAT[name] + j:VAT[name] + j + 1]

        ident, ones, meanm, rotm, before = cs("ident"), cs("ones"), cs("mean"), cs("rot"), cs("before")
        eps_ln, eps_rms = cs("eps")[:, 0:1], cs("eps")[:, 1:2]

        xrows = Q[:, :].rearrange("p (t f) -> p t f", t=4)
        vrows = K[:, 0:2 * P].rearrange("p (t f) -> p t f", t=2)
        crows = K[0:CONV_W, 512:512 + HID]
        uT = U[:, :].rearrange("p (j t) -> p j t", j=KT)
        oT = uT
        qT = Q[:, :].rearrange("p (j t) -> p j t", j=KT)
        gT = G[:, :].rearrange("p (j t) -> p j t", j=KT)
        kTa = K[:, 0:1024].rearrange("p (j t) -> p j t", j=2)
        kSa = K[:, 1024:2048].rearrange("p (j t) -> p j t", j=2)
        va = K[:, 2048:3072].rearrange("p (t f) -> p t f", t=4)
        qTb = Q[:, 0:2048].rearrange("p (j t) -> p j t", j=KT)
        gTb = Q[:, 2048:4096].rearrange("p (j t) -> p j t", j=KT)
        kTb = K[:, :].rearrange("p (j t) -> p j t", j=KT)
        vb = G[:, :].rearrange("p (t f) -> p t f", t=4)
        sq = Q[:, :].rearrange("p (j t) -> p j t", j=KT)
        rstd = prob[:, 0, 0:512]
        mixT = U[:, 0:2048].rearrange("p (j t) -> p j t", j=KT)
        h1T = U[:, 2048:4096].rearrange("p (j t) -> p j t", j=KT)
        qTc = K[:, 0:1024].rearrange("p (j t) -> p j t", j=4)
        kTc = K[:, 1024:2048].rearrange("p (j t) -> p j t", j=4)
        vcr = K[:, 2048:3072].rearrange("p (t f) -> p t f", t=2)
        sigb = K[:, 3072:4096].rearrange("p (j t) -> p j t", j=4)
        GLU_W = CONV_W - 1 + S
        glu = G[:, 0:4 * GLU_W].rearrange("p (j t) -> p j t", j=4)
        convo = G[:, 2048:3072].rearrange("p (j t) -> p j t", j=4)
        csq = G[:, 3072:4096].rearrange("p (j t) -> p j t", j=4)
        sq2 = Q[:, 0:2048].rearrange("p (j t) -> p j t", j=KT)
        h2T = Q[:, 2048:4096].rearrange("p (j t) -> p j t", j=KT)
        yacc = U[:, 0:2048]
        h2rows = U[:, 2048:4096].rearrange("p (t f) -> p t f", t=2)
        pick = Q[:, :].rearrange("p (t s) -> p t s", t=2)
        wpick = G[:, :].rearrange("p (t s) -> p t s", t=2)
        wpickT = K[:, :]
        xg = prob[:, 0, :].rearrange("p (j s) -> p j s", j=KT)
        yrows = probT[:, 0, :]
        hidT = prob[:, 1, 0:512].rearrange("p (k s) -> p k s", k=4)
        sgl, hid = probT[:, 1, 0:512], probT[:, 1, 512:1024]
        modrow = prob[:, 1, :].rearrange("p (b n) -> p b n", b=2)
        route = K[:, 0:1024].rearrange("p (r n) -> p r n", n=2 * 32)
        outrows = Q[:, 0:2048].rearrange("p (t f) -> p t f", t=2)
        wr = probT[:, 1, 0:KT * 36].rearrange("p (j n) -> p j n", j=KT)
        rbias = probT[:, 1, 512:548]
        keysel = sb("keysel", [P, 2, NE])
        wsel = sb("wsel", [P, 2, NE])

        table_in = sem("table_in")
        cst_in, vec_in, x_in, sink_in = sem("cst_in"), sem("vec_in"), sem("x_in"), sem("sink_in")
        rel_in, rel_out, rel_zero = sem("rel_in"), sem("rel_out"), sem("rel_zero")
        full = [sem(f"full{i}") for i in range(SLOTS)]
        pe_vec, vec_ok = sem("pe_vec"), sem("vec_ok")
        pe_x, x_ok = sem("pe_x"), sem("x_ok")
        sil_ok = sem("sil_ok")
        st = {n: sem(n + "_done") for n in ("ada0", "a_in", "a_out", "ada1", "b_in", "b_out", "mod_a", "c_in",
                                            "c_out", "mod_b")}
        tk = {(n, e): sem(f"{n}_taken_{e}") for n in ("a_in", "b_in", "c_in") for e in ("act", "dve")}
        tk.update({(n, "dve"): sem(f"{n}_taken_dve") for n in ("a_out", "b_out", "c_out")})
        mod_ok, u_ok, alpha_ok = sem("mod_ok"), sem("u_ok"), sem("alpha_ok")
        rot_done, rope_ok, swap_ok = sem("rot_done"), sem("rope_ok"), sem("swap_ok")
        dve_step, over_step = sem("dve_step"), sem("over_step")
        at = {}
        for L in "abc":
            for n in ("scores", "max", "exp", "prob", "turned", "turn_act", "turn_dve", "pv", "o"):
                if L != "c" or n != "turn_dve":
                    at[L, n] = sem(f"{L}_{n}")
        bias_in, bias_ok, bias_used = [sem("bias_in0"), sem("bias_in1")], sem("bias_ok"), sem("bias_used")
        nm = {}
        for N in ("lna", "lnb", "rms1", "lnc", "rms2", "rmsf"):
            for n in ("mean", "cent", "sq", "var", "std", "out"):
                if N[:2] == "ln" or n != "mean" and (n != "cent" or N == "rmsf"):
                    nm[N, n] = sem(f"{N}_{n}")
        glu_ok, conv_ok, zero_ok = sem("glu_ok"), sem("conv_ok"), sem("zero_ok")
        rt_in, logits, h2r_turn, h2r_ok = sem("rt_in"), sem("logits"), sem("h2r_turn"), sem("h2r_ok")
        gsub, gexp, tdif, texp, sel_ok, ranks = (sem(n) for n in ("gsub", "gexp", "tdif", "texp", "sel_ok", "ranks"))
        peak_ok, pick_ok, wpick_ok = sem("peak_ok"), sem("pick_ok"), sem("wpick_ok")
        wturn, wturn_ok = sem("wturn"), sem("wturn_ok")
        gath, xg_act, xg_dve = sem("gath"), sem("xg_act"), sem("xg_dve")
        gate_done, up_done, down_done = sem("gate_done"), sem("up_done"), sem("down_done")
        sg_ok, hid_ok, hid_turn, hidT_ok = sem("sg_ok"), sem("hid_ok"), sem("hid_turn"), sem("hidT_ok")
        yr_act, yr_dve = sem("yr_act"), sem("yr_dve")
        row_ok = {n: sem(n + "_rows") for n in ("ada0", "ada1", "mod_a", "mod_b")}
        col_done = {n: sem(n + "_cols") for n in ("ada0", "ada1", "mod_a", "mod_b")}
        sil_zero = sem("sil_zero")
        scat, acc_ok, acc_zero = sem("scat"), sem("acc_ok"), sem("acc_zero")
        oturn, orow_ok, out_done = sem("oturn"), sem("orow_ok"), sem("out_done")
        acc2_ok = sem("acc2_ok")

        UN = {L: units(L) for L in "abc"}
        JOBS = {s: in_jobs(s) for s in ("a_in", "b_in", "c_in")}
        used = {}
        for s in JOBS:
            used[s] = [sum(1 for j in JOBS[s] if j[2] <= c) for c in range(1 + max(j[2] for j in JOBS[s]))]
        for s in ("a_out", "b_out", "c_out"):
            used[s] = [4, 8]
        for s in ("ada0", "ada1", "mod_a", "mod_b"):
            used[s] = [c + 1 for c in range(6)]

        def slot(n):
            return ring[:, n % SLOTS, :].rearrange("p (k n) -> p k n", k=KT)

        def turned_by_dve(L, n):
            return sum(1 for u in UN[L][:n] if len(u[2]) == 4)

        def dslot(n):
            return ring[:, n, :].rearrange("p (k n) -> p k n", k=4)

        block = ctx.enter_context(nc.Block())

        @block.sync
        def _(sp):
            sp.dma_start(cst[:, :], consts_dram[:, 0:CR]).then_inc(cst_in, 16)
            sp.dma_start(bias[:, :, 0:S], consts_dram[:, CR:CN].rearrange("p (a t) -> p a t", a=2)
                         ).then_inc(table_in, 16)
            sp.dma_start(xrows[:, 0:2, :], IN["x"][0].rearrange("(t p) f -> p t f", p=P)).then_inc(x_in, 16)
            sp.dma_start(xrows[:, 2:4, :], IN["ctx"][0].rearrange("(t p) f -> p t f", p=P)).then_inc(x_in, 16)
            for n, (stage, src, l, c) in enumerate(PLAN):
                if n >= SLOTS:
                    was = PLAN[n - SLOTS][0]
                    sp.wait_ge(st[was], used[was][n - SLOTS - STAGE_AT[was]])
                w = IN[src][l, :, c * COLS:(c + 1) * COLS].rearrange("(k p) n -> p k n", p=P)
                sp.dma_start(slot(n), w).then_inc(full[n % SLOTS], 16)

            wg, wu, wd = (IN[f"w_exp_{n}_2"][0] for n in ("gate", "up", "down"))

            def load_pair(e, free):
                for i, w in enumerate((wg, wu, wd)):
                    for x in range(2):
                        s = 2 * i + x
                        view = dslot(s) if i == 2 else slot(s)
                        free(s, i)
                        sp.dma_start(view, w[bass.ds(e + x, 1)].rearrange("e (k p) n -> p (e k) n", p=P)
                                     ).then_inc(full[s], 16)

            def after_plan(s, i):
                stage = PLAN[len(PLAN) - SLOTS + s][0]
                sp.wait_ge(st[stage], used[stage][len(PLAN) - SLOTS + s - STAGE_AT[stage]])

            load_pair(0, after_plan)

            def stream(r, pair):
                n = r * PAIRS + pair
                load_pair(pair * 2, lambda s, i: sp.wait_ge((gate_done, up_done, down_done)[i], n))

            with sp.Fori(1, PAIRS) as pair:
                stream(0, pair)
            sp.wait_ge(peak_ok, 1)
            most = sp.value_load(peak[:, :], min_val=0, max_val=S)
            for r in range(1, PASSES):
                with sp.If(most > CAP * r):
                    with sp.Fori(0, PAIRS) as pair:
                        stream(r, pair)
            sp.wait_ge(orow_ok, 4)
            sp.dma_start(out[0].rearrange("(t p) f -> p t f", p=P), outrows).then_inc(out_done, 16)
            sp.wait_ge(out_done, 16)

        @block.gpsimd
        def _(pool):
            pool.wait_ge(cst_in, 16)
            padr = probT[0:120, 0, 0:2 * PADW].rearrange("p (a w) -> p a w", a=2)
            pool.memset(padr, 0.0).then_inc(rel_zero, 1)
            pool.wait_ge(rel_zero, 1)
            relr = probT[0:120, 1, 0:2 * REL_W].rearrange("p (a w) -> p a w", a=2)
            pool.dma_start(relr, IN["b_rel_bias"][0].rearrange("h d w -> (h d) w").rearrange("(a p) w -> p a w", a=2)
                           ).then_inc(rel_in, 16)
            pool.wait_ge(rel_in, 16)
            backwards = bass.AP(relr.tensor, relr.offset + REL_W - 1,
                                [list(relr.ap[0]), [REL_W, 2], [-1, REL_W]])
            pool.tensor_copy(padr[:, :, GRID_W - KW:GRID_W - KW + REL_W], backwards).then_inc(rel_zero, 1)
            pool.wait_ge(rel_zero, 2)
            pool.dma_start(relpad.rearrange("(a p) w -> p a w", a=2), padr).then_inc(rel_out, 16)
            pool.wait_ge(rel_out, 16)
            pool.wait_ge(rope_ok, 10)
            for h in range(NH):
                if h >= 2:
                    pool.wait_ge(bias_used, h - 1)
                for half in range(2):
                    first = (h * REL_H + BROWS - 1 - half) * PADW
                    src = bass.AP(relpad.tensor, first, [[1, GRID_W], [PADW, BROWS], [1, GRID_W]])
                    pool.dma_start(bias[half * 64:half * 64 + 64, h % 2].rearrange("p (r c) -> p r c", r=BROWS),
                                   src).then_inc(bias_in[h % 2], 16)
                pool.wait_ge(bias_in[h % 2], 32 * (h // 2 + 1))
                tile = bias[:, h % 2].rearrange("p (r c) -> p r c", r=BROWS)
                pool.tensor_tensor(tile, tile, cs("col").unsqueeze(1).broadcast_to([P, BROWS, GRID_W]),
                                   ALU.add).then_inc(bias_ok, 1)
            pool.wait_ge(at["b", "pv"], NH)
            pool.memset(glu[:, :, 0:CONV_W - 1], 0.0).then_inc(zero_ok, 1)
            pool.wait_ge(tk["c_out", "dve"], KT)
            pool.memset(yacc, 0.0).then_inc(acc_zero, 1)

        @block.tensor
        def _(pe):
            mm, tr = nc.tensor.matmul, nc.tensor.transpose

            def landed(n):
                pe.wait_ge(full[n % SLOTS], 16 * (n // SLOTS + 1))

            pe.wait_ge(cst_in, 16)
            pe.wait_ge(vec_in, 16 * (len(VEC) + 1))
            tr(ps[:, 0, 0:P], vrows[:, 0, :], ident)
            tr(ps[:, 0, P:P + VROWS1], vrows[0:VROWS1, 1, :], ident[0:VROWS1, 0:VROWS1])
            for c in range(4):
                last = tr(ps[:, 0, 256 + 32 * c:256 + 32 * c + CONV_W], crows[:, c * P:(c + 1) * P],
                          ident[0:CONV_W, 0:CONV_W])
            last.then_inc(pe_vec, 1)
            pe.wait_ge(x_in, 32)
            for j in range(KT):
                if j >= 4:
                    pe.wait_ge(x_ok, j - 3)
                for t in range(4):
                    last = tr(ps[:, 1 + j % 4, t * P:(t + 1) * P], xrows[:, t, j * P:(j + 1) * P], ident)
                last.then_inc(pe_x, 1)

            def modulation(stage, chunks, v0, nv, banks):
                def fold(c):
                    pe.wait_ge(row_ok[stage], c + 1)
                    for m in range(4):
                        col = (4 * c + m) * nv
                        last = mm(ps[:, 7, col:col + nv], modrow[:, c % 2, m * P:(m + 1) * P],
                                  cs("fold")[:, v0:v0 + nv], start=True, stop=True)
                    last.then_inc(col_done[stage], 1)

                for c in chunks:
                    n = STAGE_AT[stage] + c
                    landed(n)
                    for i in range(2):
                        for t in range(4):
                            k = 2 * t + i
                            last = mm(ps[32 * t:32 * t + 32, banks[c % 2], :], sil[:, k, :], slot(n)[:, k, :],
                                      start=(i == 0), stop=(i == 1))
                    last.then_inc(st[stage], 1)
                    if c != chunks[0]:
                        fold(c - 1)
                fold(chunks[-1])

            pe.wait_ge(sil_ok, 1)
            modulation("ada0", range(6), 0, 2, (5, 6))

            def in_proj(stage, src, widths, after=None):
                jobs = JOBS[stage]
                seen = -1
                for i, (kind, m, c, col, _) in enumerate(jobs):
                    n = STAGE_AT[stage] + c
                    if c != seen:
                        landed(n)
                        seen = c
                    if i >= 4:
                        e, cnt = taken_by(jobs, i - 4)
                        pe.wait_ge(tk[stage, e], cnt)
                    b = i % 4
                    for k in range(KT):
                        if i == 0:
                            pe.wait_ge(*src_ready(stage, k))
                        w = slot(n)[:, k, :]
                        if kind == "v":
                            t = m[1] if stage == "b_in" else m
                            wid = 256 if stage == "a_in" else 512
                            last = mm(ps[:, b, 0:wid], src[:, k, t * P:(t + 1) * P], w[:, col:col + wid],
                                      start=(k == 0), stop=(k == KT - 1))
                        else:
                            wid = widths[kind]
                            last = mm(ps[:, b, 0:wid], w[:, col:col + P], src[:, k, 0:wid],
                                      start=(k == 0), stop=(k == KT - 1))
                    last.then_inc(st[stage], 1)
                    if after:
                        after(i)

            def src_ready(stage, k):
                if stage == "a_in":
                    return u_ok, k + 1
                if stage == "b_in":
                    return u_ok, KT + k + 1
                return nm["rms1", "out"], k + 1

            def rotate(i):
                if 1 <= i <= 10:
                    r = i - 1
                    pe.wait_ge(tk["a_in", "act"], r + 1)
                    if r >= 2:
                        pe.wait_ge(rope_ok, r - 1)
                    src = qT[:, r, 0:S] if r < 8 else kTa[:, r - 8, 0:S]
                    mm(ps[:, 4 + r % 2, 0:S], rotm, src, start=True, stop=True).then_inc(rot_done, 1)

            in_proj("a_in", uT, {"q": T, "k": T, "g": T}, rotate)

            def attention(L, q_of, k_of, v_of):
                un = UN[L]

                def scores(n):
                    h, kind, kts, _ = un[n]
                    for qb in range(2):
                        last = mm(ps[:, 2 * (n % 2) + qb, 0:len(kts) * P], q_of(h, kind, qb), k_of(h, kts),
                                  start=True, stop=True)
                    last.then_inc(at[L, "scores"], 1)

                scores(0)
                scores(1)
                for n, (h, kind, kts, closes) in enumerate(un):
                    pe.wait_ge(at[L, "prob"], n + 1)
                    for i in range(len(kts)):
                        for qb in range(2):
                            last = tr(ps[:, 4 + i // 2, (i % 2) * S + qb * P:(i % 2) * S + (qb + 1) * P],
                                      prob[:, n % 2, qb * T + i * P:qb * T + (i + 1) * P], ident)
                    last.then_inc(at[L, "turned"], 1)
                    if n + 2 < len(un):
                        scores(n + 2)
                    pe.wait_ge(at[L, "turn_act"], n + 1)
                    if len(kts) == 4:
                        pe.wait_ge(at[L, "turn_dve"], turned_by_dve(L, n + 1))
                    g = n // 2
                    if n % 2 == 0 and g >= 2:
                        pe.wait_ge(at[L, "o"], g - 1)
                    r0 = (h % 2) * HD
                    for i, kt in enumerate(kts):
                        last = mm(ps[r0:r0 + HD, 6 + g % 2, 0:S], v_of(h, kt),
                                  probT[:, n % 2, i * S:(i + 1) * S], start=(i == 0), stop=(i == len(kts) - 1))
                    last.then_inc(at[L, "pv"], 1)

            def half(h):
                return slice((h % 2) * HD, (h % 2) * HD + HD)

            def q_a(h, kind, qb):
                c0 = (0 if kind == "lat" else S) + qb * P
                return qT[half(h), h // 2, c0:c0 + P]

            def k_a(h, kts):
                kv = h // (NH // KVH)
                src = kTa if kv % 2 == h % 2 else kSa
                return src[half(h), kv // 2, kts[0] * P:(kts[-1] + 1) * P]

            def v_a(h, kt):
                kv = h // (NH // KVH)
                return va[:, kt, kv * HD:(kv + 1) * HD]

            pe.wait_ge(rope_ok, 10)
            pe.wait_ge(swap_ok, 2)
            pe.wait_ge(tk["a_in", "dve"], 4)
            pe.wait_ge(tk["a_in", "act"], 18)
            attention("a", q_a, k_a, v_a)

            def out_proj(stage, src, width):
                for m in range(KT):
                    n = STAGE_AT[stage] + m // 4
                    if m % 4 == 0:
                        landed(n)
                    if m >= 4:
                        pe.wait_ge(tk[stage, "dve"], m - 3)
                    for k in range(KT):
                        last = mm(ps[:, m % 4, 0:width], slot(n)[:, k, (m % 4) * P:(m % 4 + 1) * P], src[:, k, 0:width],
                                  start=(k == 0), stop=(k == KT - 1))
                    last.then_inc(st[stage], 1)

            def feature_sum(bank, mat, src, n, width, ready, done):
                for j in range(n):
                    pe.wait_ge(ready, j + 1)
                    last = mm(ps[:, bank, 0:width], mat, src[:, j, 0:width], start=(j == 0), stop=(j == n - 1))
                last.then_inc(done, 1)

            pe.wait_ge(at["a", "o"], NH)
            out_proj("a_out", oT, T)
            feature_sum(4, meanm, H, KT, T, tk["a_out", "dve"], nm["lna", "mean"])
            modulation("ada1", range(3), 0, 2, (3, 6))
            feature_sum(5, meanm, sq, KT, T, nm["lna", "sq"], nm["lna", "var"])
            modulation("ada1", range(3, 6), 0, 2, (3, 6))

            in_proj("b_in", uT, {"q": S, "k": T, "g": S})
            pe.wait_ge(tk["b_in", "dve"], sum(j[4] == "dve" for j in JOBS["b_in"]))
            pe.wait_ge(tk["b_in", "act"], sum(j[4] == "act" for j in JOBS["b_in"]))
            attention("b", lambda h, kind, qb: qTb[half(h), h // 2, qb * P:(qb + 1) * P],
                      lambda h, kts: kTb[half(h), h // 2, :],
                      lambda h, kt: vb[:, kt, h * HD:(h + 1) * HD])
            pe.wait_ge(at["b", "o"], NH // 2)
            out_proj("b_out", oT, S)
            feature_sum(4, meanm, H, KT, S, tk["b_out", "dve"], nm["lnb", "mean"])
            modulation("mod_a", range(3), 2, 1, (3, 6))
            feature_sum(5, meanm, sq, KT, S, nm["lnb", "sq"], nm["lnb", "var"])
            modulation("mod_a", range(3, 6), 2, 1, (3, 6))
            feature_sum(4, meanm, sq2, KT, S, nm["rms1", "sq"], nm["rms1", "var"])

            in_proj("c_in", h1T, {"a": S, "b": S, "q": S, "k": S})
            pe.wait_ge(tk["c_in", "act"], sum(j[4] == "act" for j in JOBS["c_in"]))
            pe.wait_ge(tk["c_in", "dve"], 4)
            modulation("mod_b", range(6), 2, 1, (5, 6))
            pe.wait_ge(mod_ok, 4)
            attention("c", lambda h, kind, qb: qTc[half(h), h // 2, qb * P:(qb + 1) * P],
                      lambda h, kts: kTc[half(h), h // 2, :],
                      lambda h, kt: vcr[:, kt, h * HD:(h + 1) * HD])
            feature_sum(4, ones, convo, 4, S, conv_ok, nm["lnc", "mean"])
            feature_sum(5, ones, csq, 4, S, nm["lnc", "sq"], nm["lnc", "var"])
            pe.wait_ge(at["c", "o"], NH2 // 2)
            pe.wait_ge(nm["lnc", "out"], 4)
            out_proj("c_out", mixT, S)
            feature_sum(4, meanm, sq2, KT, S, nm["rms2", "sq"], nm["rms2", "var"])
            pe.wait_ge(rt_in, 64)
            pe.wait_ge(nm["rms2", "out"], KT)
            for t in range(2):
                for k in range(KT):
                    last = mm(ps[:, 0, t * 64:t * 64 + 36], h2T[:, k, t * P:(t + 1) * P], wr[:, k, :],
                              start=(k == 0), stop=(k == KT - 1))
            last.then_inc(logits, 1)
            for b in range(4):
                t, f0 = b // 2, (b % 2) * 4
                for f in range(4):
                    last = tr(ps[:, 1 + b, f * P:(f + 1) * P], h2T[:, f0 + f, t * P:(t + 1) * P], ident)
                last.then_inc(h2r_turn, 1)
            sel = route[:, 14, :].rearrange("p (t e) -> p t e", t=2)
            pe.wait_ge(sel_ok, 1)
            mm(ps[:, 5, 0:NE], before, sel[:, 0, :], start=True, stop=True)
            mm(ps[:, 5, NE:2 * NE], ones, sel[:, 0, :], start=True, stop=False)
            mm(ps[:, 5, NE:2 * NE], before, sel[:, 1, :], start=False, stop=True)
            mm(ps[:, 5, 64:64 + NE], ones, sel[:, 0, :], start=True, stop=False)
            mm(ps[:, 5, 64:64 + NE], ones, sel[:, 1, :], start=False, stop=True).then_inc(ranks, 1)

            def turn_weights(r):
                pe.wait_ge(wpick_ok, r + 1)
                for i in range(PAIRS // 2):
                    if i >= 4:
                        pe.wait_ge(wturn_ok, r * PAIRS // 2 + i - 3)
                    for x in range(2):
                        for t in range(2):
                            last = tr(ps[:, 4 + i % 4, (2 * x + t) * P:(2 * x + t + 1) * P],
                                      wpick[:, t, (2 * i + x) * P:(2 * i + x + 1) * P], ident)
                    last.then_inc(wturn, 1)
                pe.wait_ge(wturn_ok, (r + 1) * PAIRS // 2)

            def gather(pair):
                for j in range(KT):
                    for t in range(2):
                        last = mm(ps[:, j // 4, (j % 4) * P:(j % 4 + 1) * P], h2rows[:, t, j * P:(j + 1) * P],
                                  pick[:, t, bass.ds(pair * P, P)], start=(t == 0), stop=(t == 1))
                    if j % 4 == 3:
                        last.then_inc(gath, 1)

            def scatter(pair):
                for m in range(KT):
                    last = mm(ps[:, (7, 2, 3, 0)[m // 2], (m % 2) * S:(m % 2 + 1) * S], yrows[:, m * P:(m + 1) * P],
                              wpickT[:, bass.ds(pair * S, S)], start=True, stop=True)
                    if m % 2 == 1:
                        last.then_inc(scat, 1)

            def experts(r, pair, first=False, final=False):
                n = r * PAIRS + pair
                pe.wait_ge(xg_act, n + 1)
                pe.wait_ge(xg_dve, n + 1)
                if not first:
                    pe.wait_ge(acc_ok, (n - 1) * 4)
                for i, done in enumerate((gate_done, up_done)):
                    for x in range(2):
                        pe.wait_ge(full[2 * i + x], (n + ROUNDS + 1) * 16)
                    for k in range(KT):
                        for x in range(2):
                            last = mm(ps[x * CAP:(x + 1) * CAP, 2 + i, :], xg[:, k, x * CAP:(x + 1) * CAP],
                                      slot(2 * i + x)[:, k, :], start=(k == 0), stop=(k == KT - 1))
                    last.then_inc(done, 1)
                if not final:
                    gather(pair + 1)
                pe.wait_ge(hid_ok, n + 1)
                for k in range(4):
                    last = tr(ps[:, 4, k * P:(k + 1) * P], hid[:, k * P:(k + 1) * P], ident)
                last.then_inc(hid_turn, 1)
                if not first:
                    if not final:
                        pe.wait_ge(xg_act, n + 2)
                    pe.wait_ge(yr_act, n)
                    pe.wait_ge(yr_dve, n)
                    scatter(pair - 1)
                for x in range(2):
                    pe.wait_ge(full[4 + x], (n + ROUNDS + 1) * 16)
                pe.wait_ge(hidT_ok, n + 1)
                for k in range(4):
                    for c in range(2):
                        for x in range(2):
                            last = mm(ps[x * CAP:(x + 1) * CAP, 5 + c, :], hidT[:, k, x * CAP:(x + 1) * CAP],
                                      dslot(4 + x)[:, k, c * 512:(c + 1) * 512], start=(k == 0), stop=(k == 3))
                last.then_inc(down_done, 1)
                if final:
                    pe.wait_ge(yr_act, n + 1)
                    pe.wait_ge(yr_dve, n + 1)
                    pe.wait_ge(acc_ok, n * 4)
                    scatter(pair)

            def all_pairs(r):
                gather(0)
                experts(r, 0, first=True)
                with pe.Fori(1, PAIRS - 1) as pair:
                    experts(r, pair)
                experts(r, PAIRS - 1, final=True)

            turn_weights(0)
            pe.wait_ge(pick_ok, 1)
            pe.wait_ge(h2r_ok, 4)
            all_pairs(0)
            pe.wait_ge(peak_ok, 1)
            most = pe.value_load(peak[:, :], min_val=0, max_val=S)
            for r in range(1, PASSES):
                with pe.If(most > CAP * r):
                    turn_weights(r)
                    pe.wait_ge(pick_ok, r + 1)
                    pe.wait_ge(acc_ok, r * PAIRS * 4)
                    all_pairs(r)

            feature_sum(4, meanm, sq2, KT, S, nm["rmsf", "sq"], nm["rmsf", "var"])
            pe.wait_ge(nm["rmsf", "out"], KT)
            for b in range(4):
                t, f0 = b // 2, (b % 2) * 4
                for f in range(4):
                    last = tr(ps[:, b, f * P:(f + 1) * P], H[:, f0 + f, t * P:(t + 1) * P], ident)
                last.then_inc(oturn, 1)

        @block.scalar
        def _(act):
            a = nc.scalar.activation
            row = 0
            for name, n in VEC:
                src = IN[name]
                names = "a b" if len(src.shape) == 2 else "b"
                flat = src.rearrange("a b -> (a b)") if len(src.shape) == 2 else src
                r, t = row % P, row // P
                act.dma_start(vrows[r:r + n, t, :], flat.rearrange("(r f) -> r f", f=P)).then_inc(vec_in, 16)
                row += n
            act.dma_start(crows, IN["conv_w_2"][0]).then_inc(vec_in, 16)
            act.dma_start(sink[:, :], IN["a_sink"].broadcast_to([P, NH])).then_inc(sink_in, 16)

            act.wait_ge(cst_in, 16)
            act.wait_ge(vec_ok, 1)
            act.wait_ge(sil_zero, 1)
            a(sil[:, :, 0:3], vec[:, 0:3 * KT].rearrange("p (v k) -> p k v", v=3), ACT.Silu).then_inc(sil_ok, 1)

            def mod_rows(stage, chunks, banks):
                for c in chunks:
                    act.wait_ge(st[stage], c + 1)
                    if c >= 2:
                        act.wait_ge(col_done[stage], c - 1)
                    a(modrow[:, c % 2, :], ps[:, banks[c % 2], :], ACT.Copy).then_inc(row_ok[stage], 1)

            mod_rows("ada0", range(6), (5, 6))

            def evac_in(stage, how):
                jobs = JOBS[stage]
                for i, (kind, m, _, _, eng) in enumerate(jobs):
                    if eng == "act":
                        act.wait_ge(st[stage], i + 1)
                        how(kind, m, i % 4).then_inc(tk[stage, "act"], 1)

            def from_a(kind, m, b):
                if kind == "q":
                    return a(qT[:, m, :], ps[:, b, :], ACT.Copy, scale=HD ** -0.5)
                if kind == "k":
                    return a(kTa[:, m, :], ps[:, b, :], ACT.Copy)
                return a(gT[:, m, :], ps[:, b, :], ACT.Silu)

            evac_in("a_in", from_a)
            for j in range(KT):
                act.wait_ge(u_ok, j + 1)
                a(H[:, j, :], H[:, j, :], ACT.Copy, scale=ALPHA).then_inc(alpha_ok, 1)

            def attention(L):
                un = UN[L]

                def exps(n):
                    h, kind, kts, _ = un[n]
                    w = len(kts) * P
                    act.wait_ge(at[L, "max"], n + 1)
                    if n >= 2:
                        act.wait_ge(at[L, "turned"], n - 1)
                    if n == 0 and L == "a":
                        act.wait_ge(sink_in, 16)
                    s = soft[:, n % 2]
                    for qb in range(2):
                        last = a(prob[:, n % 2, qb * T:qb * T + w], ps[:, 2 * (n % 2) + qb, 0:w], ACT.Exp,
                                 bias=s[:, 1, qb:qb + 1], accum_out=None if L == "c" else s[:, 2, qb:qb + 1])
                    if L == "a":
                        last = a(s[:, 3, :], s[:, 1, :], ACT.Exp, bias=sink[:, h:h + 1])
                    last.then_inc(at[L, "exp"], 1)

                exps(0)
                for n in range(len(un)):
                    act.wait_ge(at[L, "turned"], n + 1)
                    if n >= 2:
                        act.wait_ge(at[L, "pv"], n - 1)
                    a(probT[:, n % 2, 0:512], ps[:, 4, :], ACT.Copy).then_inc(at[L, "turn_act"], 1)
                    if n + 1 < len(un):
                        exps(n + 1)

            attention("a")

            def squares(N, src, dst, n, width, ready, base=0):
                for j in range(n):
                    act.wait_ge(ready, base + j + 1)
                    a(dst[:, j, 0:width], src[:, j, 0:width], ACT.Square).then_inc(nm[N, "sq"], 1)

            def root(N, bank, width, eps, scale=1.0):
                act.wait_ge(nm[N, "var"], 1)
                a(rstd[:, 0:width], ps[:, bank, 0:width], ACT.Sqrt, bias=eps, scale=scale).then_inc(nm[N, "std"], 1)

            mod_rows("ada1", range(1), (3, 6))
            squares("lna", H, sq, KT, T, nm["lna", "cent"])
            mod_rows("ada1", range(1, 3), (3, 6))
            root("lna", 5, T, eps_ln)
            mod_rows("ada1", range(3, 6), (3, 6))

            def from_b(kind, m, b):
                if kind == "q":
                    return a(qTb[:, m, :], ps[:, b, 0:S], ACT.Copy, scale=HD ** -0.5)
                if kind == "k":
                    return a(kTb[:, m, :], ps[:, b, :], ACT.Copy)
                if kind == "v":
                    return a(vb[:, m[1], m[0] * 512:(m[0] + 1) * 512], ps[:, b, :], ACT.Copy)
                return a(gTb[:, m, :], ps[:, b, 0:S], ACT.Silu)

            evac_in("b_in", from_b)
            for j in range(KT):
                act.wait_ge(u_ok, KT + j + 1)
                a(H[:, j, 0:S], H[:, j, 0:S], ACT.Copy, scale=ALPHA).then_inc(alpha_ok, 1)
            attention("b")
            mod_rows("mod_a", range(1), (3, 6))
            squares("lnb", H, sq, KT, S, nm["lnb", "cent"])
            mod_rows("mod_a", range(1, 3), (3, 6))
            root("lnb", 5, S, eps_ln)
            mod_rows("mod_a", range(3, 6), (3, 6))
            squares("rms1", H, sq2, KT, S, nm["lnb", "out"])
            root("rms1", 4, S, eps_rms)

            def from_c(kind, m, b):
                if kind == "b":
                    return a(sigb[:, m, :], ps[:, b, 0:S], ACT.Sigmoid)
                if kind == "q":
                    return a(qTc[:, m, :], ps[:, b, 0:S], ACT.Copy, scale=HD ** -0.5)
                if kind == "k":
                    return a(kTc[:, m, :], ps[:, b, 0:S], ACT.Copy)
                return a(vcr[:, m, :], ps[:, b, :], ACT.Copy)

            evac_in("c_in", from_c)
            mod_rows("mod_b", range(6), (5, 6))
            attention("c")
            squares("lnc", convo, csq, 4, S, nm["lnc", "cent"])
            root("lnc", 5, S, eps_rms, scale=1.0 / HID)
            for j in range(4):
                act.wait_ge(acc2_ok, j + 1)
                a(mixT[:, 4 + j, :], convo[:, j, :], ACT.Silu, scale=vc("conv_ln_g_2", j),
                  bias=vc("conv_ln_b_2", j)).then_inc(nm["lnc", "out"], 1)
            squares("rms2", H, sq2, KT, S, tk["c_out", "dve"])
            act.dma_start(wr[:, :, 0:NG], IN["w_router_group_2"][0].rearrange("(k p) n -> p k n", p=P)
                          ).then_inc(rt_in, 16)
            act.dma_start(wr[:, :, NG:NG + NE], IN["w_router_expert_2"][0].rearrange("(k p) n -> p k n", p=P)
                          ).then_inc(rt_in, 16)
            act.dma_start(rbias[:, 0:NG], IN["b_router_group_2"].broadcast_to([P, NG])).then_inc(rt_in, 16)
            act.dma_start(rbias[:, NG:NG + NE], IN["b_router_expert_2"].broadcast_to([P, NE])).then_inc(rt_in, 16)
            root("rms2", 4, S, eps_rms)

            for b in range(0, 4, 2):
                act.wait_ge(h2r_turn, b + 1)
                a(h2rows[:, b // 2, 0:512], ps[:, 1 + b, :], ACT.Copy).then_inc(h2r_ok, 1)
            act.wait_ge(gsub, 1)
            a(route[:, 2, 0:8], route[:, 1, 0:8], ACT.Exp).then_inc(gexp, 1)
            act.wait_ge(tdif, 1)
            a(route[:, 11, 2:4], route[:, 11, 0:2], ACT.Exp).then_inc(texp, 1)

            def turn_weights(r):
                for i in range(PAIRS // 2):
                    act.wait_ge(wturn, r * PAIRS // 2 + i + 1)
                    a(wpickT[:, i * 512:(i + 1) * 512], ps[:, 4 + i % 4, :], ACT.Copy).then_inc(wturn_ok, 1)

            def take_gather(n):
                act.wait_ge(gath, n * 2 + 1)
                a(xg[:, 0:4, :], ps[:, 0, :], ACT.Copy).then_inc(xg_act, 1)

            def experts(r, pair, final=False):
                n = r * PAIRS + pair
                act.wait_ge(gate_done, n + 1)
                a(sgl, ps[:, 2, :], ACT.Silu).then_inc(sg_ok, 1)
                if not final:
                    take_gather(n + 1)
                act.wait_ge(hid_turn, n + 1)
                a(hidT[:, :, :], ps[:, 4, :], ACT.Copy).then_inc(hidT_ok, 1)
                act.wait_ge(down_done, n + 1)
                a(yrows[:, 0:512], ps[:, 5, :], ACT.Copy).then_inc(yr_act, 1)

            def all_pairs(r):
                take_gather(r * PAIRS)
                with act.Fori(0, PAIRS - 1) as pair:
                    experts(r, pair)
                experts(r, PAIRS - 1, final=True)

            turn_weights(0)
            all_pairs(0)
            act.wait_ge(peak_ok, 1)
            most = act.value_load(peak[:, :], min_val=0, max_val=S)
            for r in range(1, PASSES):
                with act.If(most > CAP * r):
                    turn_weights(r)
                    all_pairs(r)

            squares("rmsf", H, sq2, KT, S, nm["rmsf", "cent"])
            root("rmsf", 4, S, eps_rms)
            for b in range(0, 4, 2):
                act.wait_ge(oturn, b + 1)
                a(outrows[:, b // 2, 0:512], ps[:, b, :], ACT.Copy).then_inc(orow_ok, 1)

        @block.vector
        def _(dve):
            v = nc.vector
            steps = [0]

            def step(ins):
                steps[0] += 1
                ins.then_inc(dve_step, 1)

            def settle():
                dve.wait_ge(dve_step, steps[0])

            over = [0]

            def do_over(ins):
                over[0] += 1
                ins.then_inc(over_step, 1)
                dve.wait_ge(over_step, over[0])

            v.memset(sil[:, :, :], 0.0).then_inc(sil_zero, 1)
            dve.wait_ge(cst_in, 16)
            dve.wait_ge(pe_vec, 1)
            step(v.tensor_copy(conv_taps[:, :, :],
                               ps[:, 0, 256:384].rearrange("p (c k) -> p c k", c=4)[:, :, 0:CONV_W]))
            v.tensor_copy(vec[:, :], ps[:, 0, 0:NVEC]).then_inc(vec_ok, 1)
            for j in range(KT):
                dve.wait_ge(pe_x, j + 1)
                v.tensor_copy(H[:, j, :], ps[:, 1 + j % 4, :]).then_inc(x_ok, 1)

            def take_modulation(l):
                stage = f"ada{l}"
                dve.wait_ge(col_done[stage], 6)
                if l == 0:
                    dve.wait_ge(vec_ok, 1)
                b = vec[:, VAT["b_ada"] + 24 * l:VAT["b_ada"] + 24 * (l + 1)]
                step(v.tensor_tensor(mod[:, l], ps[:, 7, 0:48].rearrange("p (m c) -> p m c", c=2),
                                     b.unsqueeze(2).broadcast_to([P, 24, 2]), ALU.add))
                settle()
                v.tensor_scalar(mod[:, l, 8:16, :], mod[:, l, 8:16, :], 1.0, None, ALU.add).then_inc(mod_ok, 1)
                dve.wait_ge(mod_ok, l + 1)

            def modulate(l):
                for j in range(KT):
                    step(v.tensor_scalar(uT[:, j, 0:S], H[:, j, 0:S], mod[:, l, 8 + j, 0:1], mod[:, l, j, 0:1],
                                         ALU.mult, ALU.add))
                    v.tensor_scalar(uT[:, j, S:T], H[:, j, S:T], mod[:, l, 8 + j, 1:2], mod[:, l, j, 1:2],
                                    ALU.mult, ALU.add).then_inc(u_ok, 1)

            take_modulation(0)
            dve.wait_ge(x_ok, KT)
            modulate(0)

            tmp = probT[:, 0, 0:512].rearrange("p (a t) -> p a t", a=2)
            dve.wait_ge(table_in, 16)
            dve.wait_ge(rel_out, 16)

            def rope(r):
                x = qT[:, r, 0:S] if r < 8 else kTa[:, r - 8, 0:S]
                dve.wait_ge(tk["a_in", "act"], r + 1)
                if r >= 1:
                    dve.wait_ge(rope_ok, r)
                step(v.tensor_tensor(tmp[:, 0, :], x, cos, ALU.mult))
                dve.wait_ge(rot_done, r + 1)
                step(v.tensor_tensor(tmp[:, 1, :], ps[:, 4 + r % 2, 0:S], sin, ALU.mult))
                settle()
                v.tensor_tensor(x, tmp[:, 0, :], tmp[:, 1, :], ALU.add).then_inc(rope_ok, 1)

            for r in range(10):
                rope(r)
                if r == 9:
                    for t in range(4):
                        dve.wait_ge(st["a_in"], 10 + t + 1)
                        v.tensor_copy(va[:, t, :], ps[:, (10 + t) % 4, 0:256]).then_inc(tk["a_in", "dve"], 1)
            dve.wait_ge(rope_ok, 10)
            for x in range(2):
                v.tensor_copy(kSa[64 * x:64 * x + 64], kTa[64 * (1 - x):64 * (1 - x) + 64]).then_inc(swap_ok, 1)

            def attention(L, prepare):
                un = UN[L]

                def row_max(n):
                    h, kind, kts, _ = un[n]
                    w = len(kts) * P
                    dve.wait_ge(at[L, "scores"], n + 1)
                    prepare(n, h, kind)
                    sc = ps[:, 2 * (n % 2):2 * (n % 2) + 2, 0:w]
                    s = soft[:, n % 2]
                    if n >= 2:
                        dve.wait_ge(at[L, "prob"], n - 1)
                    if L == "a":
                        step(v.tensor_reduce(s[:, 0, :], sc, AX.X, ALU.max))
                        settle()
                        v.tensor_scalar(s[:, 1, :], s[:, 0, :], sink[:, h:h + 1], -1.0, ALU.max, ALU.mult
                                        ).then_inc(at[L, "max"], 1)
                    else:
                        v.tensor_reduce(s[:, 1, :], sc, AX.X, ALU.max, negate=True).then_inc(at[L, "max"], 1)

                def normalise(n):
                    h, kind, kts, _ = un[n]
                    w = len(kts) * P
                    s = soft[:, n % 2]
                    dve.wait_ge(at[L, "exp"], n + 1)
                    if L == "a":
                        step(v.tensor_tensor(s[:, 2, :], s[:, 2, :], s[:, 3, :], ALU.add))
                        settle()
                    if L == "c":
                        mult = cs("mult").rearrange("p (q k) -> p q k", q=2)
                        for qb in range(2):
                            pr = prob[:, n % 2, qb * T:qb * T + w]
                            step(v.scalar_tensor_tensor(pr, pr, 1.0, mult[:, qb, :], ALU.mult, ALU.mult,
                                                        accum_out=s[:, 2, qb:qb + 1]))
                        settle()
                    step(v.reciprocal(s[:, 4, :], s[:, 2, :]))
                    settle()
                    for qb in range(2):
                        pr = prob[:, n % 2, qb * T:qb * T + w]
                        last = v.tensor_scalar(pr, pr, s[:, 4, qb:qb + 1], None, ALU.mult)
                    last.then_inc(at[L, "prob"], 1)

                def take_out(n):
                    g = n // 2
                    h, kind = un[n][0], un[n][1]
                    dve.wait_ge(at[L, "pv"], n + 1)
                    src = ps[:, 6 + g % 2, 0:S]
                    j, c0 = h // 2, 0 if kind == "lat" else S
                    if L == "a":
                        o = v.tensor_tensor(oT[:, j, c0:c0 + S], src, gT[:, j, c0:c0 + S], ALU.mult)
                    elif L == "b":
                        o = v.tensor_tensor(oT[:, j, 0:S], src, gTb[:, j, :], ALU.mult)
                    else:
                        o = v.tensor_copy(mixT[:, j, :], src)
                    o.then_inc(at[L, "o"], 1)

                row_max(0)
                normalise(0)
                row_max(1)
                for n in range(len(un)):
                    if len(un[n][2]) == 4:
                        dve.wait_ge(at[L, "turned"], n + 1)
                        if n >= 2:
                            dve.wait_ge(at[L, "pv"], n - 1)
                        v.tensor_copy(probT[:, n % 2, 512:1024], ps[:, 5, :]).then_inc(at[L, "turn_dve"], 1)
                    if n >= 1 and un[n - 1][3]:
                        take_out(n - 1)
                    if n + 1 < len(un):
                        normalise(n + 1)
                    if n + 2 < len(un):
                        row_max(n + 2)
                take_out(len(un) - 1)

            def mask_a(n, h, kind):
                if kind == "lat":
                    band = cs("band").rearrange("p (q k) -> p q k", q=2)
                    s0 = ps[:, 2 * (n % 2), P:2 * P]
                    s1 = ps[:, 2 * (n % 2) + 1, 0:P]
                    step(v.tensor_tensor(s0, s0, band[:, 0, :], ALU.add))
                    step(v.tensor_tensor(s1, s1, band[:, 1, :], ALU.add))
                    settle()

            def bias_b(n, h, kind):
                dve.wait_ge(bias_ok, h + 1)
                for qb in range(2):
                    sc = ps[:, 2 * (n % 2) + qb, 0:S].rearrange("p (r c) -> p r c", r=4)
                    b = bias[:, h % 2, (2 - 2 * qb) * GRID_W:(6 - 2 * qb) * GRID_W]
                    forwards = bass.AP(b.tensor, b.offset + GRID_W - 1,
                                       [list(b.ap[0]), [GRID_W, 4], [-1, GRID_W]])
                    ins = v.tensor_tensor(sc, sc, forwards, ALU.add)
                    if qb == 0:
                        step(ins)
                    else:
                        ins.then_inc(bias_used, 1)
                settle()
                dve.wait_ge(bias_used, h + 1)

            def bias_c(n, h, kind):
                slope = 2.0 ** (-8.0 * (h + 1) / NH2)
                dist = cs("dist").rearrange("p (q k) -> p q k", q=2)
                for qb in range(2):
                    sc = ps[:, 2 * (n % 2) + qb, 0:S]
                    step(v.scalar_tensor_tensor(sc, dist[:, qb, :], -slope, sc, ALU.mult, ALU.add))
                settle()

            dve.wait_ge(sink_in, 16)
            attention("a", mask_a)

            def residual(stage, l, parts, base):
                for m in range(KT):
                    dve.wait_ge(st[stage], m + 1)
                    dve.wait_ge(alpha_ok, base + m + 1)
                    for i, (c0, c1) in enumerate(parts):
                        ins = v.scalar_tensor_tensor(H[:, m, c0:c1], ps[:, m % 4, c0:c1], mod[:, l, 16 + m, i:i + 1],
                                                     H[:, m, c0:c1], ALU.mult, ALU.add)
                        if i < len(parts) - 1:
                            step(ins)
                            settle()
                    ins.then_inc(tk[stage, "dve"], 1)

            def layer_norm(N, l, w):
                dve.wait_ge(nm[N, "mean"], 1)
                for j in range(KT):
                    v.tensor_tensor(H[:, j, 0:w], H[:, j, 0:w], ps[:, 4, 0:w], ALU.subtract).then_inc(nm[N, "cent"], 1)
                dve.wait_ge(nm[N, "std"], 1)
                step(v.reciprocal(rstd[:, 0:w], rstd[:, 0:w]))
                settle()
                dve.wait_ge(nm[N, "sq"], KT)
                for j in range(KT):
                    step(v.tensor_tensor(H[:, j, 0:w], H[:, j, 0:w], rstd[:, 0:w], ALU.mult))
                    settle()
                    v.tensor_scalar(H[:, j, 0:w], H[:, j, 0:w], vc("ln_g", 8 * l + j), vc("ln_b", 8 * l + j),
                                    ALU.mult, ALU.add).then_inc(nm[N, "out"], 1)
                    if j == KT - 1:
                        dve.wait_ge(nm[N, "out"], KT)

            residual("a_out", 0, ((0, S), (S, T)), 0)
            layer_norm("lna", 0, T)
            take_modulation(1)
            modulate(1)

            jobs = JOBS["b_in"]
            for i, (kind, m, _, _, eng) in enumerate(jobs):
                if eng == "dve":
                    dve.wait_ge(st["b_in"], i + 1)
                    dst = kTb[:, m, :] if kind == "k" else vb[:, m[1], m[0] * 512:(m[0] + 1) * 512]
                    v.tensor_copy(dst, ps[:, i % 4, :]).then_inc(tk["b_in", "dve"], 1)
            attention("b", bias_b)
            residual("b_out", 1, ((0, S),), KT)
            layer_norm("lnb", 1, S)

            def gains(i, name, col):
                step(v.scalar_tensor_tensor(gain[:, i, :], mod2[:, col:col + KT], 1.0,
                                            vec[:, VAT[name]:VAT[name] + KT], ALU.add, ALU.mult))
                settle()

            def rms_norm(N, dst, gain_of, shift_of, sem_out):
                dve.wait_ge(nm[N, "std"], 1)
                step(v.reciprocal(rstd[:, 0:S], rstd[:, 0:S]))
                settle()
                for j in range(KT):
                    step(v.tensor_tensor(dst[:, j, 0:S], H[:, j, 0:S], rstd[:, 0:S], ALU.mult))
                    settle()
                    v.tensor_scalar(dst[:, j, 0:S], dst[:, j, 0:S], gain_of(j), shift_of(j), ALU.mult,
                                    ALU.add if shift_of(j) is not None else ALU.bypass).then_inc(sem_out, 1)

            dve.wait_ge(col_done["mod_a"], 6)
            v.tensor_tensor(mod2[:, 0:24], ps[:, 7, 0:24], vec[:, VAT["b_mod_2"]:VAT["b_mod_2"] + 24],
                            ALU.add).then_inc(mod_ok, 1)
            dve.wait_ge(mod_ok, 3)
            gains(0, "g_norm1_2", 8)
            rms_norm("rms1", h1T, lambda j: gain[:, 0, j:j + 1], lambda j: mod2[:, j:j + 1], nm["rms1", "out"])

            dve.wait_ge(zero_ok, 1)
            for m in range(4):
                dve.wait_ge(st["c_in"], 4 + m + 1)
                dve.wait_ge(tk["c_in", "act"], 4)
                v.tensor_tensor(glu[:, m, CONV_W - 1:], ps[:, m, 0:S], sigb[:, m, :], ALU.mult
                                ).then_inc(tk["c_in", "dve"], 1)
            dve.wait_ge(tk["c_in", "dve"], 4)
            base = steps[0]
            for j in range(4):
                step(v.tensor_scalar(convo[:, j, :], glu[:, j, 0:S], conv_taps[:, j, 0:1], vc("conv_b_2", j),
                                     ALU.mult, ALU.add))
            for k in range(1, CONV_W):
                for j in range(4):
                    dve.wait_ge(dve_step, base + 4 * (k - 1) + j + 1)
                    ins = v.scalar_tensor_tensor(convo[:, j, :], glu[:, j, k:k + S], conv_taps[:, j, k:k + 1],
                                                 convo[:, j, :], ALU.mult, ALU.add)
                    if k < CONV_W - 1:
                        step(ins)
                    else:
                        ins.then_inc(conv_ok, 1)
            dve.wait_ge(col_done["mod_b"], 6)
            v.tensor_tensor(mod2[:, 24:48], ps[:, 7, 0:24], vec[:, VAT["b_mod_2"] + 24:VAT["b_mod_2"] + 48],
                            ALU.add).then_inc(mod_ok, 1)
            dve.wait_ge(mod_ok, 4)
            attention("c", bias_c)
            dve.wait_ge(nm["lnc", "mean"], 1)
            step(v.tensor_scalar(probT[:, 0, 0:S], ps[:, 4, 0:S], 1.0 / HID, None, ALU.mult))
            settle()
            dve.wait_ge(conv_ok, 4)
            for j in range(4):
                v.tensor_tensor(convo[:, j, :], convo[:, j, :], probT[:, 0, 0:S], ALU.subtract
                                ).then_inc(nm["lnc", "cent"], 1)
            dve.wait_ge(nm["lnc", "std"], 1)
            step(v.reciprocal(rstd[:, 0:S], rstd[:, 0:S]))
            settle()
            for j in range(4):
                v.tensor_tensor(convo[:, j, :], convo[:, j, :], rstd[:, 0:S], ALU.mult).then_inc(acc2_ok, 1)

            for m in range(KT):
                dve.wait_ge(st["c_out"], m + 1)
                v.scalar_tensor_tensor(H[:, m, 0:S], ps[:, m % 4, 0:S], mod2[:, 16 + m:17 + m], H[:, m, 0:S],
                                       ALU.mult, ALU.add).then_inc(tk["c_out", "dve"], 1)
            dve.wait_ge(tk["c_out", "dve"], KT)
            gains(1, "g_norm2_2", 32)
            rms_norm("rms2", h2T, lambda j: gain[:, 1, j:j + 1], lambda j: mod2[:, 24 + j:25 + j], nm["rms2", "out"])

            def rr(i):
                return route[:, i, :].rearrange("p (t e) -> p t e", t=2)

            def r8(i):
                return route[:, i, 0:8].rearrange("p (t g) -> p t g", t=2)

            def r2(i, a=0):
                return route[:, i, a:a + 2]

            def bc(x, n):
                return x.unsqueeze(2).broadcast_to([P, 2, n])

            def do(ins):
                step(ins)
                settle()

            dve.wait_ge(logits, 1)
            dve.wait_ge(rt_in, 64)
            lg = ps[:, 0, 0:128].rearrange("p (t e) -> p t e", t=2)
            do(v.tensor_tensor(r8(0), lg[:, :, 0:NG], rbias[:, 0:NG].unsqueeze(1).broadcast_to([P, 2, NG]), ALU.add))
            do(v.tensor_tensor(rr(3), lg[:, :, NG:NG + NE], rbias[:, NG:NG + NE].unsqueeze(1).broadcast_to([P, 2, NE]),
                               ALU.add))
            do(v.tensor_reduce(r2(4), r8(0), AX.X, ALU.max))
            v.tensor_tensor(r8(1), r8(0), bc(r2(4), NG), ALU.subtract).then_inc(gsub, 1)

            def first_max(onehot, score, x, top, n, desc):
                do(v.tensor_tensor(score, x, bc(top, n), ALU.is_equal))
                do(v.tensor_tensor(score, score, desc.unsqueeze(1).broadcast_to([P, 2, n]), ALU.mult))
                do(v.tensor_reduce(r2(5), score, AX.X, ALU.max))
                do(v.tensor_tensor(onehot, score, bc(r2(5), n), ALU.is_equal))

            first_max(r8(6), r8(7), r8(0), r2(4), NG, cs("desc")[:, NE - NG:NE])
            do(v.tensor_scalar(r8(6), r8(6), BIG, -BIG, ALU.mult, ALU.add))
            for t in range(2):
                e3 = route[:, 3, t * NE:(t + 1) * NE].rearrange("p (g e) -> p g e", g=NG)
                pen = route[:, 6, t * NG:(t + 1) * NG].unsqueeze(2).broadcast_to([P, NG, EPG])
                do(v.tensor_tensor(e3, e3, pen, ALU.add))
            do(v.tensor_reduce(r2(8), rr(3), AX.X, ALU.max))
            first_max(rr(12), rr(9), rr(3), r2(8), NE, cs("desc"))
            do(v.scalar_tensor_tensor(rr(3), rr(12), -3 * BIG, rr(3), ALU.mult, ALU.add))
            do(v.tensor_reduce(r2(10), rr(3), AX.X, ALU.max))
            first_max(rr(13), rr(9), rr(3), r2(10), NE, cs("desc"))
            sel = rr(14)
            v.tensor_tensor(sel, rr(12), rr(13), ALU.add).then_inc(sel_ok, 1)
            v.tensor_tensor(r2(11), r2(10), r2(8), ALU.subtract).then_inc(tdif, 1)
            dve.wait_ge(gexp, 1)
            do(v.tensor_reduce(r2(15), r8(2), AX.X, ALU.add))
            dve.wait_ge(texp, 1)
            do(v.tensor_scalar(r2(15, 2), r2(11, 2), 1.0, None, ALU.add))
            do(v.tensor_tensor(r2(15, 4), r2(15, 0), r2(15, 2), ALU.mult))
            do(v.reciprocal(r2(15, 6), r2(15, 4)))
            do(v.tensor_tensor(r2(15, 8), r2(15, 6), r2(11, 2), ALU.mult))
            do(v.tensor_tensor(rr(12), rr(12), bc(r2(15, 6), NE), ALU.mult))
            do(v.tensor_tensor(rr(13), rr(13), bc(r2(15, 8), NE), ALU.mult))
            do(v.tensor_tensor(wsel[:, :, :], rr(12), rr(13), ALU.add))
            dve.wait_ge(ranks, 1)
            dve.wait_ge(sel_ok, 1)
            rk = ps[:, 5, 0:2 * NE].rearrange("p (t e) -> p t e", t=2)
            do(v.scalar_tensor_tensor(keysel[:, :, :], rk, 1.0, sel, ALU.add, ALU.mult))
            do(v.tensor_scalar(keysel[:, :, :], keysel[:, :, :], -1.0, None, ALU.add))
            do(v.tensor_reduce(peakf[:, :], ps[:, 5, 64:64 + NE], AX.X, ALU.max))
            v.tensor_copy(peak[:, :], peakf[0:1, :]).then_inc(peak_ok, 1)
            for b in range(1, 4, 2):
                dve.wait_ge(h2r_turn, b + 1)
                v.tensor_copy(h2rows[:, b // 2, 512:1024], ps[:, 1 + b, :]).then_inc(h2r_ok, 1)

            def slots(r, do):
                if r:
                    do(v.tensor_scalar(keysel[:, :, :], keysel[:, :, :], -1.0 * CAP, None, ALU.add))
                for t in range(2):
                    ins = v.tensor_tensor(pick[:, t, :].rearrange("p (e s) -> p e s", e=NE),
                                          keysel[:, t, :].unsqueeze(2).broadcast_to([P, NE, CAP]),
                                          cs("slot").unsqueeze(1).broadcast_to([P, NE, CAP]), ALU.is_equal)
                ins.then_inc(pick_ok, 1)
                dve.wait_ge(pick_ok, r + 1)
                for t in range(2):
                    ins = v.tensor_tensor(wpick[:, t, :].rearrange("p (e s) -> p e s", e=NE),
                                          pick[:, t, :].rearrange("p (e s) -> p e s", e=NE),
                                          wsel[:, t, :].unsqueeze(2).broadcast_to([P, NE, CAP]), ALU.mult)
                ins.then_inc(wpick_ok, 1)

            def take_gather(n):
                dve.wait_ge(gath, n * 2 + 2)
                v.tensor_copy(xg[:, 4:8, :], ps[:, 1, :]).then_inc(xg_dve, 1)

            def accumulate(n):
                for i, b in enumerate((7, 2, 3, 0)):
                    dve.wait_ge(scat, n * 4 + i + 1)
                    y = yacc[:, i * 512:(i + 1) * 512]
                    v.tensor_tensor(y, ps[:, b, :], y, ALU.add).then_inc(acc_ok, 1)

            def experts(r, pair, first=False, final=False):
                n = r * PAIRS + pair
                dve.wait_ge(up_done, n + 1)
                dve.wait_ge(sg_ok, n + 1)
                v.tensor_tensor(hid, ps[:, 3, :], sgl, ALU.mult).then_inc(hid_ok, 1)
                if not final:
                    take_gather(n + 1)
                if not first:
                    accumulate(n - 1)
                dve.wait_ge(down_done, n + 1)
                v.tensor_copy(yrows[:, 512:1024], ps[:, 6, :]).then_inc(yr_dve, 1)
                if final:
                    accumulate(n)

            def all_pairs(r):
                take_gather(r * PAIRS)
                experts(r, 0, first=True)
                with dve.Fori(1, PAIRS - 1) as pair:
                    experts(r, pair)
                experts(r, PAIRS - 1, final=True)

            slots(0, do)
            dve.wait_ge(acc_zero, 1)
            all_pairs(0)
            dve.wait_ge(peak_ok, 1)
            most = dve.value_load(peak[:, :], min_val=0, max_val=S)
            for r in range(1, PASSES):
                with dve.If(most > CAP * r):
                    slots(r, do_over)
                    all_pairs(r)
                    dve.wait_ge(acc_ok, 4 * PAIRS * (r + 1))

            dve.wait_ge(acc_ok, 4 * PAIRS)
            for m in range(KT):
                v.scalar_tensor_tensor(H[:, m, 0:S], yacc[:, m * S:(m + 1) * S], mod2[:, 40 + m:41 + m],
                                       H[:, m, 0:S], ALU.mult, ALU.add).then_inc(nm["rmsf", "cent"], 1)
            dve.wait_ge(nm["rmsf", "cent"], KT)
            dve.wait_ge(nm["rmsf", "sq"], KT)
            rms_norm("rmsf", H, lambda j: vc("g_final_2", j), lambda j: None, nm["rmsf", "out"])
            for b in range(1, 4, 2):
                dve.wait_ge(oturn, b + 1)
                v.tensor_copy(outrows[:, b // 2, 512:1024], ps[:, b, :]).then_inc(orow_ok, 1)


_INS = ["x", "c", "ctx", "c_ctx", "w_ada", "b_ada", "ln_g", "ln_b", "a_w_in", "a_w_out", "a_sink", "b_w_in",
        "b_w_out", "b_rel_bias", "c_2", "w_mod_2", "b_mod_2", "g_norm1_2", "w_in_2", "conv_w_2", "conv_b_2",
        "conv_ln_g_2", "conv_ln_b_2", "w_out_2", "g_norm2_2", "w_router_group_2", "b_router_group_2",
        "w_router_expert_2", "b_router_expert_2", "w_exp_gate_2", "w_exp_up_2", "w_exp_down_2", "g_final_2"]


def kernel(**inputs):
    import numpy as _np
    import concourse.bacc as _bacc
    from concourse import mybir as _mybir
    from concourse.bass_utils import run_bass_kernel_spmd as _run

    nc = _bacc.Bacc("TRN2", target_bir_lowering=False, num_devices=1)
    arrays, aps = {}, {}
    for name in _INS:
        a = _np.ascontiguousarray(inputs[name])
        arrays[f"in_{name}"] = a
        aps[name] = nc.dram_tensor(f"in_{name}", a.shape, _mybir.dt.from_np(a.dtype), kind="ExternalInput").ap()
    arrays["in_consts"] = constants()
    consts = nc.dram_tensor("in_consts", arrays["in_consts"].shape, _mybir.dt.float32, kind="ExternalInput").ap()
    relpad = nc.dram_tensor("relpad", (NH * REL_H, PADW), _mybir.dt.float32, kind="Internal").ap()
    out = nc.dram_tensor("out_0", (1, S, D), _mybir.dt.float32, kind="ExternalOutput").ap()
    build(nc, aps, consts, relpad, out)
    r = _run(nc, [arrays], core_ids=[0])
    return r.results[0]["out_0"]
```

```python
from contextlib import ExitStack

import numpy as np
import concourse.bass as bass
from concourse import mybir

F32 = mybir.dt.float32
I32 = mybir.dt.int32
ACT = mybir.ActivationFunctionType
ALU = mybir.AluOpType
AX = mybir.AxisListType

P = 128
D = 1024
KT = D // P
S = 256
C = 256
T = S + C
NH = 16
HD = 64
KVH = 4
GRID_W = 64
KW = 16
REL_W, REL_H = 2 * KW - 1, 15
PADW = 2 * GRID_W - 1
BROWS = 6
NH2 = 8
CONV_W = 31
NG, EPG = 4, 8
NE = NG * EPG
HID = 512
CAP = 64
PAIRS = NE // 2
PASSES = -(-S // CAP)
COLS = 512
SLOTS = 6
ALPHA = 4.0 ** 0.25
BIG = 1e30


def const_layout():
    at, n = {}, 0
    for name, w in (("ident", P), ("fold", 3), ("eps", 2), ("mean", P), ("before", P), ("dist", 2 * S),
                    ("mult", 2 * S), ("col", GRID_W), ("slot", CAP), ("desc", NE),
                    ("cos", S), ("sin", S), ("rot", P), ("band", 2 * P)):
        at[name] = (n, n + w)
        n += w
    return at, n


def constants():
    at, n = const_layout()
    out = np.zeros((P, n), np.float32)

    def put(name, a):
        out[:, at[name][0]:at[name][1]] = np.asarray(a, np.float32).reshape(a.shape[0], -1)

    p, q = np.arange(P)[:, None], np.arange(P)[None, :]
    put("ident", (p == q) * 1.0)
    put("mean", np.full((P, P), 1.0 / D))
    rot = np.zeros((P, P), np.float32)
    for m in range(P):
        if m % 32 < 16:
            rot[m + 16, m] = -1.0
        else:
            rot[m - 16, m] = 1.0
    put("rot", rot)
    put("before", (p < q) * 1.0)
    t = np.arange(S)
    inv = np.float32(10000.0) ** (-np.arange(16, dtype=np.float32) / np.float32(16))
    sub = np.arange(P) % HD
    pos = np.where((sub < 32)[:, None], (t // GRID_W)[None, :], (t % GRID_W)[None, :]).astype(np.float32)
    ang = (pos * inv[sub % 16][:, None]).astype(np.float32)
    put("cos", np.cos(ang))
    put("sin", np.sin(ang))
    put("band", np.concatenate([np.where(q > p, -BIG, 0.0), np.where(p > q, -BIG, 0.0)], axis=1))
    d = (np.arange(2)[None, :, None] * P + np.arange(P)[:, None, None]) - np.arange(S)[None, None, :]
    mult = np.where(d >= 0, (d <= 128) * 1.0 + (d % 4 == 0) + (d % 16 == 0), 0.0)
    put("dist", np.where(mult > 0, d, BIG))
    put("mult", mult)
    qc, kc = np.arange(P)[:, None] % GRID_W, np.arange(GRID_W)[None, :]
    first = np.clip(qc - KW // 2, 0, GRID_W - KW)
    put("col", np.where((kc >= first) & (kc < first + KW), 0.0, -BIG)[:, ::-1])
    put("slot", np.tile(np.arange(CAP), (P, 1)))
    put("desc", np.tile(NE - np.arange(NE), (P, 1)))
    put("fold", np.arange(P)[:, None] % 32 == np.arange(3)[None, :])
    put("eps", np.tile(np.array([1e-5, 1e-6]), (P, 1)))
    return out


VEC = [("c", 8), ("c_ctx", 8), ("c_2", 8), ("b_ada", 48), ("ln_g", 16), ("ln_b", 16), ("g_norm1_2", 8),
       ("g_norm2_2", 8), ("g_final_2", 8), ("b_mod_2", 48), ("conv_b_2", 4), ("conv_ln_g_2", 4), ("conv_ln_b_2", 4)]
VAT = {}
for _name, _n in VEC:
    VAT[_name] = sum(VAT_n for _, VAT_n in VEC[:[v[0] for v in VEC].index(_name)])
NVEC = sum(n for _, n in VEC)
VROWS1 = NVEC - P


def chunk_plan():
    plan = []
    for stage, src, l, columns in (
            ("ada0", "w_ada", 0, range(4)), ("a_in", "a_w_in", 0, range(3)),
            ("ada0", "w_ada", 0, (4, 5)),
            ("a_in", "a_w_in", 0, (3, 4)),
            ("ada1", "w_ada", 1, range(4)), ("a_out", "a_w_out", 0, range(2)), ("ada1", "w_ada", 1, (4, 5)),
            ("b_in", "b_w_in", 0, range(8)),
            ("mod_a", "w_mod_2", 0, range(4)), ("b_out", "b_w_out", 0, range(2)), ("mod_a", "w_mod_2", 0, (4, 5)),
            ("c_in", "w_in_2", 0, (4, 3, 0, 1, 2)),
            ("mod_b", "w_mod_2", 0, range(6, 12)), ("c_out", "w_out_2", 0, range(2))):
        plan += [(stage, src, l, c) for c in columns]
    return plan


PLAN = chunk_plan()
ROUNDS = len(PLAN) // SLOTS
PLACE = {}
for _i, _c in enumerate(PLAN):
    PLACE.setdefault(_c[0], []).append(_i)


def in_jobs(stage):
    if stage == "a_in":
        jobs = [("q", m, m // 4, (m % 4) * P, "act") for m in range(8)]
        jobs += [("k", m, 2, m * P, "act") for m in range(2)]
        jobs += [("v", t, 2, 2 * P, "dve") for t in range(4)]
        jobs += [("g", m, 3 + m // 4, (m % 4) * P, "act") for m in range(8)]
    elif stage == "b_in":
        jobs = [("q", m, m // 4, (m % 4) * P, "act") for m in range(8)]
        jobs += [("k", m, 2 + m // 4, (m % 4) * P, "dve" if m % 2 else "act") for m in range(8)]
        jobs += [("v", (h, t), 4 + h, 0, "dve" if t % 2 else "act") for h in range(2) for t in range(4)]
        jobs += [("g", m, 6 + m // 4, (m % 4) * P, "act") for m in range(8)]
    else:
        jobs = [("b", m, 0, m * P, "act") for m in range(4)]
        jobs += [("a", m, 1, m * P, "dve") for m in range(4)]
        jobs += [("q", m, 2, m * P, "act") for m in range(4)]
        jobs += [("k", m, 3, m * P, "act") for m in range(4)]
        jobs += [("v", t, 4, 0, "act") for t in range(2)]
    return jobs


def taken_by(jobs, i):
    eng = jobs[i][4]
    return eng, sum(1 for j in jobs[:i + 1] if j[4] == eng)


def units(layer):
    if layer == "a":
        return [(p, kind, qb, kts) for kind, kts in (("lat", (0, 1, 2, 3)), ("ctx", (2, 3)))
                for p in range(NH // 2) for qb in range(2)]
    if layer == "b":
        return [(p, "lat", qb, (0, 1, 2, 3)) for p in range(NH // 2) for qb in range(2)]
    return [(p, "lat", qb, (0, 1)[:qb + 1]) for p in range(NH2 // 2) for qb in range(2)]


AHEAD = 3


def build(nc, IN, consts_dram, relpad, out):
    CA, CN = const_layout()
    with ExitStack() as ctx:
        def sb(name, shape, dt=F32):
            return ctx.enter_context(nc.sbuf_tensor(name, shape, dt))

        def sem(name):
            return ctx.enter_context(nc.semaphore(name))

        ring = sb("ring", [P, SLOTS, KT * COLS])
        CR = CA["cos"][0]
        cst = sb("cst", [P, CR])
        H = sb("H", [P, KT, T])
        U = sb("U", [P, KT * T])
        Q = sb("Q", [P, KT * T])
        G = sb("G", [P, KT * T])
        K = sb("K", [P, KT * T])
        prob = sb("prob", [P, AHEAD, 2 * T])
        probT = sb("probT", [P, 2 * T])
        bias = sb("bias", [P, 4, BROWS * GRID_W])
        vec = sb("vec", [P, NVEC])
        conv_taps = sb("conv_taps", [P, 4, CONV_W])
        sil = sb("sil", [P, KT, 32])
        mod = sb("mod", [P, 2, 24, 2])
        mod2 = sb("mod2", [P, 48])
        gain = sb("gain", [P, 2, KT])
        sink = sb("sink", [P, NH])
        negsink = sb("negsink", [P, NH])
        soft = sb("soft", [P, 4, 5, 2])
        peak = sb("peak", [1, 1], I32)
        peakf = sb("peakf", [P, 1])
        ps = ctx.enter_context(nc.psum_tensor("ps", [P, 8, 512], F32))

        def cs(name):
            return cst[:, CA[name][0]:CA[name][1]]

        flat = bias[:, :, :].rearrange("p a b -> p (a b)")

        def table(name):
            return flat[:, CA[name][0] - CR:CA[name][1] - CR]

        cos, sin, rotm, band = table("cos"), table("sin"), table("rot"), table("band")

        def vc(name, j=0):
            return vec[:, VAT[name] + j:VAT[name] + j + 1]

        ident, meanm, before = cs("ident"), cs("mean"), cs("before")
        eps_ln, eps_rms = cs("eps")[:, 0:1], cs("eps")[:, 1:2]

        xrows = Q[:, :].rearrange("p (t f) -> p t f", t=4)
        vrows = K[:, 0:2 * P].rearrange("p (t f) -> p t f", t=2)
        crows = K[0:CONV_W, 512:512 + HID]
        uT = U[:, :].rearrange("p (j t) -> p j t", j=KT)
        oT = uT
        qT = Q[:, :].rearrange("p (j t) -> p j t", j=KT)
        gT = G[:, :].rearrange("p (j t) -> p j t", j=KT)
        kTa = K[:, 0:1024].rearrange("p (j t) -> p j t", j=2)
        kSa = K[:, 1024:2048].rearrange("p (j t) -> p j t", j=2)
        va = K[:, 2048:3072].rearrange("p (t f) -> p t f", t=4)
        qTb = Q[:, 0:2048].rearrange("p (j t) -> p j t", j=KT)
        gTb = Q[:, 2048:4096].rearrange("p (j t) -> p j t", j=KT)
        kTb = K[:, :].rearrange("p (j t) -> p j t", j=KT)
        vb = G[:, :].rearrange("p (t f) -> p t f", t=4)
        sq = Q[:, :].rearrange("p (j t) -> p j t", j=KT)
        rstd = prob[:, 0, 0:512]
        mixT = U[:, 0:2048].rearrange("p (j t) -> p j t", j=KT)
        h1T = U[:, 2048:4096].rearrange("p (j t) -> p j t", j=KT)
        qTc = K[:, 0:1024].rearrange("p (j t) -> p j t", j=4)
        kTc = K[:, 1024:2048].rearrange("p (j t) -> p j t", j=4)
        vcr = K[:, 2048:3072].rearrange("p (t f) -> p t f", t=2)
        sigb = K[:, 3072:4096].rearrange("p (j t) -> p j t", j=4)
        GLU_W = CONV_W - 1 + S
        glu = G[:, 0:4 * GLU_W].rearrange("p (j t) -> p j t", j=4)
        convo = G[:, 2048:3072].rearrange("p (j t) -> p j t", j=4)
        csq = G[:, 3072:4096].rearrange("p (j t) -> p j t", j=4)
        sq2 = Q[:, 0:2048].rearrange("p (j t) -> p j t", j=KT)
        h2T = Q[:, 2048:4096].rearrange("p (j t) -> p j t", j=KT)
        yacc = U[:, 0:2048]
        h2rows = U[:, 2048:4096].rearrange("p (t f) -> p t f", t=2)
        pick = flat[:, 0:2 * P].rearrange("p (t s) -> p t s", t=2)
        wpick = flat[:, 2 * P:4 * P].rearrange("p (t s) -> p t s", t=2)
        wpickT = flat[:, 4 * P:6 * P]
        xg = prob[:, 0, :].rearrange("p (j s) -> p j s", j=KT)
        yrows = probT[:, :]
        hidT = prob[:, 1, 0:512].rearrange("p (k s) -> p k s", k=4)
        sgl, hid = prob[:, 2, 0:512], prob[:, 2, 512:1024]
        modrow = prob[:, 1, :].rearrange("p (b n) -> p b n", b=2)
        route = probT[:, :].rearrange("p (r n) -> p r n", n=2 * 32)
        outrows = Q[:, 0:2048].rearrange("p (t f) -> p t f", t=2)
        wr = flat[:, 6 * P:6 * P + KT * 36].rearrange("p (j n) -> p j n", j=KT)
        rbias = flat[:, 9 * P:9 * P + 36]
        keysel = H[:, 0, S:S + 2 * NE].rearrange("p (t e) -> p t e", t=2)
        wsel = H[:, 1, S:S + 2 * NE].rearrange("p (t e) -> p t e", t=2)
        ones = H[:, 2, S:S + P]

        table_in = sem("table_in")
        cst_in, vec_in, x_in, sink_in = sem("cst_in"), sem("vec_in"), sem("x_in"), sem("sink_in")
        rel_in, rel_out, rel_zero = sem("rel_in"), sem("rel_out"), sem("rel_zero")
        full = [sem(f"full{i}") for i in range(SLOTS)]
        pe_vec, vec_ok = sem("pe_vec"), sem("vec_ok")
        pe_x, x_ok = sem("pe_x"), sem("x_ok")
        sil_ok = sem("sil_ok")
        st = {n: sem(n + "_done") for n in ("ada0", "a_in", "a_out", "ada1", "b_in", "b_out", "mod_a", "c_in",
                                            "c_out", "mod_b")}
        tk = {(n, e): sem(f"{n}_taken_{e}") for n in ("a_in", "b_in", "c_in") for e in ("act", "dve")}
        tk.update({(n, "dve"): sem(f"{n}_taken_dve") for n in ("a_out", "b_out", "c_out")})
        mod_ok, u_ok, alpha_ok = sem("mod_ok"), sem("u_ok"), sem("alpha_ok")
        rot_done, rope_ok, swap_ok = sem("rot_done"), sem("rope_ok"), sem("swap_ok")
        dve_step, over_step = sem("dve_step"), sem("over_step")
        at = {}
        for L in "abc":
            for n in ("scores", "max", "exp", "sums", "prob", "turned", "copied", "pv", "o"):
                at[L, n] = sem(f"{L}_{n}")
        bias_in, bias_ok, bias_used = [sem(f"bias_in{i}") for i in range(4)], sem("bias_ok"), sem("bias_used")
        nm = {}
        for N in ("lna", "lnb", "rms1", "lnc", "rms2", "rmsf"):
            for n in ("mean", "cent", "sq", "var", "std", "out"):
                if N[:2] == "ln" or n != "mean" and (n != "cent" or N == "rmsf"):
                    nm[N, n] = sem(f"{N}_{n}")
        conv_ok, zero_ok = sem("conv_ok"), sem("zero_ok")
        rt_in, logits, h2r_turn, h2r_ok = sem("rt_in"), sem("logits"), sem("h2r_turn"), sem("h2r_ok")
        gsub, gexp, tdif, texp, sel_ok, ranks = (sem(n) for n in ("gsub", "gexp", "tdif", "texp", "sel_ok", "ranks"))
        peak_ok, pick_ok, wpick_ok = sem("peak_ok"), sem("pick_ok"), sem("wpick_ok")
        wturn, wturn_ok = sem("wturn"), sem("wturn_ok")
        gath, xg_act, xg_dve = sem("gath"), sem("xg_act"), sem("xg_dve")
        gate_done, up_done, down_done = sem("gate_done"), sem("up_done"), sem("down_done")
        sg_ok, hid_ok, hid_turn, hidT_ok = sem("sg_ok"), sem("hid_ok"), sem("hid_turn"), sem("hidT_ok")
        yr_act, yr_dve = sem("yr_act"), sem("yr_dve")
        row_ok, col_done = sem("row_ok"), sem("col_done")
        CHUNKS = {"ada0": 0, "ada1": 6, "mod_a": 12, "mod_b": 18}
        sil_zero = sem("sil_zero")
        extra_in = sem("extra_in")
        scaled = sem("scaled")
        scat, acc_ok, acc_zero = sem("scat"), sem("acc_ok"), sem("acc_zero")
        oturn, orow_ok, out_done = sem("oturn"), sem("orow_ok"), sem("out_done")
        acc2_ok, ones_ok = sem("acc2_ok"), sem("ones_ok")

        UN = {L: units(L) for L in "abc"}
        JOBS = {s: in_jobs(s) for s in ("a_in", "b_in", "c_in")}
        used = {}
        for s in JOBS:
            used[s] = [sum(1 for j in JOBS[s] if j[2] <= c) for c in range(1 + max(j[2] for j in JOBS[s]))]
        for s in ("a_out", "b_out", "c_out"):
            used[s] = [4, 8]
        for s in ("ada0", "ada1", "mod_a", "mod_b"):
            used[s] = [c + 1 for c in range(6)]

        def slot(n):
            return ring[:, n % SLOTS, :].rearrange("p (k n) -> p k n", k=KT)

        def dslot(n):
            return ring[:, n, :].rearrange("p (k n) -> p k n", k=4)

        def chunk(n, c):
            second, first = isinstance(n, int) and n == 1, isinstance(n, int) and n == 0
            if second and c < SLOTS // 2:
                return (K, G, Q)[c][:, :].rearrange("p (k n) -> p k n", k=KT), extra_in, 16 * SLOTS // 2
            s = c if first else (c + SLOTS // 2) % SLOTS
            count = ROUNDS + 1 if first else ROUNDS + n + (s < SLOTS // 2)
            return (dslot if c >= 4 else slot)(s), full[s], count * 16

        block = ctx.enter_context(nc.Block())

        @block.sync
        def _(sp):
            def load_bias(heads):
                sp.wait_ge(rel_out, 16)
                sp.wait_ge(at["a", "max"], len(UN["a"]))
                for h in heads:
                    if h >= 4:
                        sp.wait_ge(bias_used, 2 * (h // 2 - 1))
                    for half in range(2):
                        first = (h * REL_H + BROWS - 1 - half) * PADW
                        src = bass.AP(relpad.tensor, first, [[1, GRID_W], [PADW, BROWS], [1, GRID_W]])
                        sp.dma_start(bias[half * 64:half * 64 + 64, h % 4].rearrange("p (r c) -> p r c", r=BROWS),
                                     src).then_inc(bias_in[h % 4], 16)

            CF = CA["mean"][0]
            sp.dma_start(cst[:, 0:CF], consts_dram[:, 0:CF]).then_inc(cst_in, 16)
            sp.dma_start(xrows[:, 0:2, :], IN["x"][0].rearrange("(t p) f -> p t f", p=P)).then_inc(x_in, 16)
            sp.dma_start(xrows[:, 2:4, :], IN["ctx"][0].rearrange("(t p) f -> p t f", p=P)).then_inc(x_in, 16)
            sp.wait_ge(vec_in, 16 * (len(VEC) + 1))
            for n, (stage, src, l, c) in enumerate(PLAN):
                if n - SLOTS == PLACE["b_in"][2]:
                    load_bias(range(4))
                if n - SLOTS == PLACE["mod_a"][0]:
                    load_bias(range(4, NH))
                if n >= SLOTS:
                    was = PLAN[n - SLOTS][0]
                    sp.wait_ge(st[was], used[was][PLACE[was].index(n - SLOTS)])
                w = IN[src][l, :, c * COLS:(c + 1) * COLS].rearrange("(k p) n -> p k n", p=P)
                sp.dma_start(slot(n), w).then_inc(full[n % SLOTS], 16)
                if n == 4:
                    sp.dma_start(flat[:, 0:CN - CR], consts_dram[:, CR:CN]).then_inc(table_in, 16)
                    sp.dma_start(cst[:, CF:CR], consts_dram[:, CF:CR]).then_inc(table_in, 16)

            wg, wu, wd = (IN[f"w_exp_{n}_2"][0] for n in ("gate", "up", "down"))

            def load_pair(n, e, free):
                for i, w in enumerate((wg, wu, wd)):
                    for x in range(2):
                        view, landed, _ = chunk(n, 2 * i + x)
                        free(2 * i + x)
                        sp.dma_start(view, w[bass.ds(e + x, 1)].rearrange("e (k p) n -> p (e k) n", p=P)
                                     ).then_inc(landed, 16)

            def after_plan(c):
                stage = PLAN[len(PLAN) - SLOTS + c][0]
                sp.wait_ge(st[stage], used[stage][PLACE[stage].index(len(PLAN) - SLOTS + c)])

            load_pair(0, 0, after_plan)

            def after_first(c):
                sp.wait_ge(*((at["c", "o"], len(UN["c"])), (nm["lnc", "out"], 4), (h2r_ok, 4),
                             (gate_done, 1), (gate_done, 1), (up_done, 1))[c])

            load_pair(1, 2, after_first)

            def stream(n, pair):
                load_pair(n, pair * 2, lambda c: sp.wait_ge((gate_done, up_done, down_done)[c // 2], n))

            load_pair(2, 4, lambda c: sp.wait_ge(*((up_done, 1), (down_done, 1), (down_done, 1),
                                                   (up_done, 2), (down_done, 2), (down_done, 2))[c]))
            with sp.Fori(3, PAIRS) as pair:
                stream(pair, pair)
            sp.wait_ge(peak_ok, 1)
            most = sp.value_load(peak[:, :], min_val=0, max_val=S)
            for r in range(1, PASSES):
                with sp.If(most > CAP * r):
                    with sp.Fori(0, PAIRS) as pair:
                        stream(r * PAIRS + pair, pair)
            sp.wait_ge(orow_ok, 4)
            sp.dma_start(out[0].rearrange("(t p) f -> p t f", p=P), outrows).then_inc(out_done, 16)
            sp.wait_ge(out_done, 16)

        @block.gpsimd
        def _(pool):
            pool.wait_ge(cst_in, 16)
            padr = probT[0:120, 0:2 * PADW].rearrange("p (a w) -> p a w", a=2)
            pool.memset(padr, 0.0).then_inc(rel_zero, 1)
            pool.wait_ge(rel_zero, 1)
            relr = probT[0:120, 512:512 + 2 * REL_W].rearrange("p (a w) -> p a w", a=2)
            pool.dma_start(relr, IN["b_rel_bias"][0].rearrange("h d w -> (h d) w").rearrange("(a p) w -> p a w", a=2)
                           ).then_inc(rel_in, 16)
            pool.wait_ge(rel_in, 16)
            backwards = bass.AP(relr.tensor, relr.offset + REL_W - 1,
                                [list(relr.ap[0]), [REL_W, 2], [-1, REL_W]])
            pool.tensor_copy(padr[:, :, GRID_W - KW:GRID_W - KW + REL_W], backwards).then_inc(rel_zero, 1)
            pool.wait_ge(rel_zero, 2)
            pool.dma_start(relpad.rearrange("(a p) w -> p a w", a=2), padr).then_inc(rel_out, 16)

            def mask_bias(p):
                for h in (2 * p, 2 * p + 1):
                    pool.wait_ge(bias_in[h % 4], 32 * (h // 4 + 1))
                    tile = bias[:, h % 4].rearrange("p (r c) -> p r c", r=BROWS)
                    pool.tensor_tensor(tile, tile, cs("col").unsqueeze(1).broadcast_to([P, BROWS, GRID_W]),
                                       ALU.add).then_inc(bias_ok, 1)

            for p in range(NH // 2):
                mask_bias(p)
            pool.wait_ge(at["b", "pv"], len(UN["b"]))
            pool.memset(glu[:, :, 0:CONV_W - 1], 0.0).then_inc(zero_ok, 1)
            pool.memset(ones, 1.0).then_inc(ones_ok, 1)
            pool.wait_ge(tk["c_out", "dve"], KT)
            pool.memset(yacc, 0.0).then_inc(acc_zero, 1)

        @block.tensor
        def _(pe):
            mm, tr = nc.tensor.matmul, nc.tensor.transpose

            def landed(n):
                pe.wait_ge(full[n % SLOTS], 16 * (n // SLOTS + 1))

            pe.wait_ge(cst_in, 16)
            pe.wait_ge(vec_in, 16 * (len(VEC) + 1))
            tr(ps[:, 0, 0:P], vrows[:, 0, :], ident)
            tr(ps[:, 0, P:P + VROWS1], vrows[0:VROWS1, 1, :], ident[0:VROWS1, 0:VROWS1])
            for c in range(4):
                last = tr(ps[:, 0, 256 + 32 * c:256 + 32 * c + CONV_W], crows[:, c * P:(c + 1) * P],
                          ident[0:CONV_W, 0:CONV_W])
            last.then_inc(pe_vec, 1)
            pe.wait_ge(x_in, 32)
            for j in range(KT):
                if j >= 4:
                    pe.wait_ge(x_ok, j - 3)
                for t in range(4):
                    last = tr(ps[:, 1 + j % 4, t * P:(t + 1) * P], xrows[:, t, j * P:(j + 1) * P], ident)
                last.then_inc(pe_x, 1)

            def stream(stage, c, bank):
                n = PLACE[stage][c]
                landed(n)
                for i in range(2):
                    for t in range(4):
                        k = 2 * t + i
                        last = mm(ps[32 * t:32 * t + 32, bank, :], sil[:, k, :], slot(n)[:, k, :],
                                  start=(i == 0), stop=(i == 1))
                last.then_inc(st[stage], 1)

            def fold(stage, c, v0, nv, bank):
                pe.wait_ge(row_ok, CHUNKS[stage] + c + 1)
                for m in range(4):
                    col = (4 * c + m) * nv
                    last = mm(ps[:, bank, col:col + nv], modrow[:, c % 2, m * P:(m + 1) * P],
                              cs("fold")[:, v0:v0 + nv], start=True, stop=True)
                last.then_inc(col_done, 1)

            def modulation(stage, chunks, v0, nv, banks, to):
                for c in chunks:
                    stream(stage, c, banks[c % 2])
                    if c != chunks[0]:
                        fold(stage, c - 1, v0, nv, to)
                fold(stage, chunks[-1], v0, nv, to)
            pe.wait_ge(sil_ok, 1)
            modulation("ada0", range(4), 0, 2, (5, 6), 7)

            def in_proj(stage, src, widths, after=None):
                jobs = JOBS[stage]
                seen = -1
                for i, (kind, m, c, col, _) in enumerate(jobs):
                    n = PLACE[stage][c]
                    if c != seen:
                        landed(n)
                        seen = c
                    if i >= 4:
                        e, cnt = taken_by(jobs, i - 4)
                        pe.wait_ge(tk[stage, e], cnt)
                    b = i % 4
                    for k in range(KT):
                        if i == 0:
                            pe.wait_ge(*src_ready(stage, k))
                        w = slot(n)[:, k, :]
                        if kind == "v":
                            t = m[1] if stage == "b_in" else m
                            wid = 256 if stage == "a_in" else 512
                            last = mm(ps[:, b, 0:wid], src[:, k, t * P:(t + 1) * P], w[:, col:col + wid],
                                      start=(k == 0), stop=(k == KT - 1))
                        else:
                            wid = widths[kind]
                            last = mm(ps[:, b, 0:wid], w[:, col:col + P], src[:, k, 0:wid],
                                      start=(k == 0), stop=(k == KT - 1))
                    last.then_inc(st[stage], 1)
                    if after:
                        after(i)

            def src_ready(stage, k):
                if stage == "a_in":
                    return u_ok, k + 1
                if stage == "b_in":
                    return u_ok, KT + k + 1
                return nm["rms1", "out"], k + 1

            pe.wait_ge(table_in, 32)

            def beside(i):
                rotate(i)
                if i == 13:
                    pe.wait_ge(rope_ok, 10)
                    modulation("ada0", (4, 5), 0, 2, (5, 6), 4)

            def rotate(i):
                if 1 <= i <= 10:
                    r = i - 1
                    pe.wait_ge(tk["a_in", "act"], r + 1)
                    if r >= 2:
                        pe.wait_ge(rope_ok, r - 1)
                    src = qT[:, r, 0:S] if r < 8 else kTa[:, r - 8, 0:S]
                    mm(ps[:, 4 + r % 2, 0:S], rotm, src, start=True, stop=True).then_inc(rot_done, 1)

            in_proj("a_in", uT, {"q": T, "k": T, "g": T}, beside)
            pe.wait_ge(mod_ok, 2)

            def attention(L, q_of, k_of, v_of):
                un = UN[L]

                def scores(n):
                    p, kind, qb, kts = un[n]
                    if n >= 2:
                        pe.wait_ge(at[L, "exp"], n - 1)
                    for x in range(2):
                        h = 2 * p + x
                        last = mm(ps[:, 2 * (n % 2) + x, 0:len(kts) * P], q_of(h, kind, qb), k_of(h, kts),
                                  start=True, stop=True)
                    last.then_inc(at[L, "scores"], 1)

                for n in range(AHEAD):
                    scores(n)
                for n, (p, kind, qb, kts) in enumerate(un):
                    pe.wait_ge(at[L, "prob"], n + 1)
                    for i in range(len(kts)):
                        for x in range(2):
                            last = tr(ps[:, 4 + i // 2, (i % 2) * S + x * P:(i % 2) * S + (x + 1) * P],
                                      prob[:, n % AHEAD, x * T + i * P:x * T + (i + 1) * P], ident)
                    last.then_inc(at[L, "turned"], 1)
                    if n + AHEAD < len(un):
                        scores(n + AHEAD)
                    pe.wait_ge(at[L, "copied"], n + 1)
                    if n >= 2:
                        pe.wait_ge(at[L, "o"], n - 1)
                    for i, kt in enumerate(kts):
                        for x in range(2):
                            last = mm(ps[x * HD:(x + 1) * HD, 6 + n % 2, 0:P], v_of(2 * p + x, kt),
                                      probT[:, i * S + x * P:i * S + (x + 1) * P],
                                      start=(i == 0), stop=(i == len(kts) - 1))
                    last.then_inc(at[L, "pv"], 1)

            def half(h):
                return slice((h % 2) * HD, (h % 2) * HD + HD)

            def q_a(h, kind, qb):
                c0 = (0 if kind == "lat" else S) + qb * P
                return qT[half(h), h // 2, c0:c0 + P]

            def k_a(h, kts):
                kv = h // (NH // KVH)
                src = kTa if kv % 2 == h % 2 else kSa
                return src[half(h), kv // 2, kts[0] * P:(kts[-1] + 1) * P]

            def v_a(h, kt):
                kv = h // (NH // KVH)
                return va[:, kt, kv * HD:(kv + 1) * HD]

            pe.wait_ge(rope_ok, 10)
            pe.wait_ge(swap_ok, 2)
            pe.wait_ge(tk["a_in", "dve"], 4)
            pe.wait_ge(tk["a_in", "act"], 18)
            attention("a", q_a, k_a, v_a)

            def out_proj(stage, src, width, late=KT):
                def part(m, ks):
                    n = PLACE[stage][m // 4]
                    if m % 4 == 0:
                        landed(n)
                    if m >= 4 and ks[0] == 0:
                        pe.wait_ge(tk[stage, "dve"], m - 3)
                    for k in ks:
                        last = mm(ps[:, m % 4, 0:width], slot(n)[:, k, (m % 4) * P:(m % 4 + 1) * P], src[:, k, 0:width],
                                  start=(k == 0), stop=(k == KT - 1))
                    if k == KT - 1:
                        last.then_inc(st[stage], 1)

                if late < KT:
                    for m in range(4):
                        part(m, range(late))
                    pe.wait_ge(nm["lnc", "out"], 4)
                    for m in range(4):
                        part(m, range(late, KT))
                for m in range(4 if late < KT else 0, KT):
                    part(m, range(KT))

            def feature_sum(bank, mat, src, n, width, ready, done):
                for j in range(n):
                    pe.wait_ge(ready, j + 1)
                    last = mm(ps[:, bank, 0:width], mat, src[:, j, 0:width], start=(j == 0), stop=(j == n - 1))
                last.then_inc(done, 1)

            def norm_stats(N, src, width, before, gates):
                feature_sum(4, meanm, H, KT, width, before, nm[N, "mean"])
                stage, v0, nv = gates
                for c in (4, 5):
                    stream(stage, c, (3, 6)[c % 2])
                feature_sum(5, meanm, src, KT, width, nm[N, "sq"], nm[N, "var"])
                for c in (4, 5):
                    fold(stage, c, v0, nv, 7)

            pe.wait_ge(at["a", "o"], len(UN["a"]) - 1)
            modulation("ada1", range(4), 0, 2, (4, 5), 6)
            pe.wait_ge(at["a", "o"], len(UN["a"]))
            out_proj("a_out", oT, T)
            pe.wait_ge(mod_ok, 3)
            norm_stats("lna", sq, T, tk["a_out", "dve"], ("ada1", 0, 2))

            in_proj("b_in", uT, {"q": S, "k": T, "g": S})
            pe.wait_ge(tk["b_in", "dve"], sum(j[4] == "dve" for j in JOBS["b_in"]))
            pe.wait_ge(tk["b_in", "act"], sum(j[4] == "act" for j in JOBS["b_in"]))
            pe.wait_ge(mod_ok, 4)
            attention("b", lambda h, kind, qb: qTb[half(h), h // 2, qb * P:(qb + 1) * P],
                      lambda h, kts: kTb[half(h), h // 2, 0:len(kts) * P],
                      lambda h, kt: vb[:, kt, h * HD:(h + 1) * HD])
            pe.wait_ge(at["b", "o"], len(UN["b"]) - 1)
            modulation("mod_a", range(4), 2, 1, (4, 5), 6)
            pe.wait_ge(at["b", "o"], len(UN["b"]))
            out_proj("b_out", oT, S)
            pe.wait_ge(mod_ok, 5)
            norm_stats("lnb", sq, S, tk["b_out", "dve"], ("mod_a", 2, 1))
            feature_sum(4, meanm, sq2, KT, S, nm["rms1", "sq"], nm["rms1", "var"])

            in_proj("c_in", h1T, {"a": S, "b": S, "q": S, "k": S})
            pe.wait_ge(tk["c_in", "act"], sum(j[4] == "act" for j in JOBS["c_in"]))
            pe.wait_ge(tk["c_in", "dve"], 4)
            pe.wait_ge(mod_ok, 6)
            modulation("mod_b", range(3), 2, 1, (5, 6), 7)
            pe.wait_ge(mod_ok, 7)
            attention("c", lambda h, kind, qb: qTc[half(h), h // 2, qb * P:(qb + 1) * P],
                      lambda h, kts: kTc[half(h), h // 2, 0:len(kts) * P],
                      lambda h, kt: vcr[:, kt, h * HD:(h + 1) * HD])
            pe.wait_ge(at["c", "o"], len(UN["c"]) - 1)
            stream("mod_b", 3, 5)
            pe.wait_ge(conv_ok, 4)
            feature_sum(4, meanm, convo, 4, S, conv_ok, nm["lnc", "mean"])
            stream("mod_b", 4, 3)
            fold("mod_b", 3, 2, 1, 6)
            feature_sum(2, meanm, csq, 4, S, nm["lnc", "sq"], nm["lnc", "var"])
            stream("mod_b", 5, 5)
            fold("mod_b", 4, 2, 1, 6)
            fold("mod_b", 5, 2, 1, 6)
            pe.wait_ge(at["c", "o"], len(UN["c"]))
            pe.wait_ge(nm["lnc", "std"], 1)
            out_proj("c_out", mixT, S, late=4)
            feature_sum(4, meanm, sq2, KT, S, nm["rms2", "sq"], nm["rms2", "var"])
            pe.wait_ge(rt_in, 64)
            for t in range(2):
                for k in range(KT):
                    if t == 0:
                        pe.wait_ge(nm["rms2", "out"], k + 1)
                    last = mm(ps[:, 0, t * 64:t * 64 + 36], h2T[:, k, t * P:(t + 1) * P], wr[:, k, :],
                              start=(k == 0), stop=(k == KT - 1))
            last.then_inc(logits, 1)
            for b in range(4):
                t, f0 = b // 2, (b % 2) * 4
                for f in range(4):
                    last = tr(ps[:, 1 + b, f * P:(f + 1) * P], h2T[:, f0 + f, t * P:(t + 1) * P], ident)
                last.then_inc(h2r_turn, 1)
            sel = route[:, 14, :].rearrange("p (t e) -> p t e", t=2)
            pe.wait_ge(sel_ok, 1)
            pe.wait_ge(ones_ok, 1)
            mm(ps[:, 5, 0:NE], before, sel[:, 0, :], start=True, stop=True)
            mm(ps[:, 5, NE:2 * NE], ones, sel[:, 0, :], start=True, stop=False)
            mm(ps[:, 5, NE:2 * NE], before, sel[:, 1, :], start=False, stop=True)
            mm(ps[:, 5, 64:64 + NE], ones, sel[:, 0, :], start=True, stop=False)
            mm(ps[:, 5, 64:64 + NE], ones, sel[:, 1, :], start=False, stop=True).then_inc(ranks, 1)

            def gather(n):
                pe.wait_ge(pick_ok, n + 1)
                for j in range(KT):
                    for t in range(2):
                        last = mm(ps[:, j // 4, (j % 4) * P:(j % 4 + 1) * P], h2rows[:, t, j * P:(j + 1) * P],
                                  pick[:, t, :], start=(t == 0), stop=(t == 1))
                    if j % 4 == 3:
                        last.then_inc(gath, 1)

            def scatter(n):
                pe.wait_ge(wturn_ok, n + 1)
                for m in range(KT):
                    last = mm(ps[:, (7, 2, 3, 0)[m // 2], (m % 2) * S:(m % 2 + 1) * S], yrows[:, m * P:(m + 1) * P],
                              wpickT, start=True, stop=True)
                    if m % 2 == 1:
                        last.then_inc(scat, 1)

            def experts(r, pair, first=False, final=False):
                n = r * PAIRS + pair
                pe.wait_ge(xg_act, n + 1)
                pe.wait_ge(xg_dve, n + 1)
                if not first:
                    pe.wait_ge(acc_ok, (n - 1) * 4)
                for i, done in enumerate((gate_done, up_done)):
                    for x in range(2):
                        pe.wait_ge(*chunk(n, 2 * i + x)[1:])
                    for k in range(KT):
                        for x in range(2):
                            last = mm(ps[x * CAP:(x + 1) * CAP, 2 + i, :], xg[:, k, x * CAP:(x + 1) * CAP],
                                      chunk(n, 2 * i + x)[0][:, k, :], start=(k == 0), stop=(k == KT - 1))
                    last.then_inc(done, 1)
                if not final:
                    gather(n + 1)
                pe.wait_ge(hid_ok, n + 1)
                if not (first and r == 0):
                    pe.wait_ge(wturn_ok, n)
                for k in range(4):
                    last = tr(ps[:, 4, k * P:(k + 1) * P], hid[:, k * P:(k + 1) * P], ident)
                last.then_inc(hid_turn, 1)
                if not first:
                    if not final:
                        pe.wait_ge(xg_act, n + 2)
                    pe.wait_ge(yr_act, n)
                    pe.wait_ge(yr_dve, n)
                    scatter(n - 1)
                for x in range(2):
                    pe.wait_ge(*chunk(n, 4 + x)[1:])
                pe.wait_ge(hidT_ok, n + 1)
                pe.wait_ge(wpick_ok, n + 1)
                for t in range(2):
                    last = tr(ps[:, 4, t * P:(t + 1) * P], wpick[:, t, :], ident)
                last.then_inc(wturn, 1)
                for k in range(4):
                    for c in range(2):
                        for x in range(2):
                            last = mm(ps[x * CAP:(x + 1) * CAP, 5 + c, :], hidT[:, k, x * CAP:(x + 1) * CAP],
                                      chunk(n, 4 + x)[0][:, k, c * 512:(c + 1) * 512], start=(k == 0), stop=(k == 3))
                last.then_inc(down_done, 1)
                if final:
                    pe.wait_ge(yr_act, n + 1)
                    pe.wait_ge(yr_dve, n + 1)
                    pe.wait_ge(acc_ok, n * 4)
                    scatter(n)

            def all_pairs(r):
                gather(r * PAIRS)
                experts(r, 0, first=True)
                if r == 0:
                    experts(r, 1)
                with pe.Fori(1 if r else 2, PAIRS - 1) as pair:
                    experts(r, pair)
                experts(r, PAIRS - 1, final=True)

            pe.wait_ge(h2r_ok, 4)
            all_pairs(0)
            pe.wait_ge(peak_ok, 1)
            most = pe.value_load(peak[:, :], min_val=0, max_val=S)
            for r in range(1, PASSES):
                with pe.If(most > CAP * r):
                    pe.wait_ge(acc_ok, r * PAIRS * 4)
                    all_pairs(r)

            feature_sum(4, meanm, sq2, KT, S, nm["rmsf", "sq"], nm["rmsf", "var"])
            pe.wait_ge(nm["rmsf", "out"], KT)
            for b in range(4):
                t, f0 = b // 2, (b % 2) * 4
                for f in range(4):
                    last = tr(ps[:, b, f * P:(f + 1) * P], H[:, f0 + f, t * P:(t + 1) * P], ident)
                last.then_inc(oturn, 1)

        @block.scalar
        def _(act):
            a = nc.scalar.activation
            row = 0
            for name, n in VEC:
                src = IN[name]
                names = "a b" if len(src.shape) == 2 else "b"
                flat = src.rearrange("a b -> (a b)") if len(src.shape) == 2 else src
                r, t = row % P, row // P
                act.dma_start(vrows[r:r + n, t, :], flat.rearrange("(r f) -> r f", f=P)).then_inc(vec_in, 16)
                row += n
            act.dma_start(crows, IN["conv_w_2"][0]).then_inc(vec_in, 16)
            act.dma_start(sink[:, :], IN["a_sink"].broadcast_to([P, NH])).then_inc(sink_in, 16)

            act.wait_ge(cst_in, 16)
            act.wait_ge(vec_ok, 1)
            act.wait_ge(sil_zero, 1)
            a(sil[:, :, 0:3], vec[:, 0:3 * KT].rearrange("p (v k) -> p k v", v=3), ACT.Silu).then_inc(sil_ok, 1)

            def mod_rows(stage, chunks, banks):
                for c in chunks:
                    act.wait_ge(st[stage], c + 1)
                    if c >= 2:
                        act.wait_ge(col_done, CHUNKS[stage] + c - 1)
                    a(modrow[:, c % 2, :], ps[:, banks[c % 2], :], ACT.Copy).then_inc(row_ok, 1)

            mod_rows("ada0", range(4), (5, 6))

            def evac_in(stage, how):
                jobs = JOBS[stage]
                for i, (kind, m, _, _, eng) in enumerate(jobs):
                    if stage == "a_in" and i == 14:
                        mod_rows("ada0", (4, 5), (5, 6))
                    if eng == "act":
                        act.wait_ge(st[stage], i + 1)
                        how(kind, m, i % 4).then_inc(tk[stage, "act"], 1)

            def from_a(kind, m, b):
                if kind == "q":
                    return a(qT[:, m, :], ps[:, b, :], ACT.Copy, scale=HD ** -0.5)
                if kind == "k":
                    return a(kTa[:, m, :], ps[:, b, :], ACT.Copy)
                return a(gT[:, m, :], ps[:, b, :], ACT.Silu)

            evac_in("a_in", from_a)
            for j in range(KT):
                act.wait_ge(u_ok, j + 1)
                a(H[:, j, :], H[:, j, :], ACT.Copy, scale=ALPHA).then_inc(alpha_ok, 1)

            def attention(L):
                un = UN[L]

                def exps(n):
                    w = len(un[n][3]) * P
                    act.wait_ge(at[L, "max"], n + 1)
                    if n >= AHEAD:
                        act.wait_ge(at[L, "turned"], n - AHEAD + 1)
                    s = soft[:, n % 4]
                    for x in range(2):
                        last = a(prob[:, n % AHEAD, x * T:x * T + w], ps[:, 2 * (n % 2) + x, 0:w], ACT.Exp,
                                 bias=s[:, 1, x:x + 1], accum_out=None if L == "c" else s[:, 2, x:x + 1])
                    for x in range(2 if L == "a" else 0):
                        h = 2 * un[n][0] + x
                        last = a(s[:, 3, x:x + 1], sink[:, h:h + 1], ACT.Exp, bias=s[:, 1, x:x + 1])
                    last.then_inc(at[L, "exp"], 1)

                exps(0)
                exps(1)
                for n in range(len(un)):
                    kts = len(un[n][3])
                    src = ps[:, 4, 0:kts * S] if kts <= 2 else ps[:, 4:6, :]
                    act.wait_ge(at[L, "turned"], n + 1)
                    if n >= 1:
                        act.wait_ge(at[L, "pv"], n)
                    a(probT[:, 0:kts * S], src, ACT.Copy).then_inc(at[L, "copied"], 1)
                    if n + 2 < len(un):
                        exps(n + 2)

            attention("a")

            mod_rows("ada1", range(4), (4, 5))

            def squares(N, src, dst, n, width, ready, base=0):
                for j in range(n):
                    act.wait_ge(ready, base + j + 1)
                    a(dst[:, j, 0:width], src[:, j, 0:width], ACT.Square).then_inc(nm[N, "sq"], 1)

            def root(N, bank, width, eps, scale=1.0):
                act.wait_ge(nm[N, "var"], 1)
                a(rstd[:, 0:width], ps[:, bank, 0:width], ACT.Sqrt, bias=eps, scale=scale).then_inc(nm[N, "std"], 1)

            def norm_stats(N, stage, width):
                squares(N, H, sq, KT, width, nm[N, "cent"])
                mod_rows(stage, (4, 5), (3, 6))
                root(N, 5, width, eps_ln)

            norm_stats("lna", "ada1", T)
            for j in range(KT):
                act.wait_ge(scaled, j + 1)
                a(uT[:, j, 0:S], H[:, j, 0:S], ACT.Identity, scale=mod[:, 1, 8 + j, 0:1], bias=mod[:, 1, j, 0:1])
                a(uT[:, j, S:T], H[:, j, S:T], ACT.Identity, scale=mod[:, 1, 8 + j, 1:2], bias=mod[:, 1, j, 1:2]
                  ).then_inc(u_ok, 1)

            def from_b(kind, m, b):
                if kind == "q":
                    return a(qTb[:, m, :], ps[:, b, 0:S], ACT.Copy, scale=HD ** -0.5)
                if kind == "k":
                    return a(kTb[:, m, :], ps[:, b, :], ACT.Copy)
                if kind == "v":
                    return a(vb[:, m[1], m[0] * 512:(m[0] + 1) * 512], ps[:, b, :], ACT.Copy)
                return a(gTb[:, m, :], ps[:, b, 0:S], ACT.Silu)

            evac_in("b_in", from_b)
            attention("b")
            act.dma_start(wr[:, :, 0:NG], IN["w_router_group_2"][0].rearrange("(k p) n -> p k n", p=P)
                          ).then_inc(rt_in, 16)
            act.dma_start(wr[:, :, NG:NG + NE], IN["w_router_expert_2"][0].rearrange("(k p) n -> p k n", p=P)
                          ).then_inc(rt_in, 16)
            act.dma_start(rbias[:, 0:NG], IN["b_router_group_2"].broadcast_to([P, NG])).then_inc(rt_in, 16)
            act.dma_start(rbias[:, NG:NG + NE], IN["b_router_expert_2"].broadcast_to([P, NE])).then_inc(rt_in, 16)
            mod_rows("mod_a", range(4), (4, 5))
            norm_stats("lnb", "mod_a", S)
            squares("rms1", H, sq2, KT, S, nm["lnb", "out"])
            root("rms1", 4, S, eps_rms)

            def rms_out(N, base, dst, gain_of, shift_of):
                for j in range(KT):
                    act.wait_ge(scaled, base + j + 1)
                    if shift_of:
                        ins = a(dst[:, j, 0:S], dst[:, j, 0:S], ACT.Identity, scale=gain_of(j), bias=shift_of(j))
                    else:
                        ins = a(dst[:, j, 0:S], dst[:, j, 0:S], ACT.Copy, scale=gain_of(j))
                    ins.then_inc(nm[N, "out"], 1)

            rms_out("rms1", KT, h1T, lambda j: gain[:, 0, j:j + 1], lambda j: mod2[:, j:j + 1])

            def from_c(kind, m, b):
                if kind == "b":
                    return a(sigb[:, m, :], ps[:, b, 0:S], ACT.Sigmoid)
                if kind == "q":
                    return a(qTc[:, m, :], ps[:, b, 0:S], ACT.Copy, scale=HD ** -0.5)
                if kind == "k":
                    return a(kTc[:, m, :], ps[:, b, 0:S], ACT.Copy)
                return a(vcr[:, m, :], ps[:, b, :], ACT.Copy)

            evac_in("c_in", from_c)
            mod_rows("mod_b", range(3), (5, 6))
            attention("c")
            mod_rows("mod_b", (3,), (3, 5))
            squares("lnc", convo, csq, 4, S, nm["lnc", "cent"])
            mod_rows("mod_b", (4,), (3, 5))
            root("lnc", 2, S, eps_rms, scale=float(D // HID))
            mod_rows("mod_b", (5,), (3, 5))
            for j in range(4):
                act.wait_ge(acc2_ok, j + 1)
                a(mixT[:, 4 + j, :], convo[:, j, :], ACT.Silu, scale=vc("conv_ln_g_2", j),
                  bias=vc("conv_ln_b_2", j)).then_inc(nm["lnc", "out"], 1)
            squares("rms2", H, sq2, KT, S, tk["c_out", "dve"])
            root("rms2", 4, S, eps_rms)
            rms_out("rms2", 2 * KT, h2T, lambda j: gain[:, 1, j:j + 1], lambda j: mod2[:, 24 + j:25 + j])

            def take_rows(b):
                act.wait_ge(h2r_turn, b + 1)
                a(h2rows[:, b // 2, (b % 2) * 512:(b % 2 + 1) * 512], ps[:, 1 + b, :], ACT.Copy).then_inc(h2r_ok, 1)

            take_rows(0)
            take_rows(1)
            act.wait_ge(gsub, 1)
            a(route[:, 2, 0:8], route[:, 1, 0:8], ACT.Exp).then_inc(gexp, 1)
            take_rows(2)
            take_rows(3)
            act.wait_ge(tdif, 1)
            a(route[:, 11, 2:4], route[:, 11, 0:2], ACT.Exp).then_inc(texp, 1)

            def take_gather(n):
                act.wait_ge(gath, n * 2 + 1)
                a(xg[:, 0:4, :], ps[:, 0, :], ACT.Copy).then_inc(xg_act, 1)

            def experts(r, pair, final=False):
                n = r * PAIRS + pair
                act.wait_ge(gate_done, n + 1)
                a(sgl, ps[:, 2, :], ACT.Silu).then_inc(sg_ok, 1)
                if not final:
                    take_gather(n + 1)
                act.wait_ge(hid_turn, n + 1)
                a(hidT[:, :, :], ps[:, 4, :], ACT.Copy).then_inc(hidT_ok, 1)
                act.wait_ge(wturn, n + 1)
                a(wpickT, ps[:, 4, 0:2 * P], ACT.Copy).then_inc(wturn_ok, 1)
                act.wait_ge(down_done, n + 1)
                a(yrows[:, 0:512], ps[:, 5, :], ACT.Copy).then_inc(yr_act, 1)

            def all_pairs(r):
                take_gather(r * PAIRS)
                with act.Fori(0, PAIRS - 1) as pair:
                    experts(r, pair)
                experts(r, PAIRS - 1, final=True)

            all_pairs(0)
            act.wait_ge(peak_ok, 1)
            most = act.value_load(peak[:, :], min_val=0, max_val=S)
            for r in range(1, PASSES):
                with act.If(most > CAP * r):
                    all_pairs(r)

            squares("rmsf", H, sq2, KT, S, nm["rmsf", "cent"])
            root("rmsf", 4, S, eps_rms)
            rms_out("rmsf", 3 * KT, H, lambda j: vc("g_final_2", j), None)
            for b in range(0, 4, 2):
                act.wait_ge(oturn, b + 1)
                a(outrows[:, b // 2, 0:512], ps[:, b, :], ACT.Copy).then_inc(orow_ok, 1)

        @block.vector
        def _(dve):
            v = nc.vector
            steps = [0]

            def step(ins):
                steps[0] += 1
                ins.then_inc(dve_step, 1)

            def settle():
                dve.wait_ge(dve_step, steps[0])

            over = [0]

            def do_over(ins):
                over[0] += 1
                ins.then_inc(over_step, 1)
                dve.wait_ge(over_step, over[0])

            v.memset(sil[:, :, :], 0.0).then_inc(sil_zero, 1)
            dve.wait_ge(cst_in, 16)
            dve.wait_ge(pe_vec, 1)
            step(v.tensor_copy(conv_taps[:, :, :],
                               ps[:, 0, 256:384].rearrange("p (c k) -> p c k", c=4)[:, :, 0:CONV_W]))
            v.tensor_copy(vec[:, :], ps[:, 0, 0:NVEC]).then_inc(vec_ok, 1)
            for j in range(KT):
                dve.wait_ge(pe_x, j + 1)
                v.tensor_copy(H[:, j, :], ps[:, 1 + j % 4, :]).then_inc(x_ok, 1)

            def take_modulation(l):
                stage = f"ada{l}"
                dve.wait_ge(col_done, CHUNKS[stage] + 4)
                if l == 0:
                    dve.wait_ge(vec_ok, 1)
                step(take_columns(l, 0, 16))
                settle()
                v.tensor_scalar(mod[:, l, 8:16, :], mod[:, l, 8:16, :], 1.0, None, ALU.add).then_inc(mod_ok, 1)
                dve.wait_ge(mod_ok, 2 * l + 1)

            def take_gates(l):
                dve.wait_ge(col_done, CHUNKS[f"ada{l}"] + 6)
                take_columns(l, 16, 24).then_inc(mod_ok, 1)

            def take_columns(l, c0, c1):
                bank = (7, 4)[c0 > 0] if l == 0 else (6, 7)[c0 > 0]
                b = vec[:, VAT["b_ada"] + 24 * l + c0:VAT["b_ada"] + 24 * l + c1]
                return v.tensor_tensor(mod[:, l, c0:c1], ps[:, bank, 2 * c0:2 * c1].rearrange("p (m c) -> p m c", c=2),
                                       b.unsqueeze(2).broadcast_to([P, c1 - c0, 2]), ALU.add)

            def modulate(l):
                for j in range(KT):
                    step(v.tensor_scalar(uT[:, j, 0:S], H[:, j, 0:S], mod[:, l, 8 + j, 0:1], mod[:, l, j, 0:1],
                                         ALU.mult, ALU.add))
                    v.tensor_scalar(uT[:, j, S:T], H[:, j, S:T], mod[:, l, 8 + j, 1:2], mod[:, l, j, 1:2],
                                    ALU.mult, ALU.add).then_inc(u_ok, 1)

            take_modulation(0)
            dve.wait_ge(x_ok, KT)
            modulate(0)

            tmp = probT[:, 0:512].rearrange("p (a t) -> p a t", a=2)
            dve.wait_ge(table_in, 32)
            dve.wait_ge(rel_out, 16)

            def rope(r):
                x = qT[:, r, 0:S] if r < 8 else kTa[:, r - 8, 0:S]
                dve.wait_ge(tk["a_in", "act"], r + 1)
                if r >= 1:
                    dve.wait_ge(rope_ok, r)
                step(v.tensor_tensor(tmp[:, 0, :], x, cos, ALU.mult))
                dve.wait_ge(rot_done, r + 1)
                step(v.tensor_tensor(tmp[:, 1, :], ps[:, 4 + r % 2, 0:S], sin, ALU.mult))
                settle()
                v.tensor_tensor(x, tmp[:, 0, :], tmp[:, 1, :], ALU.add).then_inc(rope_ok, 1)

            for r in range(10):
                rope(r)
                if r == 9:
                    for t in range(4):
                        dve.wait_ge(st["a_in"], 10 + t + 1)
                        v.tensor_copy(va[:, t, :], ps[:, (10 + t) % 4, 0:256]).then_inc(tk["a_in", "dve"], 1)
            take_gates(0)
            dve.wait_ge(rope_ok, 10)
            for x in range(2):
                v.tensor_copy(kSa[64 * x:64 * x + 64], kTa[64 * (1 - x):64 * (1 - x) + 64]).then_inc(swap_ok, 1)

            def attention(L, prepare):
                un = UN[L]

                def row_max(n):
                    p, kind, qb, kts = un[n]
                    dve.wait_ge(at[L, "scores"], n + 1)
                    prepare(n, p, kind, qb)
                    sc = ps[:, 2 * (n % 2):2 * (n % 2) + 2, 0:len(kts) * P]
                    s = soft[:, n % 4]
                    if L == "a":
                        step(v.tensor_reduce(s[:, 0, :], sc, AX.X, ALU.max, negate=True))
                        settle()
                        v.tensor_tensor(s[:, 1, :], s[:, 0, :], negsink[:, 2 * p:2 * p + 2], ALU.min
                                        ).then_inc(at[L, "max"], 1)
                    else:
                        v.tensor_reduce(s[:, 1, :], sc, AX.X, ALU.max, negate=True).then_inc(at[L, "max"], 1)

                def sums(n):
                    w = len(un[n][3]) * P
                    s = soft[:, n % 4]
                    dve.wait_ge(at[L, "exp"], n + 1)
                    if L == "a":
                        step(v.tensor_tensor(s[:, 2, :], s[:, 2, :], s[:, 3, :], ALU.add))
                        settle()
                    if L == "c":
                        qb = un[n][2]
                        mult = cs("mult")[:, qb * S:qb * S + w]
                        for x in range(2):
                            pr = prob[:, n % AHEAD, x * T:x * T + w]
                            step(v.scalar_tensor_tensor(pr, pr, 1.0, mult, ALU.mult, ALU.mult,
                                                        accum_out=s[:, 2, x:x + 1]))
                        settle()
                    v.reciprocal(s[:, 4, :], s[:, 2, :]).then_inc(at[L, "sums"], 1)
                    dve.wait_ge(at[L, "sums"], n + 1)
                    for x in range(2):
                        pr = prob[:, n % AHEAD, x * T:x * T + w]
                        last = v.tensor_scalar(pr, pr, s[:, 4, x:x + 1], None, ALU.mult)
                    last.then_inc(at[L, "prob"], 1)

                def take_out(n):
                    p, kind, qb, _ = un[n]
                    dve.wait_ge(at[L, "pv"], n + 1)
                    src = ps[:, 6 + n % 2, 0:P]
                    c0 = (0 if kind == "lat" else S) + qb * P
                    if L == "a":
                        o = v.tensor_tensor(oT[:, p, c0:c0 + P], src, gT[:, p, c0:c0 + P], ALU.mult)
                    elif L == "b":
                        o = v.tensor_tensor(oT[:, p, c0:c0 + P], src, gTb[:, p, c0:c0 + P], ALU.mult)
                    else:
                        o = v.tensor_copy(mixT[:, p, c0:c0 + P], src)
                    o.then_inc(at[L, "o"], 1)

                row_max(0)
                row_max(1)
                sums(0)
                row_max(2)
                sums(1)
                for n in range(len(un)):
                    if n >= 1:
                        take_out(n - 1)
                    if n + 3 < len(un):
                        row_max(n + 3)
                    if n + 2 < len(un):
                        sums(n + 2)
                take_out(len(un) - 1)

            def mask_a(n, p, kind, qb):
                if kind == "lat":
                    sc = ps[:, 2 * (n % 2):2 * (n % 2) + 2, (1 - qb) * P:(2 - qb) * P]
                    step(v.tensor_tensor(sc, sc, band[:, qb * P:(qb + 1) * P].unsqueeze(1).broadcast_to([P, 2, P]),
                                         ALU.add))
                    settle()

            def bias_b(n, p, kind, qb):
                dve.wait_ge(bias_ok, 2 * p + 2)
                for x in range(2):
                    sc = ps[:, 2 * (n % 2) + x, 0:S].rearrange("p (r c) -> p r c", r=4)
                    b = bias[:, (2 * p + x) % 4, (2 - 2 * qb) * GRID_W:(6 - 2 * qb) * GRID_W]
                    forwards = bass.AP(b.tensor, b.offset + GRID_W - 1,
                                       [list(b.ap[0]), [GRID_W, 4], [-1, GRID_W]])
                    ins = v.tensor_tensor(sc, sc, forwards, ALU.add)
                ins.then_inc(bias_used, 1)
                dve.wait_ge(bias_used, n + 1)

            def bias_c(n, p, kind, qb):
                w = (qb + 1) * P
                for x in range(2):
                    slope = 2.0 ** (-8.0 * (2 * p + x + 1) / NH2)
                    sc = ps[:, 2 * (n % 2) + x, 0:w]
                    step(v.scalar_tensor_tensor(sc, cs("dist")[:, qb * S:qb * S + w], -slope, sc,
                                                ALU.mult, ALU.add))
                settle()

            dve.wait_ge(sink_in, 16)
            step(v.tensor_scalar(negsink[:, :], sink[:, :], -1.0, None, ALU.mult))
            settle()
            attention("a", mask_a)

            def residual(stage, l, parts, base):
                dve.wait_ge(mod_ok, 2 * l + 2)
                for m in range(KT):
                    dve.wait_ge(st[stage], m + 1)
                    dve.wait_ge(alpha_ok, base + m + 1)
                    for i, (c0, c1) in enumerate(parts):
                        ins = v.scalar_tensor_tensor(H[:, m, c0:c1], ps[:, m % 4, c0:c1], mod[:, l, 16 + m, i:i + 1],
                                                     H[:, m, c0:c1], ALU.mult, ALU.add)
                        if i < len(parts) - 1:
                            step(ins)
                            settle()
                    ins.then_inc(tk[stage, "dve"], 1)

            def center(N, w):
                dve.wait_ge(nm[N, "mean"], 1)
                for j in range(KT):
                    v.tensor_tensor(H[:, j, 0:w], H[:, j, 0:w], ps[:, 4, 0:w], ALU.subtract).then_inc(nm[N, "cent"], 1)
                invert(N, w)

            def invert(N, w):
                dve.wait_ge(nm[N, "std"], 1)
                step(v.reciprocal(rstd[:, 0:w], rstd[:, 0:w]))
                settle()

            def scale_all(dst, src, w):
                for j in range(KT):
                    v.tensor_tensor(dst[:, j, 0:w], src[:, j, 0:w], rstd[:, 0:w], ALU.mult).then_inc(scaled, 1)

            take_modulation(1)
            part = probT[:, 0:16].rearrange("p (j c) -> p j c", c=2)
            g0, b0 = (vec[:, VAT[x]:VAT[x] + KT] for x in ("ln_g", "ln_b"))
            step(v.tensor_tensor(part, mod[:, 1, 8:16, :], b0.unsqueeze(2).broadcast_to([P, KT, 2]), ALU.mult))
            settle()
            step(v.tensor_tensor(mod[:, 1, 0:8, :], mod[:, 1, 0:8, :], part, ALU.add))
            step(v.tensor_tensor(mod[:, 1, 8:16, :], mod[:, 1, 8:16, :], g0.unsqueeze(2).broadcast_to([P, KT, 2]),
                                 ALU.mult))
            settle()
            step(v.tensor_scalar(g0, g0, ALPHA, None, ALU.mult))
            step(v.tensor_scalar(b0, b0, ALPHA, None, ALU.mult))
            settle()
            residual("a_out", 0, ((0, S), (S, T)), 0)
            center("lna", T)
            dve.wait_ge(nm["lna", "sq"], KT)
            scale_all(H, H, T)
            for j in range(KT):
                dve.wait_ge(u_ok, KT + j + 1)
                dve.wait_ge(scaled, j + 1)
                v.tensor_scalar(H[:, j, 0:S], H[:, j, 0:S], vc("ln_g", j), vc("ln_b", j), ALU.mult, ALU.add
                                ).then_inc(alpha_ok, 1)
            take_gates(1)

            jobs = JOBS["b_in"]
            for i, (kind, m, _, _, eng) in enumerate(jobs):
                if eng == "dve":
                    dve.wait_ge(st["b_in"], i + 1)
                    dst = kTb[:, m, :] if kind == "k" else vb[:, m[1], m[0] * 512:(m[0] + 1) * 512]
                    v.tensor_copy(dst, ps[:, i % 4, :]).then_inc(tk["b_in", "dve"], 1)
            attention("b", bias_b)
            def take_mod2(chunk, col, m0, m1, bank):
                dve.wait_ge(col_done, chunk)
                return v.tensor_tensor(mod2[:, m0:m1], ps[:, bank, col:col + m1 - m0],
                                       vec[:, VAT["b_mod_2"] + m0:VAT["b_mod_2"] + m1], ALU.add).then_inc(mod_ok, 1)

            def gains(i, name, col):
                step(v.scalar_tensor_tensor(gain[:, i, :], mod2[:, col:col + KT], 1.0,
                                            vec[:, VAT[name]:VAT[name] + KT], ALU.add, ALU.mult))
                settle()

            take_mod2(CHUNKS["mod_a"] + 4, 0, 0, 16, 6)
            dve.wait_ge(mod_ok, 5)
            gains(0, "g_norm1_2", 8)
            residual("b_out", 1, ((0, S),), KT)
            center("lnb", S)
            dve.wait_ge(nm["lnb", "sq"], KT)
            for j in range(KT + 1):
                if j < KT:
                    step(v.tensor_tensor(H[:, j, 0:S], H[:, j, 0:S], rstd[:, 0:S], ALU.mult))
                if j >= 1:
                    dve.wait_ge(dve_step, steps[0] - (j < KT))
                    i = j - 1
                    v.tensor_scalar(H[:, i, 0:S], H[:, i, 0:S], vc("ln_g", 8 + i), vc("ln_b", 8 + i),
                                    ALU.mult, ALU.add).then_inc(nm["lnb", "out"], 1)

            take_mod2(CHUNKS["mod_a"] + 6, 16, 16, 24, 7)
            dve.wait_ge(nm["lnb", "out"], KT)
            invert("rms1", S)
            scale_all(h1T, H, S)

            dve.wait_ge(zero_ok, 1)
            for m in range(4):
                dve.wait_ge(st["c_in"], 4 + m + 1)
                dve.wait_ge(tk["c_in", "act"], 4)
                v.tensor_tensor(glu[:, m, CONV_W - 1:], ps[:, m, 0:S], sigb[:, m, :], ALU.mult
                                ).then_inc(tk["c_in", "dve"], 1)
            dve.wait_ge(tk["c_in", "dve"], 4)
            base = steps[0]
            for j in range(4):
                step(v.tensor_scalar(convo[:, j, :], glu[:, j, 0:S], conv_taps[:, j, 0:1], vc("conv_b_2", j),
                                     ALU.mult, ALU.add))
            for k in range(1, CONV_W):
                for j in range(4):
                    dve.wait_ge(dve_step, base + 4 * (k - 1) + j + 1)
                    ins = v.scalar_tensor_tensor(convo[:, j, :], glu[:, j, k:k + S], conv_taps[:, j, k:k + 1],
                                                 convo[:, j, :], ALU.mult, ALU.add)
                    if k < CONV_W - 1:
                        step(ins)
                    else:
                        ins.then_inc(conv_ok, 1)
            take_mod2(CHUNKS["mod_b"] + 3, 0, 24, 36, 7)
            attention("c", bias_c)
            dve.wait_ge(nm["lnc", "mean"], 1)
            step(v.tensor_scalar(probT[:, 0:S], ps[:, 4, 0:S], float(D // HID), None, ALU.mult))
            settle()
            dve.wait_ge(conv_ok, 4)
            for j in range(4):
                v.tensor_tensor(convo[:, j, :], convo[:, j, :], probT[:, 0:S], ALU.subtract
                                ).then_inc(nm["lnc", "cent"], 1)
            dve.wait_ge(nm["lnc", "std"], 1)
            step(v.reciprocal(rstd[:, 0:S], rstd[:, 0:S]))
            settle()
            for j in range(4):
                v.tensor_tensor(convo[:, j, :], convo[:, j, :], rstd[:, 0:S], ALU.mult).then_inc(acc2_ok, 1)

            take_mod2(CHUNKS["mod_b"] + 6, 12, 36, 48, 6)
            dve.wait_ge(mod_ok, 8)
            gains(1, "g_norm2_2", 32)
            for m in range(KT):
                dve.wait_ge(st["c_out"], m + 1)
                v.scalar_tensor_tensor(H[:, m, 0:S], ps[:, m % 4, 0:S], mod2[:, 16 + m:17 + m], H[:, m, 0:S],
                                       ALU.mult, ALU.add).then_inc(tk["c_out", "dve"], 1)
            dve.wait_ge(tk["c_out", "dve"], KT)
            invert("rms2", S)
            scale_all(h2T, H, S)

            def rr(i):
                return route[:, i, :].rearrange("p (t e) -> p t e", t=2)

            def r8(i):
                return route[:, i, 0:8].rearrange("p (t g) -> p t g", t=2)

            def r2(i, a=0):
                return route[:, i, a:a + 2]

            def bc(x, n):
                return x.unsqueeze(2).broadcast_to([P, 2, n])

            def do(ins):
                step(ins)
                settle()

            dve.wait_ge(logits, 1)
            dve.wait_ge(rt_in, 64)
            lg = ps[:, 0, 0:128].rearrange("p (t e) -> p t e", t=2)
            do(v.tensor_tensor(r8(0), lg[:, :, 0:NG], rbias[:, 0:NG].unsqueeze(1).broadcast_to([P, 2, NG]), ALU.add))
            do(v.tensor_tensor(rr(3), lg[:, :, NG:NG + NE], rbias[:, NG:NG + NE].unsqueeze(1).broadcast_to([P, 2, NE]),
                               ALU.add))
            do(v.tensor_reduce(r2(4), r8(0), AX.X, ALU.max))
            v.tensor_tensor(r8(1), r8(0), bc(r2(4), NG), ALU.subtract).then_inc(gsub, 1)

            def first_max(onehot, score, x, top, n, desc):
                do(v.tensor_tensor(score, x, bc(top, n), ALU.is_equal))
                do(v.tensor_tensor(score, score, desc.unsqueeze(1).broadcast_to([P, 2, n]), ALU.mult))
                do(v.tensor_reduce(r2(5), score, AX.X, ALU.max))
                do(v.tensor_tensor(onehot, score, bc(r2(5), n), ALU.is_equal))

            first_max(r8(6), r8(7), r8(0), r2(4), NG, cs("desc")[:, NE - NG:NE])
            do(v.tensor_scalar(r8(6), r8(6), BIG, -BIG, ALU.mult, ALU.add))
            for t in range(2):
                e3 = route[:, 3, t * NE:(t + 1) * NE].rearrange("p (g e) -> p g e", g=NG)
                pen = route[:, 6, t * NG:(t + 1) * NG].unsqueeze(2).broadcast_to([P, NG, EPG])
                do(v.tensor_tensor(e3, e3, pen, ALU.add))
            do(v.tensor_reduce(r2(8), rr(3), AX.X, ALU.max))
            first_max(rr(12), rr(9), rr(3), r2(8), NE, cs("desc"))
            do(v.scalar_tensor_tensor(rr(3), rr(12), -3 * BIG, rr(3), ALU.mult, ALU.add))
            do(v.tensor_reduce(r2(10), rr(3), AX.X, ALU.max))
            first_max(rr(13), rr(9), rr(3), r2(10), NE, cs("desc"))
            sel = rr(14)
            v.tensor_tensor(sel, rr(12), rr(13), ALU.add).then_inc(sel_ok, 1)
            v.tensor_tensor(r2(11), r2(10), r2(8), ALU.subtract).then_inc(tdif, 1)
            dve.wait_ge(gexp, 1)
            do(v.tensor_reduce(r2(15), r8(2), AX.X, ALU.add))
            dve.wait_ge(texp, 1)
            do(v.tensor_scalar(r2(15, 2), r2(11, 2), 1.0, None, ALU.add))
            do(v.tensor_tensor(r2(15, 4), r2(15, 0), r2(15, 2), ALU.mult))
            do(v.reciprocal(r2(15, 6), r2(15, 4)))
            do(v.tensor_tensor(r2(15, 8), r2(15, 6), r2(11, 2), ALU.mult))
            do(v.tensor_tensor(rr(12), rr(12), bc(r2(15, 6), NE), ALU.mult))
            do(v.tensor_tensor(rr(13), rr(13), bc(r2(15, 8), NE), ALU.mult))
            do(v.tensor_tensor(wsel[:, :, :], rr(12), rr(13), ALU.add))
            dve.wait_ge(ranks, 1)
            dve.wait_ge(sel_ok, 1)
            rk = ps[:, 5, 0:2 * NE].rearrange("p (t e) -> p t e", t=2)
            do(v.scalar_tensor_tensor(keysel[:, :, :], rk, 1.0, sel, ALU.add, ALU.mult))
            do(v.tensor_scalar(keysel[:, :, :], keysel[:, :, :], -1.0, None, ALU.add))
            do(v.tensor_reduce(peakf[:, :], ps[:, 5, 64:64 + NE], AX.X, ALU.max))
            v.tensor_copy(peak[:, :], peakf[0:1, :]).then_inc(peak_ok, 1)

            def choose(n, pair):
                v.tensor_tensor(pick.rearrange("p t (e s) -> p t e s", e=2),
                                keysel[:, :, bass.ds(pair * 2, 2)].unsqueeze(3).broadcast_to([P, 2, 2, CAP]),
                                cs("slot").unsqueeze(1).unsqueeze(1).broadcast_to([P, 2, 2, CAP]), ALU.is_equal
                                ).then_inc(pick_ok, 1)

            def weigh(n, pair):
                dve.wait_ge(pick_ok, n + 1)
                v.tensor_tensor(wpick.rearrange("p t (e s) -> p t e s", e=2),
                                pick.rearrange("p t (e s) -> p t e s", e=2),
                                wsel[:, :, bass.ds(pair * 2, 2)].unsqueeze(3).broadcast_to([P, 2, 2, CAP]), ALU.mult
                                ).then_inc(wpick_ok, 1)

            def take_gather(n):
                dve.wait_ge(gath, n * 2 + 2)
                v.tensor_copy(xg[:, 4:8, :], ps[:, 1, :]).then_inc(xg_dve, 1)

            def accumulate(n):
                for i, b in enumerate((7, 2, 3, 0)):
                    dve.wait_ge(scat, n * 4 + i + 1)
                    y = yacc[:, i * 512:(i + 1) * 512]
                    v.tensor_tensor(y, ps[:, b, :], y, ALU.add).then_inc(acc_ok, 1)

            def experts(r, pair, first=False, final=False):
                n = r * PAIRS + pair
                if not (first and r == 0):
                    dve.wait_ge(wturn, n)
                weigh(n, pair)
                if not final:
                    dve.wait_ge(wpick_ok, n + 1)
                    choose(n + 1, pair + 1)
                dve.wait_ge(up_done, n + 1)
                dve.wait_ge(sg_ok, n + 1)
                v.tensor_tensor(hid, ps[:, 3, :], sgl, ALU.mult).then_inc(hid_ok, 1)
                if not final:
                    take_gather(n + 1)
                if not first:
                    accumulate(n - 1)
                dve.wait_ge(down_done, n + 1)
                v.tensor_copy(yrows[:, 512:1024], ps[:, 6, :]).then_inc(yr_dve, 1)
                if final:
                    accumulate(n)

            def all_pairs(r):
                choose(r * PAIRS, 0)
                take_gather(r * PAIRS)
                experts(r, 0, first=True)
                with dve.Fori(1, PAIRS - 1) as pair:
                    experts(r, pair)
                experts(r, PAIRS - 1, final=True)

            dve.wait_ge(acc_zero, 1)
            all_pairs(0)
            dve.wait_ge(peak_ok, 1)
            most = dve.value_load(peak[:, :], min_val=0, max_val=S)
            for r in range(1, PASSES):
                with dve.If(most > CAP * r):
                    do_over(v.tensor_scalar(keysel[:, :, :], keysel[:, :, :], -1.0 * CAP, None, ALU.add))
                    all_pairs(r)
                    dve.wait_ge(acc_ok, 4 * PAIRS * (r + 1))

            dve.wait_ge(acc_ok, 4 * PAIRS)
            for m in range(KT):
                v.scalar_tensor_tensor(H[:, m, 0:S], yacc[:, m * S:(m + 1) * S], mod2[:, 40 + m:41 + m],
                                       H[:, m, 0:S], ALU.mult, ALU.add).then_inc(nm["rmsf", "cent"], 1)
            dve.wait_ge(nm["rmsf", "cent"], KT)
            dve.wait_ge(nm["rmsf", "sq"], KT)
            invert("rmsf", S)
            scale_all(H, H, S)
            for b in range(1, 4, 2):
                dve.wait_ge(oturn, b + 1)
                v.tensor_copy(outrows[:, b // 2, 512:1024], ps[:, b, :]).then_inc(orow_ok, 1)


_INS = ["x", "c", "ctx", "c_ctx", "w_ada", "b_ada", "ln_g", "ln_b", "a_w_in", "a_w_out", "a_sink", "b_w_in",
        "b_w_out", "b_rel_bias", "c_2", "w_mod_2", "b_mod_2", "g_norm1_2", "w_in_2", "conv_w_2", "conv_b_2",
        "conv_ln_g_2", "conv_ln_b_2", "w_out_2", "g_norm2_2", "w_router_group_2", "b_router_group_2",
        "w_router_expert_2", "b_router_expert_2", "w_exp_gate_2", "w_exp_up_2", "w_exp_down_2", "g_final_2"]


def kernel(**inputs):
    import numpy as _np
    import concourse.bacc as _bacc
    from concourse import mybir as _mybir
    from concourse.bass_utils import run_bass_kernel_spmd as _run

    nc = _bacc.Bacc("TRN2", target_bir_lowering=False, num_devices=1)
    arrays, aps = {}, {}
    for name in _INS:
        a = _np.ascontiguousarray(inputs[name])
        arrays[f"in_{name}"] = a
        aps[name] = nc.dram_tensor(f"in_{name}", a.shape, _mybir.dt.from_np(a.dtype), kind="ExternalInput").ap()
    arrays["in_consts"] = constants()
    consts = nc.dram_tensor("in_consts", arrays["in_consts"].shape, _mybir.dt.float32, kind="ExternalInput").ap()
    relpad = nc.dram_tensor("relpad", (NH * REL_H, PADW), _mybir.dt.float32, kind="Internal").ap()
    out = nc.dram_tensor("out_0", (1, S, D), _mybir.dt.float32, kind="ExternalOutput").ap()
    build(nc, aps, consts, relpad, out)
    r = _run(nc, [arrays], core_ids=[0])
    return r.results[0]["out_0"]
```
